# Optimizing a Trainium2 kernel written in Bass

```python
import jax, jax.numpy as jnp
from jax import lax
import numpy as np

D_MODEL = 1024
BATCH = 1
SEQ = 256
DEPTH = 1
DEC_BATCH = 1
DEC_SEQ = 1024
PAST_LEN = 512

GRID_W = 64
A_HEAD_DIM = 64
A_WIDTH = D_MODEL // 2
A_HEADS = A_WIDTH // A_HEAD_DIM
A_DECAY_RANK = 64
A_ICLR_RANK = 64
A_GATE_RANK = 128
B_HEAD_DIM = 128
B_WIDTH = D_MODEL // 2
B_HEADS = B_WIDTH // B_HEAD_DIM
B_CHUNK = 64
CONV_K = 3
N_GROUPS = 4
EXPERTS_PER_GROUP = 4
N_EXPERTS = N_GROUPS * EXPERTS_PER_GROUP
EXPERT_TOP_K = 2
D_EXPERT = D_MODEL // 4
IN_SPLITS = (A_WIDTH, A_WIDTH + B_WIDTH, A_WIDTH + 2 * B_WIDTH, A_WIDTH + 2 * B_WIDTH + D_MODEL)
IN_COLS = A_WIDTH + 2 * B_WIDTH + 2 * D_MODEL
NORM_EPS = 1e-6
RWKV_GN_EPS = 64e-5
MLSTM_GN_EPS = 1e-5

kernel_name = 'bidir_rwkv7_mlstm_hmoe_diffusion_step'

def rmsnorm(x, g):
    xf = x.astype(jnp.float32)
    return (xf * lax.rsqrt(jnp.mean(xf * xf, axis=-1, keepdims=True) + NORM_EPS)).astype(x.dtype) * g

def head_norm(y, eps):
    mu = jnp.mean(y, axis=-1, keepdims=True)
    var = jnp.mean(jnp.square(y - mu), axis=-1, keepdims=True)
    return (y - mu) * lax.rsqrt(var + eps)

def depthwise_conv(u, kernel, rows):
    Bn, T, C = u.shape
    img = u.reshape(Bn, rows, T // rows, C)
    out = lax.conv_general_dilated(img, kernel[:, :, None, :], window_strides=(1, 1), padding='SAME',
                                   dimension_numbers=('NHWC', 'HWIO', 'NHWC'), feature_group_count=C)
    return out.reshape(Bn, T, C)

def rwkv7_scan(r, decay, k, v, aa, bb, S0, reverse):
    def step(S, inp):
        r_t, w_t, k_t, v_t, a_t, b_t = inp
        sa = jnp.einsum('bhij,bhj->bhi', S, a_t)
        S = S * w_t[:, :, None, :] + sa[..., None] * b_t[:, :, None, :] + v_t[..., None] * k_t[:, :, None, :]
        return S, jnp.einsum('bhij,bhj->bhi', S, r_t)
    xs = tuple(jnp.moveaxis(t, 1, 0) for t in (r, decay, k, v, aa, bb))
    S, ys = lax.scan(step, S0, xs, reverse=reverse)
    return jnp.moveaxis(ys, 0, 1), S

def rwkv7_mix(xa, S0, p):
    Bn, T, _ = xa.shape
    hs = (Bn, T, A_HEADS, A_HEAD_DIM)
    xpad = jnp.pad(xa, ((0, 0), (1, 1), (0, 0)))
    xx = 0.5 * (xpad[:, :-2] + xpad[:, 2:]) - xa
    xr, xw, xk, xv, xi, xg = (xa + xx * p['rwkv_mu'][j] for j in range(6))
    r = (xr @ p['rwkv_w_r']).reshape(hs).astype(jnp.float32)
    k = (xk @ p['rwkv_w_k']).astype(jnp.float32)
    v = (xv @ p['rwkv_w_v']).reshape(hs).astype(jnp.float32)
    g = (jax.nn.sigmoid(xg @ p['rwkv_g1']) @ p['rwkv_g2']).astype(jnp.float32)
    kk = (k * p['rwkv_k_k']).reshape(hs)
    kk = kk / jnp.maximum(jnp.sqrt(jnp.sum(kk * kk, axis=-1, keepdims=True)), 1e-12)
    y_sum, bonus, states = 0.0, 0.0, []
    for d in range(2):
        w = -jax.nn.softplus(-(p['rwkv_w0'][d] + jnp.tanh(xw @ p['rwkv_w1'][d]) @ p['rwkv_w2'][d]).astype(jnp.float32)) - 0.5
        decay = jnp.exp(-jnp.exp(w)).reshape(hs)
        a = jax.nn.sigmoid((p['rwkv_a0'][d] + (xi @ p['rwkv_a1'][d]) @ p['rwkv_a2'][d]).astype(jnp.float32))
        kd = (k * (1.0 + (a - 1.0) * p['rwkv_k_a'])).reshape(hs)
        y, S = rwkv7_scan(r, decay, kd, v, -kk, kk * a.reshape(hs), S0[:, d], reverse=(d == 1))
        y_sum = y_sum + y
        bonus = bonus + jnp.sum(r * kd * p['rwkv_r_k'], axis=-1, keepdims=True) * v
        states.append(S)
    yn = head_norm(y_sum, RWKV_GN_EPS).reshape(Bn, T, A_WIDTH) * p['rwkv_ln_g'] + p['rwkv_ln_b']
    y = (yn + bonus.reshape(Bn, T, A_WIDTH)) * g
    return y.astype(xa.dtype), jnp.stack(states, axis=1)

def mlstm_chunkwise(q, k, v, log_i, log_f, C0, n0, m0):
    Bn, H, T, d = q.shape
    nc = T // B_CHUNK

    def chunks(a):
        return jnp.moveaxis(a.reshape(Bn, H, nc, B_CHUNK, *a.shape[3:]), 2, 0)

    causal = jnp.tril(jnp.ones((B_CHUNK, B_CHUNK), dtype=bool))

    def step(carry, inp):
        C, n, m = carry
        qc, kc, vc, ic, fc = inp
        b = jnp.cumsum(fc, axis=-1)
        logw = jnp.where(causal, b[..., :, None] - b[..., None, :] + ic[..., None, :], -jnp.inf)
        m_t = jnp.maximum(b + m[..., None], jnp.max(logw, axis=-1))
        inter = jnp.exp(b + m[..., None] - m_t)
        s = jnp.einsum('bhtk,bhsk->bhts', qc, kc) * jnp.exp(logw - m_t[..., None])
        num = inter[..., None] * jnp.einsum('bhtk,bhkv->bhtv', qc, C) + jnp.einsum('bhts,bhsv->bhtv', s, vc)
        den = inter * jnp.einsum('bhtk,bhk->bht', qc, n) + jnp.sum(s, axis=-1)
        h = num / jnp.maximum(jnp.abs(den), jnp.exp(-m_t))[..., None]
        m_new = m_t[..., -1]
        carry_decay = jnp.exp(b[..., -1] + m - m_new)
        kw = kc * jnp.exp(b[..., -1:] - b + ic - m_new[..., None])[..., None]
        C = carry_decay[..., None, None] * C + jnp.einsum('bhsk,bhsv->bhkv', kw, vc)
        n = carry_decay[..., None] * n + jnp.sum(kw, axis=2)
        return (C, n, m_new), h

    (C, n, m), hs = lax.scan(step, (C0, n0, m0), tuple(chunks(a) for a in (q, k, v, log_i, log_f)))
    return jnp.moveaxis(hs, 0, 2).reshape(Bn, H, T, d), C, n, m

def mlstm_mix(u, o_pre, C0, n0, m0, rows, p):
    Bn, T, _ = u.shape
    if rows is None:
        uc = depthwise_conv(u, p['mlstm_conv'][CONV_K // 2:CONV_K // 2 + 1], 1)
    else:
        uc = depthwise_conv(u, p['mlstm_conv'], rows)
    uc = jax.nn.silu(uc)
    uch = uc.reshape(Bn, T, B_HEADS, B_HEAD_DIM)
    q = jnp.einsum('bthd,hde->bhte', uch, p['mlstm_w_q']).astype(jnp.float32)
    k = jnp.einsum('bthd,hde->bhte', uch, p['mlstm_w_k']).astype(jnp.float32) * (B_HEAD_DIM ** -0.5)
    v = jnp.einsum('bthd,hde->bhte', u.reshape(Bn, T, B_HEADS, B_HEAD_DIM), p['mlstm_w_v']).astype(jnp.float32)
    h_sum, Cs, ns, ms = 0.0, [], [], []
    for d in range(2):
        log_i = (jnp.einsum('btc,ch->bht', uc, p['mlstm_w_i'][d]) + p['mlstm_b_i'][d][:, None]).astype(jnp.float32)
        log_f = jax.nn.log_sigmoid((jnp.einsum('btc,ch->bht', uc, p['mlstm_w_f'][d]) + p['mlstm_b_f'][d][:, None]).astype(jnp.float32))
        seq = (q, k, v, log_i, log_f)
        if d == 1:
            seq = tuple(jnp.flip(a, axis=2) for a in seq)
        h, C, n, m = mlstm_chunkwise(*seq, C0[:, d], n0[:, d], m0[:, d])
        if d == 1:
            h = jnp.flip(h, axis=2)
        h_sum = h_sum + h
        Cs.append(C); ns.append(n); ms.append(m)
    hn = jnp.moveaxis(head_norm(h_sum, MLSTM_GN_EPS), 1, 2).reshape(Bn, T, B_WIDTH).astype(u.dtype) * p['mlstm_ln_g']
    y = jax.nn.sigmoid(o_pre) * hn
    return y, jnp.stack(Cs, axis=1), jnp.stack(ns, axis=1), jnp.stack(ms, axis=1)

def hier_moe(h, p):
    Bn, T, D = h.shape
    t = h.reshape(Bn * T, D)
    g_logits = (t @ p['moe_w_group']).astype(jnp.float32) + p['moe_b_group']
    g_prob = jax.nn.softmax(g_logits, axis=-1)
    g_sel = jnp.argmax(g_logits, axis=-1)
    g_w = jnp.take_along_axis(g_prob, g_sel[:, None], axis=-1)
    e_logits = ((t @ p['moe_w_expert']).astype(jnp.float32) + p['moe_b_expert']).reshape(-1, N_GROUPS, EXPERTS_PER_GROUP)
    e_logits = jnp.take_along_axis(e_logits, g_sel[:, None, None], axis=1)[:, 0]
    top_p, top_i = lax.top_k(jax.nn.softmax(e_logits, axis=-1), EXPERT_TOP_K)
    top_w = g_w * top_p / jnp.sum(top_p, axis=-1, keepdims=True)
    expert_id = g_sel[:, None] * EXPERTS_PER_GROUP + top_i
    combine = jnp.sum(jax.nn.one_hot(expert_id, N_EXPERTS, dtype=jnp.float32) * top_w[..., None], axis=1)
    a = jnp.einsum('nd,edf->nef', t, p['moe_w1'])
    b = jnp.einsum('nd,edf->nef', t, p['moe_w3'])
    act = jax.nn.silu(a) * b * combine[..., None].astype(t.dtype)
    return jnp.einsum('nef,efd->nd', act, p['moe_w2']).reshape(Bn, T, D)

def trunk_layer(x, mod, s_rwkv, s_C, s_n, s_m, rows, p):
    shift1, scale1, gate1, shift2, scale2, gate2 = jnp.split(mod[:, None, :], 6, axis=-1)
    h = rmsnorm(x, p['norm1_g']) * (1 + scale1) + shift1
    xa, ub, o_pre, ga, gb = jnp.split(h @ p['w_in'], IN_SPLITS, axis=-1)
    ya, s_rwkv = rwkv7_mix(xa, s_rwkv, p)
    yb, s_C, s_n, s_m = mlstm_mix(ub, o_pre, s_C, s_n, s_m, rows, p)
    merged = jax.nn.sigmoid(ga) * (ya @ p['rwkv_w_proj']) + jax.nn.sigmoid(gb) * (yb @ p['mlstm_w_proj'])
    x = x + gate1 * (merged @ p['w_out'])
    h = rmsnorm(x, p['norm2_g']) * (1 + scale2) + shift2
    x = x + gate2 * hier_moe(h, p)
    return x, s_rwkv, s_C, s_n, s_m

def setup_inputs(seed: int = 0) -> dict:
    key = jax.random.key(seed)
    ks = iter(jax.random.split(key, 64))
    f32 = jnp.float32

    def nrm(shape, scale):
        return jax.random.normal(next(ks), shape, f32) * scale

    def uni(shape, lo, hi):
        return jax.random.uniform(next(ks), shape, f32, lo, hi)

    L, D = DEPTH, D_MODEL
    return {
        'x_prompt': nrm((BATCH, SEQ, D), 1.0),
        'x_sample': nrm((DEC_BATCH, DEC_SEQ, D), 1.0),
        'c': nrm((DEC_BATCH, D), 1.0),
        'c_ctx': nrm((D,), 1.0),
        'state_rwkv': nrm((DEC_BATCH, L, 2, A_HEADS, A_HEAD_DIM, A_HEAD_DIM), 0.1),
        'state_mlstm_C': nrm((DEC_BATCH, L, 2, B_HEADS, B_HEAD_DIM, B_HEAD_DIM), 0.1),
        'state_mlstm_n': nrm((DEC_BATCH, L, 2, B_HEADS, B_HEAD_DIM), 0.5),
        'state_mlstm_m': uni((DEC_BATCH, L, 2, B_HEADS), 0.0, 4.0),
        'w_mod': nrm((L, D, 6 * D), 0.3 * D ** -0.5),
        'b_mod': nrm((L, 6 * D), 0.01),
        'norm1_g': 1.0 + nrm((L, D), 0.01),
        'norm2_g': 1.0 + nrm((L, D), 0.01),
        'w_in': nrm((L, D, IN_COLS), D ** -0.5),
        'rwkv_mu': uni((L, 6, A_WIDTH), 0.0, 1.0),
        'rwkv_w_r': nrm((L, A_WIDTH, A_WIDTH), A_WIDTH ** -0.5),
        'rwkv_w_k': nrm((L, A_WIDTH, A_WIDTH), A_WIDTH ** -0.5),
        'rwkv_w_v': nrm((L, A_WIDTH, A_WIDTH), A_WIDTH ** -0.5),
        'rwkv_w0': uni((L, 2, A_WIDTH), -4.0, 0.0),
        'rwkv_w1': nrm((L, 2, A_WIDTH, A_DECAY_RANK), A_WIDTH ** -0.5),
        'rwkv_w2': nrm((L, 2, A_DECAY_RANK, A_WIDTH), 0.5 * A_DECAY_RANK ** -0.5),
        'rwkv_a0': nrm((L, 2, A_WIDTH), 0.5),
        'rwkv_a1': nrm((L, 2, A_WIDTH, A_ICLR_RANK), A_WIDTH ** -0.5),
        'rwkv_a2': nrm((L, 2, A_ICLR_RANK, A_WIDTH), 0.5 * A_ICLR_RANK ** -0.5),
        'rwkv_g1': nrm((L, A_WIDTH, A_GATE_RANK), A_WIDTH ** -0.5),
        'rwkv_g2': nrm((L, A_GATE_RANK, A_WIDTH), A_GATE_RANK ** -0.5),
        'rwkv_k_k': 1.0 + nrm((L, A_WIDTH), 0.1),
        'rwkv_k_a': 1.0 + nrm((L, A_WIDTH), 0.1),
        'rwkv_r_k': nrm((L, A_HEADS, A_HEAD_DIM), 0.1),
        'rwkv_ln_g': 1.0 + nrm((L, A_WIDTH), 0.01),
        'rwkv_ln_b': nrm((L, A_WIDTH), 0.01),
        'rwkv_w_proj': nrm((L, A_WIDTH, D), A_WIDTH ** -0.5),
        'mlstm_conv': nrm((L, CONV_K, CONV_K, B_WIDTH), 1.0 / CONV_K),
        'mlstm_w_q': nrm((L, B_HEADS, B_HEAD_DIM, B_HEAD_DIM), B_HEAD_DIM ** -0.5),
        'mlstm_w_k': nrm((L, B_HEADS, B_HEAD_DIM, B_HEAD_DIM), B_HEAD_DIM ** -0.5),
        'mlstm_w_v': nrm((L, B_HEADS, B_HEAD_DIM, B_HEAD_DIM), B_HEAD_DIM ** -0.5),
        'mlstm_w_i': nrm((L, 2, B_WIDTH, B_HEADS), 0.1 * B_WIDTH ** -0.5),
        'mlstm_b_i': nrm((L, 2, B_HEADS), 0.1),
        'mlstm_w_f': nrm((L, 2, B_WIDTH, B_HEADS), 0.1 * B_WIDTH ** -0.5),
        'mlstm_b_f': uni((L, 2, B_HEADS), 3.0, 6.0),
        'mlstm_ln_g': 1.0 + nrm((L, B_WIDTH), 0.01),
        'mlstm_w_proj': nrm((L, B_WIDTH, D), B_WIDTH ** -0.5),
        'w_out': nrm((L, D, D), D ** -0.5),
        'moe_w_group': nrm((L, D, N_GROUPS), D ** -0.5),
        'moe_b_group': nrm((L, N_GROUPS), 0.01),
        'moe_w_expert': nrm((L, D, N_EXPERTS), D ** -0.5),
        'moe_b_expert': nrm((L, N_EXPERTS), 0.01),
        'moe_w1': nrm((L, N_EXPERTS, D, D_EXPERT), D ** -0.5),
        'moe_w3': nrm((L, N_EXPERTS, D, D_EXPERT), D ** -0.5),
        'moe_w2': nrm((L, N_EXPERTS, D_EXPERT, D), D_EXPERT ** -0.5),
        'final_norm_g': 1.0 + nrm((D,), 0.01),
    }

def reference(x_prompt, x_sample, c, c_ctx, state_rwkv, state_mlstm_C, state_mlstm_n, state_mlstm_m,
              w_mod, b_mod, norm1_g, norm2_g, w_in,
              rwkv_mu, rwkv_w_r, rwkv_w_k, rwkv_w_v, rwkv_w0, rwkv_w1, rwkv_w2, rwkv_a0, rwkv_a1, rwkv_a2,
              rwkv_g1, rwkv_g2, rwkv_k_k, rwkv_k_a, rwkv_r_k, rwkv_ln_g, rwkv_ln_b, rwkv_w_proj,
              mlstm_conv, mlstm_w_q, mlstm_w_k, mlstm_w_v, mlstm_w_i, mlstm_b_i, mlstm_w_f, mlstm_b_f,
              mlstm_ln_g, mlstm_w_proj, w_out,
              moe_w_group, moe_b_group, moe_w_expert, moe_b_expert, moe_w1, moe_w3, moe_w2,
              final_norm_g):
    f32 = jnp.float32
    rows = x_sample.shape[1] // GRID_W
    Bp = x_prompt.shape[0]
    zero_rwkv = jnp.zeros((Bp, 2, A_HEADS, A_HEAD_DIM, A_HEAD_DIM), f32)
    zero_C = jnp.zeros((Bp, 2, B_HEADS, B_HEAD_DIM, B_HEAD_DIM), f32)
    zero_n = jnp.zeros((Bp, 2, B_HEADS, B_HEAD_DIM), f32)
    zero_m = jnp.zeros((Bp, 2, B_HEADS), f32)
    new_rwkv, new_C, new_n, new_m = [], [], [], []
    xp, xs = x_prompt, x_sample
    for l in range(DEPTH):
        p = {
            'norm1_g': norm1_g[l], 'norm2_g': norm2_g[l], 'w_in': w_in[l],
            'rwkv_mu': rwkv_mu[l], 'rwkv_w_r': rwkv_w_r[l], 'rwkv_w_k': rwkv_w_k[l], 'rwkv_w_v': rwkv_w_v[l],
            'rwkv_w0': rwkv_w0[l], 'rwkv_w1': rwkv_w1[l], 'rwkv_w2': rwkv_w2[l],
            'rwkv_a0': rwkv_a0[l], 'rwkv_a1': rwkv_a1[l], 'rwkv_a2': rwkv_a2[l],
            'rwkv_g1': rwkv_g1[l], 'rwkv_g2': rwkv_g2[l], 'rwkv_k_k': rwkv_k_k[l], 'rwkv_k_a': rwkv_k_a[l],
            'rwkv_r_k': rwkv_r_k[l], 'rwkv_ln_g': rwkv_ln_g[l], 'rwkv_ln_b': rwkv_ln_b[l],
            'rwkv_w_proj': rwkv_w_proj[l],
            'mlstm_conv': mlstm_conv[l], 'mlstm_w_q': mlstm_w_q[l], 'mlstm_w_k': mlstm_w_k[l],
            'mlstm_w_v': mlstm_w_v[l], 'mlstm_w_i': mlstm_w_i[l], 'mlstm_b_i': mlstm_b_i[l],
            'mlstm_w_f': mlstm_w_f[l], 'mlstm_b_f': mlstm_b_f[l], 'mlstm_ln_g': mlstm_ln_g[l],
            'mlstm_w_proj': mlstm_w_proj[l], 'w_out': w_out[l],
            'moe_w_group': moe_w_group[l], 'moe_b_group': moe_b_group[l],
            'moe_w_expert': moe_w_expert[l], 'moe_b_expert': moe_b_expert[l],
            'moe_w1': moe_w1[l], 'moe_w3': moe_w3[l], 'moe_w2': moe_w2[l],
        }
        mod_ctx = jax.nn.silu(c_ctx)[None, :] @ w_mod[l] + b_mod[l]
        mod_lat = jax.nn.silu(c) @ w_mod[l] + b_mod[l]
        xp, s_r, s_C, s_n, s_m = trunk_layer(xp, mod_ctx, zero_rwkv, zero_C, zero_n, zero_m, None, p)
        new_rwkv.append(s_r); new_C.append(s_C); new_n.append(s_n); new_m.append(s_m)
        xs, _, _, _, _ = trunk_layer(xs, mod_lat, state_rwkv[:, l].astype(f32), state_mlstm_C[:, l].astype(f32),
                                     state_mlstm_n[:, l].astype(f32), state_mlstm_m[:, l].astype(f32), rows, p)
    y_prompt = rmsnorm(xp, final_norm_g)
    y_sample = rmsnorm(xs, final_norm_g)
    dt = x_prompt.dtype
    return (y_prompt, y_sample, jnp.stack(new_rwkv, axis=1).astype(dt), jnp.stack(new_C, axis=1).astype(dt),
            jnp.stack(new_n, axis=1).astype(dt), jnp.stack(new_m, axis=1).astype(dt))


_drawn_inputs = setup_inputs


def setup_inputs(seed=0):
    import zlib

    import numpy as np

    out = dict(_drawn_inputs(seed))
    spreads = {}
    factors = {'state_rwkv': 64.0,
     'state_mlstm_C': 4.528,
     'state_mlstm_n': 6.552,
     'state_mlstm_m': 5.731,
     'norm1_g': 4.263,
     'norm2_g': 8.0,
     'rwkv_g1': 3.03,
     'rwkv_r_k': 3.167,
     'rwkv_ln_g': 31.072,
     'rwkv_ln_b': 64.0,
     'mlstm_w_f': 8.0,
     'mlstm_ln_g': 8.0,
     'moe_b_group': 8.0,
     'moe_b_expert': 8.0,
     'final_norm_g': 32.423}
    for name, (base, spread) in spreads.items():
        noise = np.random.default_rng([zlib.crc32(name.encode()), seed]).standard_normal(out[name].shape)
        drawn = base * np.exp(spread * noise) if base else spread * noise
        out[name] = __import__('jax').numpy.asarray(drawn.astype(out[name].dtype))
    for name, factor in factors.items():
        out[name] = (out[name] * factor).astype(out[name].dtype)
    return out
```

```python
from contextlib import ExitStack

import concourse.bass as bass
from concourse import mybir

F32 = mybir.dt.float32
ACT = mybir.ActivationFunctionType
ALU = mybir.AluOpType
AX = mybir.AxisListType

P = 128
D = 1024
KD = D // P
PROMPT, SAMPLE = 256, 1024
NT = PROMPT + SAMPLE
TILES = NT // P
BLOCKS = [(0, 256), (256, 512), (768, 512)]
STREAMS = [(0, PROMPT), (PROMPT, SAMPLE)]
XA_PAD = NT + 4
NORM_EPS = 1e-6

VEC_PARTS = [("b_mod", 48), ("norm1_g", 8), ("norm2_g", 8), ("rwkv_mu", 24), ("rwkv_w0", 8), ("rwkv_a0", 8),
             ("rwkv_k_k", 4), ("rwkv_k_a", 4), ("rwkv_r_k", 4), ("rwkv_ln_g", 4), ("rwkv_ln_b", 4),
             ("mlstm_conv", 36), ("mlstm_ln_g", 4)]
VEC = {}
NVEC = 0
for _name, _n in VEC_PARTS:
    VEC[_name] = NVEC
    NVEC += _n


def xa_col(t):
    return t + 1 if t < PROMPT else t + 3


class Own:

    def __init__(self, engine, sem, start=0):
        self.engine, self.sem, self.n = engine, sem, start

    def did(self, instruction):
        instruction.then_inc(self.sem, 1)
        self.n += 1
        return self.n

    def settle(self):
        self.engine.wait_ge(self.sem, self.n)


def semaphores(nc, ctx, prefix=""):
    mine = []

    def retire():
        nc.clear_and_free_semaphores(mine)
        nc.all_engine_barrier()
    ctx.callback(retire)

    def sem(name):
        mine.append(nc.alloc_semaphore(prefix + name))
        return mine[-1]
    return sem


def wait_reuse(engine, sem, count):
    if not (isinstance(count, int) and count == 0):
        engine.wait_ge(sem, count)


class Core:
    pass


def allocate(nc, ctx, io):
    c = Core()
    c.nc, c.io = nc, io

    def sb(name, shape):
        return ctx.enter_context(nc.sbuf_tensor(name, shape, F32))

    c.vec = sb("vec", [P, NVEC])
    c.ident = sb("ident", [P, P])
    c.ones = sb("ones", [P, P])
    c.mod = sb("mod", [P, 48, 2])
    c.gain = sb("gain", [P, 2, KD, 2])
    c.xa = sb("xa", [P, 4, XA_PAD])
    c.y = sb("y", [P, 8, NT])
    c.sig = nc.dram_tensor("sig_scratch", (20, P, NT), F32, kind="Internal").ap()
    c.rkv = nc.dram_tensor("rkv_scratch", (3, 4, P, NT), F32, kind="Internal").ap()
    c.hid_g = nc.dram_tensor("hid_g_scratch", (P, NT), F32, kind="Internal").ap()
    c.h2 = nc.dram_tensor("h2_scratch", (NT, D), F32, kind="Internal").ap()
    c.slot_list = nc.dram_tensor("slot_list_scratch", (SLOT_TILES * P, 1), F32, kind="Internal").ap()
    c.ys = nc.dram_tensor("ys_scratch", (SLOT_TILES * P, D), F32, kind="Internal").ap()
    return c


def norm_statistics(act, own, x, tile, junk, sumsq):
    return act.activation(junk, x, ACT.Square, accum_out=sumsq[:, tile:tile + 1])


def phase_a(c):
    nc, io = c.nc, c.io
    with ExitStack() as ctx:
        def sb(name, shape):
            return ctx.enter_context(nc.sbuf_tensor(name, shape, F32))

        sem = semaphores(nc, ctx)
        WRING = 3
        x = sb("a_x", [P, TILES, D])
        wmod = sb("a_wmod", [P, WRING, KD, 512])
        cc = sb("a_cc", [P, KD, 2])
        cs = sb("a_cs", [P, KD, 2])
        junk = sb("a_junk", [P, D])
        stat = sb("a_stat", [P, 3, TILES])
        tp = ctx.enter_context(nc.psum_tensor("a_tp", [P, 4, 512], F32))
        pm = ctx.enter_context(nc.psum_tensor("a_pm", [P, 48, 2], F32))
        consts_in, ident_set, cond_silu = sem("a_consts_in"), sem("a_ident_set"), sem("a_cond_silu")
        w_in = [sem(f"a_w_in{i}") for i in range(WRING)]
        x_in = [sem(f"a_x_in{i}") for i in range(TILES)]
        w_used, mod_half, mod_set = sem("a_w_used"), sem("a_mod_half"), sem("a_mod_set")
        squares, std_set, x_scaled = sem("a_squares"), sem("a_std_set"), sem("a_x_scaled")
        turned, act_evac, dve_evac, dve_own = sem("a_turned"), sem("a_act_evac"), sem("a_dve_evac"), sem("a_dve_own")
        block = ctx.enter_context(nc.Block())

        @block.sync
        def _(sp):
            sp.dma_start(cc[:, :, :], io["cond"]).then_inc(consts_in, 16)
            sp.dma_start(c.vec[:, :], io["vecs"]).then_inc(consts_in, 16)
            for g in range(12):
                if g >= WRING:
                    sp.wait_ge(w_used, g - WRING + 1)
                sp.dma_start(wmod[:, g % WRING], io["w_mod"][g]).then_inc(w_in[g % WRING], 16)
                if g < 2:
                    for t in range(5 * g, 5 * g + 5):
                        sp.dma_start(x[:, t], io["x"][t * P:(t + 1) * P, :]).then_inc(x_in[t], 16)

        @block.gpsimd
        def _(pool):
            pool.memset(c.ones[:, :], 1.0).then_inc(ident_set, 1)
            pool.wait_ge(ident_set, 1)
            pool.affine_select(out=c.ident[:, :], in_=c.ones[:, :], compare_op=ALU.is_equal, fill=0.0, base=0,
                               pattern=[[-1, P]], channel_multiplier=1).then_inc(ident_set, 1)

        @block.scalar
        def _(act):
            act.wait_ge(consts_in, 32)
            act.activation(cs[:, :, :], cc[:, :, :], ACT.Silu).then_inc(cond_silu, 1)
            for t in range(TILES):
                act.wait_ge(x_in[t], 16)
                act.activation(junk[:, :], x[:, t], ACT.Square, accum_out=stat[:, 0, t:t + 1]).then_inc(squares, 1)
                act.wait_ge(squares, t + 1)
            act.wait_ge(dve_own, 1)
            act.activation(stat[:, 2], stat[:, 1], ACT.Sqrt).then_inc(std_set, 1)
            act.wait_ge(mod_half, 2)
            for n in range(0, 24, 2):
                feature_evac(act, c, tp, turned, act_evac, n, 0, c.h)

        @block.vector
        def _(dve):
            dve.wait_ge(squares, TILES)
            dve.tensor_scalar(stat[:, 1], stat[:, 0], 1.0 / D, NORM_EPS, ALU.mult, ALU.add).then_inc(dve_own, 1)
            dve.wait_ge(std_set, 1)
            dve.reciprocal(stat[:, 1], stat[:, 2]).then_inc(dve_own, 1)
            dve.wait_ge(dve_own, 2)
            for t in range(TILES):
                dve.tensor_scalar(x[:, t], x[:, t], stat[:, 1, t:t + 1], None, ALU.mult).then_inc(x_scaled, 1)
            dve.wait_ge(w_used, 4)
            dve.tensor_tensor(c.mod[:, 0:16, :], pm[:, 0:16, :],
                              c.vec[:, 0:16].unsqueeze(2).to_broadcast([P, 16, 2]), ALU.add).then_inc(mod_half, 1)
            dve.wait_ge(mod_half, 1)
            dve.scalar_tensor_tensor(c.gain[:, 0], c.mod[:, 8:16, :], 1.0,
                                     c.vec[:, VEC["norm1_g"]:VEC["norm1_g"] + 8].unsqueeze(2).to_broadcast([P, 8, 2]),
                                     ALU.add, ALU.mult).then_inc(mod_half, 1)
            dve.wait_ge(mod_half, 2)
            for n in range(1, 24, 2):
                feature_evac(dve, c, tp, turned, dve_evac, n, 0, c.h)
            dve.wait_ge(w_used, 12)
            dve.tensor_tensor(c.mod[:, 16:48, :], pm[:, 16:48, :],
                              c.vec[:, 16:48].unsqueeze(2).to_broadcast([P, 32, 2]), ALU.add).then_inc(mod_set, 1)
            dve.wait_ge(mod_set, 1)
            dve.scalar_tensor_tensor(c.gain[:, 1], c.mod[:, 32:40, :], 1.0,
                                     c.vec[:, VEC["norm2_g"]:VEC["norm2_g"] + 8].unsqueeze(2).to_broadcast([P, 8, 2]),
                                     ALU.add, ALU.mult).then_inc(mod_set, 1)

        @block.tensor
        def _(pe):
            pe.wait_ge(cond_silu, 1)

            def modulation(g):
                pe.wait_ge(w_in[g % WRING], 16 * (g // WRING + 1))
                for j in range(4):
                    for k in range(KD):
                        mm = pe.matmul(pm[:, 4 * g + j, :], wmod[:, g % WRING, k, j * P:(j + 1) * P], cs[:, k, :],
                                       start=(k == 0), stop=(k == KD - 1))
                mm.then_inc(w_used, 1)
            for g in range(4):
                modulation(g)
            pe.wait_ge(ident_set, 2)
            for n in range(24):
                feature_turn(pe, c, x, tp, turned, act_evac, dve_evac, x_scaled, n)
            for g in range(4, 12):
                modulation(g)


def feature_turn(pe, c, x, tp, turned, act_evac, dve_evac, x_scaled, n):
    b, k = divmod(n, KD)
    first, width = BLOCKS[b]
    if k == 0:
        pe.wait_ge(x_scaled, (first + width) // P)
    if n >= 4:
        pe.wait_ge(act_evac if n % 2 == 0 else dve_evac, (n - 4) // 2 + 1)
    for i in range(width // P):
        mm = pe.transpose(tp[:, n % 4, i * P:(i + 1) * P], x[:, first // P + i, k * P:(k + 1) * P], c.ident[:, :])
    mm.then_inc(turned, 1)


def feature_evac(eng, c, tp, turned, evac, n, norm, h):
    b, k = divmod(n, KD)
    first, width = BLOCKS[b]
    s = 0 if b == 0 else 1
    gain = c.gain[:, norm, k, s:s + 1]
    shift = c.mod[:, 24 * norm + k, s:s + 1]
    eng.wait_ge(turned, n + 1)
    out, src = h[:, k, first:first + width], tp[:, n % 4, 0:width]
    if n % 2 == 0:
        eng.activation(out, src, ACT.Identity, bias=shift, scale=gain).then_inc(evac, 1)
    else:
        eng.tensor_scalar(out, src, gain, shift, ALU.mult, ALU.add).then_inc(evac, 1)


def phase_b(c):
    nc, io = c.nc, c.io
    with ExitStack() as ctx:
        sem = semaphores(nc, ctx)
        w = ctx.enter_context(nc.sbuf_tensor("b_w", [P, 2, KD, 256], F32))
        stage = ctx.enter_context(nc.sbuf_tensor("b_stage", [P, 4, NT], F32))
        ps = [ctx.enter_context(nc.psum_tensor(f"b_ps{i}", [P, 3, 512], F32)) for i in range(2)]
        w_in = [sem(f"b_w_in{i}") for i in range(2)]
        projected, copied, bank_free = sem("b_projected"), sem("b_copied"), sem("b_bank_free")
        sig_part, sig_set, padded = sem("b_sig_part"), sem("b_sig_set"), sem("b_padded")
        sig_stored = [sem(f"b_sig_stored{i}") for i in range(4)]
        block = ctx.enter_context(nc.Block())

        def load(sp, i, g):
            sp.dma_start(w[:, g], io["w_in"][bass.ds(i * 2 + g, 1)].rearrange("o p k n -> p (o k) n")).then_inc(w_in[g], 16)

        @block.sync
        def _(sp):
            for g in range(2):
                load(sp, 0, g)
            with sp.Fori(1, 7) as i:
                for g in range(2):
                    sp.wait_ge(projected, i * 4 + (2 * g - 2))
                    load(sp, i, g)

        @block.tensor
        def _(pe):
            def project(j):
                for n, (first, width) in enumerate(BLOCKS):
                    for k in range(KD):
                        mm = pe.matmul(ps[j % 2][:, n, 0:width], w[:, j // 2, k, (j % 2) * P:(j % 2 + 1) * P],
                                       c.h[:, k, first:first + width], start=(k == 0), stop=(k == KD - 1))
                mm.then_inc(projected, 1)
            for f in range(8):
                if f % 2 == 0:
                    pe.wait_ge(w_in[f % 4 // 2], 16 * (f // 4 + 1))
                if f >= 2:
                    pe.wait_ge(copied, f - 1)
                project(f % 4)
            with pe.Fori(0, 5) as i:
                for j in range(4):
                    if j % 2 == 0:
                        pe.wait_ge(w_in[j // 2], i * 16 + 48)
                    pe.wait_ge(bank_free, i * 4 + (j + 1))
                    project(j)

        @block.vector
        def _(dve):
            dve.memset(c.xa[:, :, 0:1], 0.0).then_inc(padded, 1)
            dve.memset(c.xa[:, :, PROMPT + 1:PROMPT + 3], 0.0).then_inc(padded, 1)
            dve.memset(c.xa[:, :, XA_PAD - 1:XA_PAD], 0.0).then_inc(padded, 1)
            for f in range(8):
                dve.wait_ge(projected, f + 1)
                for n, (first, width) in enumerate(BLOCKS):
                    at = xa_col(first)
                    out = c.xa[:, f, at:at + width] if f < 4 else c.y[:, f - 4, first:first + width]
                    cp = dve.tensor_copy(out, ps[f % 2][:, n, 0:width])
                cp.then_inc(copied, 1)

        @block.scalar
        def _(act):
            for j in range(2):
                act.wait_ge(copied, 7 + j)
                act.sem_inc(bank_free, 1)
            def sigmoids(i):
                for j in range(4):
                    act.wait_ge(projected, i * 4 + (8 + j + 1))
                    wait_reuse(act, sig_stored[j], i * 16)
                    for n, (first, width) in enumerate(BLOCKS):
                        a = act.activation(stage[:, j, first:first + width], ps[j % 2][:, n, 0:width], ACT.Sigmoid)
                        if n < 2:
                            a.then_inc(sig_part, 1)
                    a.then_inc(sig_set, 1)
                    act.wait_ge(sig_set, i * 4 + (j + 1))
                    act.sem_inc(bank_free, 1)
            sigmoids(0)
            with act.Fori(1, 5) as i:
                sigmoids(i)

        @block.gpsimd
        def _(pool):
            with pool.Fori(0, 5) as i:
                for j in range(4):
                    pool.wait_ge(sig_set, i * 4 + (j + 1))
                    pool.wait_ge(sig_part, i * 8 + (2 * j + 2))
                    pool.dma_start(c.sig[bass.ds(i * 4 + j, 1)].rearrange("o p t -> p (o t)"), stage[:, j]).then_inc(sig_stored[j], 16)
            for j in range(4):
                pool.wait_ge(sig_stored[j], 5 * 16)


CH = 128
NCH = NT // CH
BH = 4
ROWS = 36
BIG = 1e30
CONV_STEPS = BH * (1 + 8 + 2)
GATE_STEPS = 19


def phase_c_prepare(c):
    nc, io = c.nc, c.io
    with ExitStack() as ctx:
        def sb(name, shape):
            return ctx.enter_context(nc.sbuf_tensor(name, shape, F32))

        sem = semaphores(nc, ctx)
        uc = c.y[:, 4:8]
        w = sb("c_w", [P, 3, BH, P])
        wif = sb("c_wif", [P, BH, 2, ROWS])
        bif = sb("c_bif", [ROWS, 2])
        gb, keep = sb("c_beta_rows", [ROWS, NT]), sb("c_keep", [ROWS, NT])
        lf, li = c.rows[:, 1], c.rows[:, 2]
        mprev = sb("c_mprev", [ROWS, NCH])
        ps = [ctx.enter_context(nc.psum_tensor(f"c_ps{i}", [P, 3, 512], F32)) for i in range(2)]
        pt = ctx.enter_context(nc.psum_tensor("c_pt", [P, 2, BH, P], F32))
        loaded, conv_done, uc_set = sem("c_loaded"), sem("c_conv_done"), sem("c_uc_set")
        wide_ready, wide_act, wide_dve = sem("c_wide_ready"), sem("c_wide_act"), sem("c_wide_dve")
        tok_ready, tok_read = sem("c_tok_ready"), sem("c_tok_read")
        gate_act, gate_dve = sem("c_gate_act"), sem("c_gate_dve")
        masks, masks_pool = sem("c_masks"), sem("c_masks_pool")
        beta_turned = sem("c_beta_turned")
        conv = VEC["mlstm_conv"]
        block = ctx.enter_context(nc.Block())

        @block.sync
        def _(sp):
            sp.dma_start(w[:, :, :, :], io["w_qkv"]).then_inc(loaded, 16)
            sp.dma_start(wif[:, :, :, :], io["w_if"]).then_inc(loaded, 16)
            sp.dma_start(bif[:, :], io["b_if"]).then_inc(loaded, 16)
            sp.dma_start(c.m0[:, :], io["m0"]).then_inc(loaded, 16)
            sp.dma_start(c.cn[:, 1, :, 0:P], io["c0"]).then_inc(loaded, 16)
            sp.dma_start(c.n0[:, :], io["n0"]).then_inc(loaded, 16)

        @block.gpsimd
        def _(pool):
            pool.memset(c.cmask[:, :, :], 0.0).then_inc(masks_pool, 1)
            pool.wait_ge(masks_pool, 1)
            for d in range(2):
                sgn = 1 - 2 * d
                pool.affine_select(out=c.cmask[:, d], in_=c.cmask[:, d], compare_op=ALU.is_ge, fill=-BIG, base=0,
                                   pattern=[[sgn, CH]], channel_multiplier=-sgn).then_inc(masks, 1)
            pool.memset(keep[:, :], 1.0).then_inc(masks_pool, 1)
            pool.wait_ge(masks_pool, 2)
            for d in range(2):
                part = keep[32 * d:32 * d + 4, :].rearrange("p (n t) -> p n t", t=CH)
                at = (CH - 1) * d
                pool.memset(part[:, :, at:at + 1], 0.0).then_inc(masks, 1)

        @block.tensor
        def _(pe):
            def wide(n, lhs, rhs, rows):
                if n >= 2:
                    pe.wait_ge(wide_act if n % 2 == 0 else wide_dve, (n - 2) // 2 + 1)
                for m, (first, width) in enumerate(BLOCKS):
                    for k in range(len(lhs)):
                        mm = pe.matmul(ps[n % 2][0:rows, m, 0:width], lhs[k], rhs[k][:, first:first + width],
                                       start=(k == 0), stop=(k == len(lhs) - 1))
                mm.then_inc(wide_ready, 1)

            def tok(n, src, which):
                if n >= 2:
                    pe.wait_ge(tok_read, n - 1)
                t = n % NCH
                for h in range(BH):
                    mm = pe.matmul(pt[:, n % 2, h], src[:, h, t * P:(t + 1) * P], w[:, which, h], start=True, stop=True)
                mm.then_inc(tok_ready, 1)
            pe.wait_ge(loaded, 96)
            for n in range(NCH):
                tok(n, c.y, 2)
            pe.wait_ge(uc_set, BH)
            for g in range(2):
                wide(g, [wif[:, k, g, :] for k in range(BH)], [uc[:, k] for k in range(BH)], ROWS)
            for h in range(BH):
                for which in range(2):
                    wide(2 + 2 * h + which, [w[:, which, h]], [uc[:, h]], P)
            for n in range(NCH, 2 * NCH):
                tok(n, uc, 1)
            pe.wait_ge(wide_act, 1 + BH)
            pe.wait_ge(gate_dve, GATE_STEPS)
            for ch in range(NCH):
                mm = pe.transpose(ps[0][:, 0, ch * ROWS:(ch + 1) * ROWS], gb[:, ch * CH:(ch + 1) * CH], c.ident[0:ROWS, 0:ROWS])
            mm.then_inc(beta_turned, 1)

        @block.vector
        def _(dve):
            own = Own(dve, conv_done)
            last = [0] * BH
            for tap, (dy, dx) in enumerate([(1, 1)] + [(a, b) for a in range(3) for b in range(3) if (a, b) != (1, 1)]):
                for k in range(BH):
                    wcol = c.vec[:, conv + (3 * dy + dx) * BH + k:conv + (3 * dy + dx) * BH + k + 1]
                    u_lat = c.y[:, k, PROMPT:].rearrange("p (r w) -> p r w", w=64)
                    o_lat = uc[:, k, PROMPT:].rearrange("p (r w) -> p r w", w=64)
                    if tap == 0:
                        last[k] = own.did(dve.tensor_scalar(uc[:, k], c.y[:, k], wcol, None, ALU.mult))
                        continue
                    dve.wait_ge(conv_done, last[k])
                    r0, r1 = max(0, 1 - dy), 16 - max(0, dy - 1)
                    x0, x1 = max(0, 1 - dx), 64 - max(0, dx - 1)
                    o = o_lat[:, r0:r1, x0:x1]
                    last[k] = own.did(dve.scalar_tensor_tensor(
                        o, u_lat[:, r0 + dy - 1:r1 + dy - 1, x0 + dx - 1:x1 + dx - 1], wcol, o, ALU.mult, ALU.add))
                    if dy == 1:
                        x0, x1 = max(0, 1 - dx), PROMPT - max(0, dx - 1)
                        o = uc[:, k, x0:x1]
                        last[k] = own.did(dve.scalar_tensor_tensor(
                            o, c.y[:, k, x0 + dx - 1:x1 + dx - 1], wcol, o, ALU.mult, ALU.add))
            assert own.n == CONV_STEPS, own.n
            own = Own(dve, gate_dve)
            own.did(dve.memset(c.rows[:, 3], 0.0))
            dve.wait_ge(wide_ready, 2)
            dve.wait_ge(loaded, 96)
            for m, (first, width) in enumerate(BLOCKS):
                cp = dve.tensor_scalar(lf[:, first:first + width], ps[1][0:ROWS, m, 0:width], bif[:, 1:2], None, ALU.add)
                cp.then_inc(wide_dve if m == 2 else gate_dve, 1)
            own.n += 2
            for h in range(BH):
                dve.wait_ge(wide_ready, 2 + 2 * h + 2)
                for m, (first, width) in enumerate(BLOCKS):
                    cp = dve.tensor_scalar(c.kt[:, h, first:first + width], ps[1][:, m, 0:width], P ** -0.5, None, ALU.mult)
                cp.then_inc(wide_dve, 1)
            dve.wait_ge(gate_act, 3)
            own.did(dve.scalar_tensor_tensor(lf[:, :], lf[:, :], 0.0, gb[:, :], ALU.min, ALU.subtract))
            own.settle()
            dve.wait_ge(masks, 4)
            b, m = gb, c.rows[:, 3]
            fwd, bwd = (slice(0, 4), slice(None)), (slice(32, 36), slice(None, None, -1))
            for rows, step in (fwd, bwd):
                own.did(dve.tensor_tensor_scan(b[rows, step], keep[rows, step], lf[rows, step], 0.0, ALU.mult, ALU.add))
                for s, (first, width) in enumerate(STREAMS):
                    def part(t):
                        v = t[rows, first:first + width]
                        return v if step.step is None else v[:, ::-1]
                    own.did(dve.tensor_tensor_scan(part(m), part(lf), part(li), c.m0[rows, 0:1] if s else 0.0,
                                                   ALU.add, ALU.max))
            own.settle()
            mc = m.rearrange("p (n t) -> p n t", t=CH)
            own.did(dve.memset(mprev[:, :], 0.0))
            own.settle()
            own.did(dve.tensor_copy(mprev[0:4, 1:NCH], mc[0:4, 0:NCH - 1, CH - 1]))
            own.did(dve.tensor_copy(mprev[32:36, 0:NCH - 1], mc[32:36, 1:NCH, 0]))
            own.settle()
            edges = (0, PROMPT // CH, NCH)
            own.did(dve.tensor_copy(mprev[0:4, edges[1]:edges[1] + 1], c.m0[0:4, 0:1]))
            own.did(dve.tensor_copy(mprev[32:36, NCH - 1:NCH], c.m0[32:36, 0:1]))
            own.did(dve.memset(mprev[32:36, edges[1] - 1:edges[1]], 0.0))
            own.did(dve.tensor_tensor(c.rows[:, 0], b[:, :], m, ALU.subtract))
            own.settle()
            own.did(dve.tensor_tensor(b[:, :], li[:, :], b[:, :], ALU.subtract))
            own.did(dve.tensor_tensor(c.rows[:, 1].rearrange("p (n t) -> p n t", t=CH),
                                      c.rows[:, 0].rearrange("p (n t) -> p n t", t=CH),
                                      mprev[:, :].unsqueeze(2).to_broadcast([ROWS, NCH, CH]), ALU.add))
            own.settle()
            assert own.n == GATE_STEPS, own.n
            for d in range(2):
                own.did(dve.tensor_copy(c.sel[:, 4 * d:4 * d + 4, :],
                                        c.ident[0:ROWS, 32 * d:32 * d + 4].unsqueeze(2).to_broadcast([ROWS, 4, P])))
            own.did(dve.memset(c.cn[:, 0], 0.0))
            own.did(dve.tensor_copy(c.cn[:, 1, :, P:2 * P], c.n0[:, :].unsqueeze(2).to_broadcast([P, 8, P])))
            own.did(dve.tensor_scalar(c.mean[:, :], c.ones[:, :], 1.0 / P, None, ALU.mult))
            own.settle()
            own.did(dve.tensor_tensor(c.center[:, :], c.ident[:, :], c.mean[:, :], ALU.subtract))
            dve.wait_ge(beta_turned, 1)
            own.did(dve.tensor_copy(c.betat[:, :, :], ps[0][:, 0, 0:NCH * ROWS].rearrange("p (n r) -> p n r", r=ROWS)))

        @block.scalar
        def _(act):
            for n in range(NCH):
                act.wait_ge(tok_ready, n + 1)
                act.activation(c.vtok[:, n], pt[:, n % 2], ACT.Copy).then_inc(tok_read, 1)
            act.wait_ge(conv_done, CONV_STEPS)
            for k in range(BH):
                act.activation(uc[:, k], uc[:, k], ACT.Silu).then_inc(uc_set, 1)
            act.wait_ge(loaded, 96)
            act.wait_ge(wide_ready, 1)
            for m, (first, width) in enumerate(BLOCKS):
                cp = act.activation(li[:, first:first + width], ps[0][0:ROWS, m, 0:width], ACT.Identity, bias=bif[:, 0:1])
                cp.then_inc(wide_act if m == 2 else uc_set, 1)
            for h in range(BH):
                act.wait_ge(wide_ready, 2 + 2 * h + 1)
                for m, (first, width) in enumerate(BLOCKS):
                    cp = act.activation(c.qt[:, h, first:first + width], ps[0][:, m, 0:width], ACT.Copy)
                cp.then_inc(wide_act, 1)
            act.wait_ge(wide_dve, 1)
            act.wait_ge(gate_dve, 3)
            for n, (func, src, kw) in enumerate([(ACT.Abs, lf, {}), (ACT.Exp, gb, {"scale": -1.0}), (ACT.Ln, gb, {"bias": 1.0})]):
                if n:
                    act.wait_ge(gate_act, n)
                act.activation(gb[:, :], src[:, :], func, **kw).then_inc(gate_act, 1)
            for n in range(NCH, 2 * NCH):
                act.wait_ge(tok_ready, n + 1)
                act.activation(c.ktok[:, n - NCH], pt[:, n % 2], ACT.Copy, scale=P ** -0.5).then_inc(tok_read, 1)
            act.wait_ge(gate_dve, GATE_STEPS)
            act.activation(c.rows[:, 1], c.rows[:, 1], ACT.Exp).then_inc(gate_act, 1)
            act.activation(c.rows[:, 2], c.rows[:, 3], ACT.Exp, scale=-1.0).then_inc(gate_act, 1)


def phase_c_scan(c):
    nc, io = c.nc, c.io
    order = []
    np_, ns = PROMPT // CH, SAMPLE // CH
    for i in range(ns):
        order += [(1, 0, np_ + i), (1, 1, np_ + ns - 1 - i)]
        if i < np_:
            order += [(0, 0, i), (0, 1, np_ - 1 - i)]
    before, seen, first_of = [], {}, {}
    for j, (s, d, ch) in enumerate(order):
        before.append(seen.get((s, d)))
        seen[(s, d)] = j
        first_of.setdefault(ch, j)
    N = len(order)
    seconds = [sum(first_of[ch] != i for i, (_, _, ch) in enumerate(order[:j])) for j in range(N)]
    with ExitStack() as ctx:
        def sb(name, shape):
            return ctx.enter_context(nc.sbuf_tensor(name, shape, F32))

        def pb(name, shape):
            return ctx.enter_context(nc.psum_tensor(name, shape, F32))

        sem = semaphores(nc, ctx)
        expo, sd, qi, kw = (sb(f"s_{n}", [P, 2, BH, P]) for n in ("expo", "sd", "qi", "kw"))
        hn = sb("s_hn", [P, BH, P])
        absd = sb("s_absd", [P, BH, P])
        decay = sb("s_decay", [P, 2, BH])
        p_ab, p_ib, p_st, p_nu, p_de = pb("s_ab", [P, 2, BH, P]), pb("s_ib", [P, BH, P]), pb("s_st", [P, BH, P]), pb("s_nu", [P, BH, P]), pb("s_de", [P, BH, P])
        p_dc = pb("s_dc", [P, BH, 2 * P])
        ab_ready, ib_ready, st_ready, nd_ready, en_ready, dc_ready = (sem(f"s_{n}_ready") for n in ("ab", "ib", "st", "nd", "en", "dc"))
        e1_set, qi_set, sd_set, cn_set, mx_set, h_set, dve_own = (sem(f"s_{n}") for n in ("e1_set", "qi_set", "sd_set", "cn_set", "mx_set", "h_set", "dve_own"))
        exp_set, abs_set, kw_set, added, stored = (sem(f"s_{n}") for n in ("exp_set", "abs_set", "kw_set", "added", "stored"))
        kw_part, n_set = sem("s_kw_part"), sem("s_n_set")
        block = ctx.enter_context(nc.Block())

        def row(which, ch):
            return c.rows[:, which, ch * CH:(ch + 1) * CH]

        @block.tensor
        def _(pe):
            def spread(bank, which, j, ready):
                s, d, ch = order[j]
                for h in range(BH):
                    mm = pe.matmul(bank[:, h], c.sel[:, 4 * d + h], row(which, ch), start=True, stop=True)
                mm.then_inc(ready, 1)

            def alpha_inter(j):
                if j >= 2:
                    pe.wait_ge(mx_set, j - 1)
                spread(p_ab[:, j % 2], 0, j, ab_ready)
                if j >= 1:
                    pe.wait_ge(qi_set, j)
                spread(p_ib, 1, j, ib_ready)

            def scores(j):
                s, d, ch = order[j]
                if j >= 1:
                    pe.wait_ge(sd_set, j)
                for h in range(BH):
                    mm = pe.matmul(p_st[:, h], c.kt[:, h, ch * CH:(ch + 1) * CH], c.qt[:, h, ch * CH:(ch + 1) * CH], start=True, stop=True)
                mm.then_inc(st_ready, 1)
            alpha_inter(0)
            scores(0)
            for j, (s, d, ch) in enumerate(order):
                if j + 1 < N:
                    alpha_inter(j + 1)
                pe.wait_ge(qi_set, j + 1)
                pe.wait_ge(sd_set, j + 1)
                if before[j] is not None:
                    pe.wait_ge(cn_set, before[j] + 1)
                if j >= 1:
                    pe.wait_ge(h_set, j)
                    pe.wait_ge(abs_set, j)
                for h in range(BH):
                    cn = c.cn[:, s, 4 * d + h]
                    pe.matmul(p_nu[:, h], c.vtok[:, ch, h], sd[:, j % 2, h], start=True, stop=False)
                    pe.matmul(p_nu[:, h], cn[:, 0:P], qi[:, j % 2, h], start=False, stop=True)
                for h in range(BH):
                    cn = c.cn[:, s, 4 * d + h]
                    pe.matmul(p_de[:, h], c.ones[:, :], sd[:, j % 2, h], start=True, stop=False)
                    mm = pe.matmul(p_de[:, h], cn[:, P:2 * P], qi[:, j % 2, h], start=False, stop=True)
                mm.then_inc(nd_ready, 1)
                if j + 1 < N:
                    scores(j + 1)
                pe.wait_ge(e1_set, j + 1)
                spread(p_ab[:, j % 2], 2, j, en_ready)
                pe.wait_ge(kw_set, j + 1)
                if j >= 1:
                    pe.wait_ge(cn_set, j)
                for h in range(BH):
                    pe.matmul(p_dc[:, h, 0:P], kw[:, j % 2, h], c.vtok[:, ch, h], start=True, stop=True)
                    mm = pe.matmul(p_dc[:, h, P:2 * P], kw[:, j % 2, h], c.ones[:, :], start=True, stop=True)
                mm.then_inc(dc_ready, 1)

        @block.vector
        def _(dve):
            own = Own(dve, dve_own)
            def finish(j):
                s, d, ch = order[j]
                dve.wait_ge(dc_ready, j + 1)
                for h in range(BH):
                    cn = c.cn[:, s, 4 * d + h]
                    cp = dve.scalar_tensor_tensor(cn, cn, decay[:, j % 2, h:h + 1], p_dc[:, h], ALU.mult, ALU.add)
                    if h < BH - 1:
                        own.did(cp)
                own.settle()
                cp.then_inc(cn_set, 1)
                if seen[(0, d)] == j and s == 0:
                    dve.wait_ge(cn_set, j + 1)
                    dve.tensor_copy(c.n0[:, 4 * d:4 * d + 4], c.cn[:, 0, 4 * d:4 * d + 4, P]).then_inc(n_set, 1)
                dve.wait_ge(en_ready, j + 1)
                dve.wait_ge(abs_set, j + 1)
                dve.tensor_tensor(absd[:, :, :], absd[:, :, :], p_ab[:, j % 2], ALU.max).then_inc(mx_set, 1)
                dve.wait_ge(mx_set, j + 1)
                own.did(dve.reciprocal(absd[:, :, :], absd[:, :, :]))
                own.settle()
                dve.wait_ge(nd_ready, j + 1)
                out = c.y[:, 4:8, ch * CH:(ch + 1) * CH]
                if first_of[ch] != j:
                    out = hn[:, :, :]
                    if seconds[j] > 0:
                        dve.wait_ge(added, seconds[j])
                dve.tensor_tensor(out, absd[:, :, :], p_nu[:, :, :], ALU.mult).then_inc(h_set, 1)

            for j, (s, d, ch) in enumerate(order):
                dve.wait_ge(ab_ready, j + 1)
                for h in range(BH):
                    cp = dve.scalar_tensor_tensor(expo[:, j % 2, h], p_ab[:, j % 2, h],
                                                  c.betat[:, ch, 32 * d + h:32 * d + h + 1], c.cmask[:, d], ALU.add, ALU.min)
                    if h < BH - 1:
                        own.did(cp)
                own.settle()
                cp.then_inc(e1_set, 1)
                dve.wait_ge(ib_ready, j + 1)
                end = (CH - 1) * (1 - d)
                own.did(dve.tensor_copy(decay[:, j % 2], p_ib[:, :, end]))
                own.settle()
                dve.tensor_tensor(qi[:, j % 2], c.qt[:, :, ch * CH:(ch + 1) * CH], p_ib[:, :, :], ALU.mult).then_inc(qi_set, 1)
                if j >= 1:
                    finish(j - 1)
                dve.wait_ge(exp_set, j + 1)
                dve.wait_ge(st_ready, j + 1)
                dve.tensor_tensor(sd[:, j % 2], expo[:, j % 2], p_st[:, :, :], ALU.mult).then_inc(sd_set, 1)
            finish(N - 1)

        @block.scalar
        def _(act):
            for j in range(N):
                act.wait_ge(e1_set, j + 1)
                act.activation(expo[:, j % 2], expo[:, j % 2], ACT.Exp).then_inc(exp_set, 1)
                act.wait_ge(nd_ready, j + 1)
                if j >= 1:
                    act.wait_ge(h_set, j)
                act.activation(absd[:, :, :], p_de[:, :, :], ACT.Abs).then_inc(abs_set, 1)

        @block.gpsimd
        def _(pool):
            def add(j):
                s, d, ch = order[j]
                if first_of[ch] != j:
                    y = c.y[:, 4:8, ch * CH:(ch + 1) * CH]
                    pool.wait_ge(h_set, j + 1)
                    pool.tensor_tensor(y, y, hn[:, :, :], ALU.add).then_inc(added, 1)
            for j, (s, d, ch) in enumerate(order):
                end = (CH - 1) * (1 - d)
                pool.wait_ge(exp_set, j + 1)
                if j >= 2:
                    pool.wait_ge(dc_ready, j - 1)
                for h in range(BH):
                    cp = pool.tensor_scalar(kw[:, j % 2, h], c.ktok[:, ch, h], expo[:, j % 2, h, end:end + 1], None, ALU.mult)
                    cp.then_inc(kw_set if h == BH - 1 else kw_part, 1)
                if j >= 1:
                    add(j - 1)
            add(N - 1)

        @block.sync
        def _(sp):
            for d in range(2):
                sp.wait_ge(cn_set, seen[(0, d)] + 1)
                sp.dma_start(io["new_c"][d].rearrange("h k v -> k h v"), c.cn[:, 0, 4 * d:4 * d + 4, 0:P]).then_inc(stored, 16)
                sp.wait_ge(n_set, d + 1)
                sp.dma_start(io["new_n"][d], c.n0[:, 4 * d:4 * d + 4]).then_inc(stored, 16)
                at = (PROMPT - 1) * (1 - d)
                sp.dma_start(io["new_m"][d].rearrange("(h o) -> h o", o=1), c.rows[32 * d:32 * d + 4, 3, at:at + 1]).then_inc(stored, 16)
            sp.wait_ge(stored, 6 * 16)


def phase_c_norm(c):
    nc, io = c.nc, c.io
    with ExitStack() as ctx:
        def sb(name, shape):
            return ctx.enter_context(nc.sbuf_tensor(name, shape, F32))

        sem = semaphores(nc, ctx)
        so = sb("n_so", [P, BH, NT])
        sq, std, g = (sb(f"n_{n}", [P, 2, 512]) for n in ("sq", "std", "g"))
        eps = sb("n_eps", [P, 1])
        p_c = ctx.enter_context(nc.psum_tensor("n_pc", [P, 2, 512], F32))
        p_v = ctx.enter_context(nc.psum_tensor("n_pv", [P, 2, 512], F32))
        so_in, centered, squared, var_ready, std_set, dve_own, done, gone = (sem(f"n_{n}") for n in (
            "so_in", "centered", "squared", "var_ready", "std_set", "dve_own", "done", "gone"))
        block = ctx.enter_context(nc.Block())
        items = [(h, first, width) for h in range(BH) for first, width in BLOCKS]

        @block.sync
        def _(sp):
            sp.dma_start(so[:, :, :], c.sig[0:4].rearrange("h p t -> p h t")).then_inc(so_in, 16)

        @block.tensor
        def _(pe):
            def center(n):
                h, first, width = items[n]
                if n >= 2:
                    pe.wait_ge(done, n - 1)
                pe.matmul(p_c[:, n % 2, 0:width], c.center[:, :], c.y[:, 4 + h, first:first + width], start=True, stop=True).then_inc(centered, 1)
            center(0)
            for n, (h, first, width) in enumerate(items):
                if n + 1 < len(items):
                    center(n + 1)
                pe.wait_ge(squared, n + 1)
                if n >= 2:
                    pe.wait_ge(std_set, n - 1)
                pe.matmul(p_v[:, n % 2, 0:width], c.mean[:, :], sq[:, n % 2, 0:width], start=True, stop=True).then_inc(var_ready, 1)

        @block.scalar
        def _(act):
            act.wait_ge(dve_own, 1)
            for n, (h, first, width) in enumerate(items):
                act.wait_ge(centered, n + 1)
                act.activation(sq[:, n % 2, 0:width], p_c[:, n % 2, 0:width], ACT.Square).then_inc(squared, 1)
                act.wait_ge(var_ready, n + 1)
                if n >= 2:
                    act.wait_ge(done, n - 1)
                act.activation(std[:, n % 2, 0:width], p_v[:, n % 2, 0:width], ACT.Sqrt, bias=eps[:, 0:1]).then_inc(std_set, 1)

        @block.vector
        def _(dve):
            own = Own(dve, dve_own)
            own.did(dve.memset(eps[:, :], 1e-5))
            dve.wait_ge(so_in, 16)
            for n, (h, first, width) in enumerate(items):
                dve.wait_ge(std_set, n + 1)
                r = std[:, n % 2, 0:width]
                own.did(dve.reciprocal(r, r))
                own.did(dve.scalar_tensor_tensor(g[:, n % 2, 0:width], p_c[:, n % 2, 0:width],
                                                 c.vec[:, VEC["mlstm_ln_g"] + h:VEC["mlstm_ln_g"] + h + 1],
                                                 so[:, h, first:first + width], ALU.mult, ALU.mult))
                own.settle()
                dve.tensor_tensor(c.y[:, 4 + h, first:first + width], g[:, n % 2, 0:width], r, ALU.mult).then_inc(done, 1)
                dve.wait_ge(done, n + 1)


def phase_c(c):
    nc = c.nc
    with ExitStack() as ctx:
        def sb(name, shape):
            return ctx.enter_context(nc.sbuf_tensor(name, shape, F32))
        c.mean, c.center = sb("c_mean", [P, P]), sb("c_center", [P, P])
        with ExitStack() as inner:
            def sb(name, shape):
                return inner.enter_context(nc.sbuf_tensor(name, shape, F32))
            c.qt, c.kt = sb("c_qt", [P, BH, NT]), sb("c_kt", [P, BH, NT])
            c.ktok, c.vtok = sb("c_ktok", [P, NCH, BH, P]), sb("c_vtok", [P, NCH, BH, P])
            c.rows = sb("c_rows", [ROWS, 4, NT])
            c.betat = sb("c_betat", [P, NCH, ROWS])
            c.sel, c.cmask = sb("c_sel", [ROWS, 8, P]), sb("c_cmask", [P, 2, CH])
            c.cn = sb("c_cn", [P, 2, 8, 2 * P])
            c.m0, c.n0 = sb("c_m0", [ROWS, 1]), sb("c_n0", [P, 8])
            phase_c_prepare(c)
            phase_c_scan(c)
        phase_c_norm(c)


RC = 64
RCH = NT // RC
HEADS_P = 4
DECAY_C = 0.6065306597126334


def phase_d_project(c):
    nc, io = c.nc, c.io
    jobs = [("r", 0, 0, 4), ("k", 2, 4, 4), ("v", 3, 8, 4), ("w", 1, 12, 1), ("i", 4, 13, 1), ("g", 5, 14, 1)]
    RING = 6
    with ExitStack() as ctx:
        def sb(name, shape):
            return ctx.enter_context(nc.sbuf_tensor(name, shape, F32))

        sem = semaphores(nc, ctx)
        w = sb("d_w", [P, 4, 15, P])
        mix = sb("d_mix", [P, RING, NT])
        stage = sb("d_stage", [P, 3, NT])
        ps = [ctx.enter_context(nc.psum_tensor(f"d_ps{i}", [P, 3, 512], F32)) for i in range(2)]
        w_in, shift_own, mixed, chunk_ready, used = (sem(f"d_{n}") for n in ("w_in", "shift_own", "mixed", "chunk_ready", "used"))
        staged, staged_part = sem("d_staged"), sem("d_staged_part")
        stored = [sem(f"d_stored{i}") for i in range(3)]
        loaded, proj_read, hid_set = sem("d_loaded"), sem("d_proj_read"), sem("d_hid_set")
        chunks = [(name, j, f, col + f) for j, (name, _, col, n) in enumerate(jobs) for f in range(n)]
        xx = c.y
        block = ctx.enter_context(nc.Block())

        @block.sync
        def _(sp):
            sp.dma_start(w[:, :, :, :], io["w_rwkv"]).then_inc(w_in, 16)
            sp.dma_start(c.w2[:, :, :], io["w_rank"]).then_inc(loaded, 16)
            sp.dma_start(c.s_in[:, :, :, :], io["s0"]).then_inc(loaded, 16)
            count = [0] * 3
            n = 0
            for name, j, f, col in chunks:
                if name in "rkvg":
                    dst = c.rkv[{"r": 0, "k": 1, "v": 2}[name], f] if name != "g" else c.hid_g
                    sp.wait_ge(staged, n + 1)
                    sp.wait_ge(staged_part, 2 * n + 2)
                    sp.dma_start(dst, stage[:, n % 3]).then_inc(stored[n % 3], 16)
                    count[n % 3] += 16
                    n += 1
            for i in range(3):
                sp.wait_ge(stored[i], count[i])
            sp.wait_ge(loaded, 32)

        @block.vector
        def _(dve):
            own = Own(dve, shift_own)
            for s, (first, width) in enumerate(STREAMS):
                at = xa_col(first)
                own.did(dve.tensor_tensor(xx[:, 0:4, first:first + width], c.xa[:, :, at - 1:at - 1 + width],
                                          c.xa[:, :, at + 1:at + 1 + width], ALU.add))
            own.settle()
            for s, (first, width) in enumerate(STREAMS):
                at = xa_col(first)
                for k in range(4):
                    own.did(dve.scalar_tensor_tensor(xx[:, k, first:first + width], xx[:, k, first:first + width], 0.5,
                                                     c.xa[:, k, at:at + width], ALU.mult, ALU.subtract))
            own.settle()
            for q in range(4 * len(jobs)):
                j, k = divmod(q, 4)
                if q >= RING:
                    dve.wait_ge(used, (q - RING) // 4 + 1)
                mu = VEC["rwkv_mu"] + 4 * jobs[j][1] + k
                for s, (first, width) in enumerate(STREAMS):
                    cp = dve.scalar_tensor_tensor(mix[:, q % RING, first:first + width], xx[:, k, first:first + width],
                                                  c.vec[:, mu:mu + 1], c.xa[:, k, xa_col(first):xa_col(first) + width],
                                                  ALU.mult, ALU.add)
                    if s == 0:
                        own.did(cp)
                own.settle()
                cp.then_inc(mixed, 1)

        @block.tensor
        def _(pe):
            pe.wait_ge(w_in, 16)
            for n, (name, j, f, col) in enumerate(chunks):
                pe.wait_ge(mixed, 4 * j + 4)
                if n >= 2:
                    pe.wait_ge(proj_read, n - 1)
                for m, (first, width) in enumerate(BLOCKS):
                    for k in range(4):
                        mm = pe.matmul(ps[n % 2][:, m, 0:width], w[:, k, col], mix[:, (4 * j + k) % RING, first:first + width],
                                       start=(k == 0), stop=(k == 3))
                mm.then_inc(chunk_ready, 1)
                if f == jobs[j][3] - 1:
                    pe.wait_ge(chunk_ready, n + 1)
                    pe.sem_inc(used, 1)

        @block.scalar
        def _(act):
            n_st = 0
            for n, (name, j, f, col) in enumerate(chunks):
                func = {"w": ACT.Tanh, "g": ACT.Sigmoid}.get(name, ACT.Copy)
                act.wait_ge(chunk_ready, n + 1)
                if name in "wi":
                    dst = c.hid[:, "wi".index(name)]
                else:
                    dst = stage[:, n_st % 3]
                    if n_st >= 3:
                        act.wait_ge(stored[n_st % 3], 16 * (n_st // 3))
                for m, (first, width) in enumerate(BLOCKS):
                    a = act.activation(dst[:, first:first + width], ps[n % 2][:, m, 0:width], func)
                    a.then_inc((hid_set if name in "wi" else (staged_part if m < 2 else staged)), 1)
                if name in "wi":
                    act.wait_ge(hid_set, 3 * ("wi".index(name) + 1))
                else:
                    n_st += 1
                    act.wait_ge(staged, n_st)
                act.sem_inc(proj_read, 1)


def phase_d_prepare(c, p):
    nc, io = c.nc, c.io
    with ExitStack() as ctx:
        def sb(name, shape):
            return ctx.enter_context(nc.sbuf_tensor(name, shape, F32))

        sem = semaphores(nc, ctx, f"p{p}_")
        rk = sb(f"p{p}_rk", [P, 2, NT])
        sg = c.y[:, p]
        kn = c.xa[:, p, 0:NT]
        cum, eneg, av, kd, kds = (sb(f"p{p}_{n}", [P, NT]) for n in ("cum", "eneg", "av", "kd", "kds"))
        ps = [ctx.enter_context(nc.psum_tensor(f"p{p}_ps{i}", [P, 3, 512], F32)) for i in range(2)]
        loaded, wide_ready, banks_act, banks_dve = sem("loaded"), sem("wide_ready"), sem("banks_act"), sem("banks_dve")
        sq_set, sg_set, av_set, eneg_set, epos_set, ex_set = (sem(n) for n in ("sq_set", "sg_set", "av_set", "eneg_set", "epos_set", "ex_set"))
        cum_set, sx_set, own_dve, r_done, a_done = (sem(n) for n in ("cum_set", "sx_set", "own_dve", "r_done", "a_done"))
        r_done_p, a_done_p, b_set, bb_done, bb_done_p, bonus_in = (sem(n) for n in ("r_done_p", "a_done_p", "b_set", "bb_done", "bb_done_p", "bonus_in"))
        kd_done, neg_b = sem("kd_done"), sem("neg_b")
        block = ctx.enter_context(nc.Block())
        wide = [("u", 0), ("ss", 0), ("a", 0), ("u", 1), ("a", 1), ("bonus", 0)]
        reader = [banks_act, banks_act, banks_act, banks_act, banks_act, banks_dve]

        def vec(name, k):
            return c.vec[:, VEC[name] + k:VEC[name] + k + 1]

        def per_chunk(t):
            return t.rearrange("p (n t) -> p n t", t=RC)

        @block.sync
        def _(sp):
            sp.dma_start(rk[:, :, :], c.rkv[0:2, p].rearrange("w p t -> p w t")).then_inc(loaded, 16)
            sp.dma_start(c.v[:, :], c.rkv[2, p]).then_inc(loaded, 16)

        @block.tensor
        def _(pe):
            for n, (kind, d) in enumerate(wide):
                if n >= 2:
                    pe.wait_ge(banks_act, 3 * (n - 1))
                if kind == "ss":
                    pe.wait_ge(sq_set, 1)
                if kind == "bonus":
                    pe.wait_ge(bonus_in, 1)
                for m, (first, width) in enumerate(BLOCKS):
                    cols = slice(first, first + width)
                    if kind in "ua":
                        which, half = "ua".index(kind), slice(64 * d, 64 * d + 64)
                        lhs, rhs = c.w2[half, which, p * P:(p + 1) * P], c.hid[half, which, cols]
                    else:
                        lhs, rhs = c.blockones[:, :], (eneg if kind == "ss" else kd)[:, cols]
                    mm = pe.matmul(ps[n % 2][:, m, 0:width], lhs, rhs, start=True, stop=True)
                mm.then_inc(wide_ready, 1)

        @block.scalar
        def _(act):
            def from_banks(n, out, func, done, **kw):
                act.wait_ge(wide_ready, n + 1)
                for m, (first, width) in enumerate(BLOCKS):
                    act.activation(out[:, first:first + width], ps[n % 2][:, m, 0:width], func, **kw).then_inc(banks_act, 1)
                act.wait_ge(banks_act, 3 * (n + 1))
                act.sem_inc(done, 1)
            act.wait_ge(loaded, 32)
            act.activation(eneg[:, :], rk[:, 1], ACT.Square, scale=vec("rwkv_k_k", p)).then_inc(sq_set, 1)
            from_banks(0, sg, ACT.Sigmoid, sg_set, bias=vec("rwkv_w0", p))
            from_banks(1, kn, ACT.Sqrt, sq_set)
            from_banks(2, av, ACT.Sigmoid, av_set, bias=vec("rwkv_a0", p))
            for d in range(2):
                if d == 1:
                    act.wait_ge(a_done, 1)
                    act.wait_ge(a_done_p, 1)
                    from_banks(3, sg, ACT.Sigmoid, sg_set, bias=vec("rwkv_w0", 4 + p))
                    act.wait_ge(neg_b, 1)
                    act.wait_ge(b_set, 2)
                    from_banks(4, av, ACT.Sigmoid, av_set, bias=vec("rwkv_a0", 4 + p))
                act.wait_ge(cum_set, 5 * (d + 1))
                if d == 0:
                    act.wait_ge(wide_ready, 2)
                else:
                    act.wait_ge(r_done, 2)
                    act.wait_ge(r_done_p, 1)
                act.activation(eneg[:, :], cum[:, :], ACT.Exp, scale=-DECAY_C).then_inc(eneg_set, 1)
                act.wait_ge(sx_set, d + 1)
                act.activation(sg, sg, ACT.Exp, scale=-DECAY_C).then_inc(ex_set, 1)
                act.wait_ge(eneg_set, d + 1)
                act.activation(cum[:, :], cum[:, :], ACT.Exp, scale=DECAY_C).then_inc(epos_set, 1)

        @block.vector
        def _(dve):
            own = Own(dve, own_dve)

            def normalize_key():
                dve.wait_ge(sq_set, 2)
                own.did(dve.tensor_scalar(kn[:, :], kn[:, :], 1e-12, None, ALU.max))
                own.settle()
                own.did(dve.reciprocal(kn[:, :], kn[:, :]))
                own.settle()
                own.did(dve.scalar_tensor_tensor(kn[:, :], rk[:, 1], vec("rwkv_k_k", p), kn[:, :], ALU.mult, ALU.mult))
                own.settle()
            for d in range(2):
                step = slice(None, None, 1 - 2 * d)
                dve.wait_ge(sg_set, d + 1)
                if d == 1:
                    dve.wait_ge(b_set, 2)
                for b in range(5):
                    cols = slice(256 * b, 256 * b + 256)
                    dve.tensor_tensor_scan(cum[:, cols][:, step], c.keep[:, :], sg[:, cols][:, step], 0.0,
                                           ALU.mult, ALU.add).then_inc(cum_set, 1)
                if d == 0:
                    normalize_key()
                dve.wait_ge(av_set, d + 1)
                kdd = kds if d == 0 else kd
                own.did(dve.tensor_scalar(kdd[:, :], av[:, :], vec("rwkv_k_a", p), c.one_less_ka[:, p:p + 1], ALU.mult, ALU.add))
                own.settle()
                own.did(dve.tensor_tensor(kdd[:, :], kdd[:, :], rk[:, 1], ALU.mult))
                dve.scalar_tensor_tensor(av[:, :], kn[:, :], -1.0, av[:, :], ALU.mult, ALU.mult).then_inc(neg_b, 1)
                own.settle()
                dve.wait_ge(eneg_set, d + 1)
                for first, width in STREAMS:
                    chunks = slice(first // RC, (first + width) // RC)
                    own.did(dve.tensor_copy(c.pend[:, chunks, d], per_chunk(eneg[:, :])[:, chunks][:, step, (RC - 1) * (1 - d)]))
                dve.tensor_tensor(c.ar[0:64, d, :, 1, 0, :], per_chunk(rk[0:64, 0]), per_chunk(eneg[0:64, :]), ALU.mult).then_inc(r_done, 1)
                own.settle()
                dve.sem_inc(r_done, 1)
                dve.wait_ge(ex_set, d + 1)
                dve.tensor_tensor(c.ar[0:64, d, :, 0, 0, :], per_chunk(kn[0:64, :]), per_chunk(sg[0:64]), ALU.mult).then_inc(a_done, 1)
                dve.wait_ge(epos_set, d + 1)
                dve.wait_ge(neg_b, d + 1)
                dve.tensor_tensor(c.kb[:, d, :, 1, :], per_chunk(av[:, :]), per_chunk(cum[:, :]), ALU.mult).then_inc(b_set, 1)
                dve.tensor_tensor(c.kb[:, d, :, 0, :], per_chunk(kdd[:, :]), per_chunk(cum[:, :]), ALU.mult).then_inc(b_set, 1)
                dve.wait_ge(b_set, 2 * d + 1)
                dve.tensor_copy(c.bb[0:64, d, :, 0, :], c.kb[0:64, d, :, 1, :]).then_inc(bb_done, 1)
            dve.wait_ge(b_set, 4)
            own.did(dve.tensor_tensor(kds[:, :], kds[:, :], kd[:, :], ALU.add))
            own.settle()
            dve.scalar_tensor_tensor(kd[:, :], rk[:, 0], vec("rwkv_r_k", p), kds[:, :], ALU.mult, ALU.mult).then_inc(bonus_in, 1)
            dve.wait_ge(wide_ready, 6)
            dve.wait_ge(a_done_p, 2)
            dve.wait_ge(a_done, 2)
            for m, (first, width) in enumerate(BLOCKS):
                own.did(dve.tensor_tensor(c.y[:, p, first:first + width], c.v[:, first:first + width], ps[1][:, m, 0:width], ALU.mult))
            own.settle()

        @block.gpsimd
        def _(pool):
            for d in range(2):
                if d == 1:
                    pool.wait_ge(bb_done_p, 1)
                pool.wait_ge(cum_set, 5 * (d + 1))
                pool.tensor_tensor(sg, cum[:, :], sg, ALU.subtract).then_inc(sx_set, 1)
                pool.wait_ge(sx_set, d + 1)
                pool.wait_ge(eneg_set, d + 1)
                pool.wait_ge(loaded, 32)
                pool.tensor_tensor(c.ar[64:128, d, :, 1, 1, :], per_chunk(rk[64:128, 0]), per_chunk(eneg[64:128, :]), ALU.mult).then_inc(r_done_p, 1)
                pool.wait_ge(r_done_p, d + 1)
                pool.wait_ge(ex_set, d + 1)
                if d == 0:
                    pool.wait_ge(neg_b, 1)
                pool.tensor_tensor(c.ar[64:128, d, :, 0, 1, :], per_chunk(kn[64:128, :]), per_chunk(sg[64:128]), ALU.mult).then_inc(a_done_p, 1)
                pool.wait_ge(a_done_p, d + 1)
                pool.wait_ge(b_set, 2 * d + 1)
                pool.tensor_copy(c.bb[64:128, d, :, 1, :], c.kb[64:128, d, :, 1, :]).then_inc(bb_done_p, 1)


def phase_d_scan(c, p):
    nc = c.nc
    np_, ns = PROMPT // RC, SAMPLE // RC
    steps = []
    for i in range(ns):
        steps.append((1, np_ + i, np_ + ns - 1 - i))
        if i < np_:
            steps.append((0, i, np_ - 1 - i))
    N = len(steps)
    ROUNDS = N // 2
    RING = 3
    before, last, seen, adds = [], {}, set(), []
    for i, (s, cf, cb) in enumerate(steps):
        before.append(last.get(s))
        last[s] = i
        adds.append(cf in seen)
        seen.update((cf, cb))
    LEVELS = 5

    def level_slot(l):
        return 0 if l == 0 else 1 + l % 2
    with ExitStack() as ctx:
        def sb(name, shape):
            return ctx.enter_context(nc.sbuf_tensor(f"q{p}_{name}", shape, F32))

        def pb(name, shape):
            return ctx.enter_context(nc.psum_tensor(f"q{p}_{name}", shape, F32))

        sem = semaphores(nc, ctx, f"q{p}_")
        gs = sb("gs", [P, RING, 2, 256])
        bd = sb("bd", [P, 3, 4, 2, P])
        st = sb("st", [P, 3, 4, 3, RC])
        tt = sb("tt", [P, 4, P])
        kbt = sb("kbt", [P, RING, 2, P])
        uv = sb("uv", [P, RING, 2, 2, RC])
        rs = sb("rs", [P, 2, RC])
        grown = c.s_out[:, p]
        p_g, p_w, p_t = pb("pg", [P, 2, 256]), pb("pw", [P, 2, 2, P]), pb("pt", [P, 2, 2, P])
        p_a, p_nx, p_ru = pb("pa", [P, 512]), pb("pnx", [P, 4, 2, RC]), pb("pru", [P, 512])
        p_y, p_ds = pb("py", [P, 512]), pb("pds", [P, 512])
        p_a = p_a[:, 0:256].rearrange("p (q s) -> p q s", q=4)
        p_y, p_ds = (t[:, 0:128].rearrange("p (u s) -> p u s", u=2) for t in (p_y, p_ds))
        p_r = p_ru[:, 0:128].rearrange("p (u v) -> p u v", u=2)
        p_u = p_ru[:, 256:512].rearrange("p (u e v) -> p u e v", u=2, e=2)
        g_ready, w_ready, t_ready, sq_ready, x_ready, r_ready, u_ready, s_ready, y_ready = (
            sem(n + "_ready") for n in ("g", "w", "t", "sq", "x", "r", "u", "s", "y"))
        g_set, w_set, st0_set, x0_set, grow_set, grow_part, a_set, n_set = (
            sem(n) for n in ("g_set", "w_set", "st0_set", "x0_set", "grow_set", "grow_part", "a_set", "n_set"))
        t_set, r_set, u_set, state_set, y_set, own_dve, zeroed = (
            sem(n) for n in ("t_set", "r_set", "u_set", "state_set", "y_set", "own_dve", "zeroed"))
        block = ctx.enter_context(nc.Block())

        @block.tensor
        def _(pe):
            def masked_products(i):
                s, *ch = steps[i]
                if i >= 1:
                    pe.wait_ge(g_set, i)
                for u in range(2):
                    mm = pe.matmul(p_g[:, u], c.kb[:, u, ch[u]], c.ar[:, u, ch[u]], start=True, stop=True)
                mm.then_inc(g_ready, 1)

            def system(i):
                s, *ch = steps[i]
                if i >= 1:
                    pe.wait_ge(w_set, i)
                for u in range(2):
                    a, b = c.ar[:, u, ch[u], 0], c.bb[:, u, ch[u]]
                    pe.matmul(p_w[:, u, 0], a, b, start=True, stop=True)
                    mm = pe.matmul(p_w[:, u, 1], b, a, start=True, stop=True)
                mm.then_inc(w_ready, 1)

            def turn(i):
                s, *ch = steps[i]
                if i >= 1:
                    pe.wait_ge(t_set, 2 * i)
                for u in range(2):
                    pe.transpose(p_t[:, u, 0], c.kb[:, u, ch[u]], c.ident[:, :])
                    mm = pe.transpose(p_t[0:RC, u, 1], c.v[:, ch[u] * RC:(ch[u] + 1) * RC], c.ident[:, :])
                mm.then_inc(t_ready, 1)

            def square(j, l):
                if l == 1:
                    pe.wait_ge(st0_set, 4 * (j + 1))
                    if j >= 1:
                        pe.wait_ge(a_set, 3 * LEVELS * j)
                        pe.wait_ge(grow_set, LEVELS * j)
                else:
                    pe.wait_ge(a_set, 3 * (LEVELS * j + l - 1))
                    pe.wait_ge(n_set, 3 * ((LEVELS - 1) * j + l - 1))
                    if l == 2:
                        pe.wait_ge(x0_set, j + 1)
                    else:
                        pe.wait_ge(grow_set, LEVELS * j + l - 2)
                src = level_slot(l - 1)
                part = slice(1 if l == LEVELS else 0, 1 if l == 1 else 2)
                for q in range(4):
                    pe.matmul(p_a[:, q], bd[:, src, q, 1], st[:, src, q, 0], start=True, stop=True)
                    mm = pe.matmul(p_nx[:, q, part], bd[:, src, q, 0], st[:, src, q, part.start + 1:part.stop + 1], start=True, stop=True)
                mm.then_inc(sq_ready, 1)

            def last_product(j):
                pe.wait_ge(a_set, 3 * LEVELS * (j + 1))
                pe.wait_ge(grow_set, LEVELS * j + LEVELS - 1)
                src = level_slot(LEVELS)
                for q in range(4):
                    mm = pe.matmul(p_nx[:, q, 1], bd[:, src, q, 0], st[:, src, q, 2], start=True, stop=True)
                mm.then_inc(x_ready, 1)

            def right_side(i):
                s, *ch = steps[i]
                pe.wait_ge(g_set, i + 1)
                pe.wait_ge(t_set, 2 * (i + 1))
                if i >= 1:
                    pe.wait_ge(u_set, i)
                if before[i] is not None:
                    pe.wait_ge(state_set, before[i] + 1)
                for u in range(2):
                    for e in range(2):
                        pe.matmul(p_r[64 * e:64 * e + 64, u], gs[0:RC, i % RING, u, 64 * e:64 * e + 64], uv[0:RC, i % RING, u, e],
                                  start=True, stop=False, skip_group_check=True)
                    mm = pe.matmul(p_r[:, u], c.ar[:, u, ch[u], 0], c.s[:, s, u], start=False, stop=True, skip_group_check=True)
                mm.then_inc(r_ready, 1)

            def corrections(i):
                pe.wait_ge(r_set, i + 1)
                pe.wait_ge(grow_set, LEVELS * (i // 2 + 1))
                for u in range(2):
                    for e in range(2):
                        mm = pe.matmul(p_u[64:128, u, e], tt[:, 2 * (i % 2) + u, 64 * e:64 * e + 64], rs[:, u], start=True, stop=True)
                mm.then_inc(u_ready, 1)

            def outputs(i):
                s, *ch = steps[i]
                pe.wait_ge(u_set, i + 1)
                if i >= 1:
                    pe.wait_ge(state_set, i)
                for u in range(2):
                    for e in range(2):
                        mm = pe.matmul(p_ds[64 * e:64 * e + 64, u], kbt[:, i % RING, u, 64 * e:64 * e + 64], uv[:, i % RING, u, e],
                                       start=True, stop=True)
                mm.then_inc(s_ready, 1)
                if i >= 1:
                    pe.wait_ge(y_set, i)
                for u in range(2):
                    for e in range(2):
                        out = p_y[64 * e:64 * e + 64, u]
                        pe.matmul(out, uv[:, i % RING, u, e], gs[:, i % RING, u, 128 + 64 * e:128 + 64 * e + 64], start=True, stop=False)
                        mm = pe.matmul(out, c.s[:, s, u], c.ar[:, u, ch[u], 1, e, :], start=False, stop=True)
                mm.then_inc(y_ready, 1)
            pe.wait_ge(zeroed, 6)
            system(0)
            system(1)
            for j in range(ROUNDS + 1):
                now, ahead, back = j < ROUNDS, j + 1 < ROUNDS, j >= 1
                if now:
                    square(j, 1)
                if back:
                    right_side(2 * j - 2)
                if now:
                    masked_products(2 * j)
                    square(j, 2)
                if back:
                    corrections(2 * j - 2)
                if now:
                    turn(2 * j)
                    square(j, 3)
                if back:
                    outputs(2 * j - 2)
                if ahead:
                    system(2 * j + 2)
                if now:
                    square(j, 4)
                if back:
                    right_side(2 * j - 1)
                if ahead:
                    system(2 * j + 3)
                if now:
                    square(j, 5)
                if back:
                    corrections(2 * j - 1)
                if now:
                    masked_products(2 * j + 1)
                    turn(2 * j + 1)
                    last_product(j)
                if back:
                    outputs(2 * j - 1)

        @block.vector
        def _(dve):
            own = Own(dve, own_dve)
            for t in (bd[:, 1:3], tt[:, :, :], c.s[:, 0], uv[:, :, :, :, :]):
                dve.memset(t, 0.0).then_inc(zeroed, 1)
            dve.tensor_copy(c.s[:, 1], c.s_in[:, p]).then_inc(zeroed, 1)
            dve.sem_inc(zeroed, 1)

            def masks(i):
                dve.wait_ge(w_ready, i + 1)
                dve.tensor_tensor(bd[:, 0, 2 * (i % 2):2 * (i % 2) + 2], p_w[:, :, :, :], c.mask_na[:, :, :, :], ALU.mult).then_inc(w_set, 1)

            def product_masks(i):
                dve.wait_ge(g_ready, i + 1)
                dve.tensor_tensor(gs[:, i % RING].rearrange("p u (x e t) -> p (u x) e t", x=2, e=2),
                                  p_g[:, :, :].rearrange("p u (x e t) -> p (u x) e t", x=2, e=2),
                                  c.mask_g[:, :, :].rearrange("p u (x t) -> p (u x) t", x=2).unsqueeze(2).to_broadcast([P, 4, 2, RC]),
                                  ALU.mult).then_inc(g_set, 1)

            def level(j, l):
                dve.wait_ge(sq_ready, LEVELS * j + l)
                for e in range(2):
                    half = slice(64 * e, 64 * e + 64)
                    dve.tensor_copy(bd[half, level_slot(l), :, 1, half], p_nx[half, :, 0]).then_inc(n_set, 1)
                dve.tensor_copy(st[:, level_slot(l), :, 1], p_nx[:, :, 0]).then_inc(n_set, 1)

            def grow(j, k):
                dve.wait_ge(sq_ready, LEVELS * j + k + 1)
                dve.tensor_tensor(st[:, level_slot(k + 1), :, 2], st[:, level_slot(k), :, 2], p_nx[:, :, 1], ALU.add).then_inc(grow_set, 1)
                dve.wait_ge(grow_set, LEVELS * j + k)

            def grow_last(j):
                dve.wait_ge(x_ready, j + 1)
                if j >= 1:
                    dve.wait_ge(u_ready, 2 * j)
                for e in range(2):
                    half = slice(64 * e, 64 * e + 64)
                    cp = dve.tensor_tensor(tt[half, :, half], st[half, level_slot(LEVELS), :, 2], p_nx[half, :, 1], ALU.add)
                    cp.then_inc(grow_set if e else grow_part, 1)

            def carry(i):
                s, cf, cb = steps[i]
                dve.wait_ge(s_ready, i + 1)
                own.did(dve.tensor_tensor(grown, p_ds, c.s[:, s], ALU.add))
                own.settle()
                dve.wait_ge(y_ready, i + 1)
                dve.tensor_tensor(c.s[:, s], grown, c.pend[:, cf, :].unsqueeze(2).to_broadcast([P, 2, RC]), ALU.mult).then_inc(state_set, 1)
                chunks_ = c.xa[:, p, 0:NT].rearrange("p (n t) -> p n t", t=RC)
                end = cb + (1 if cb > cf else -1)
                dst = chunks_[:, cf:(None if end < 0 else end):cb - cf]
                if adds[i]:
                    dve.tensor_tensor(dst, dst, p_y, ALU.add).then_inc(y_set, 1)
                else:
                    dve.tensor_copy(dst, p_y).then_inc(y_set, 1)
                dve.wait_ge(state_set, i + 1)
            masks(0)
            masks(1)
            for j in range(ROUNDS + 1):
                now, ahead, back = j < ROUNDS, j + 1 < ROUNDS, j >= 1
                if now:
                    dve.wait_ge(st0_set, 4 * (j + 1))
                    if j >= 1:
                        dve.wait_ge(grow_set, LEVELS * j)
                    dve.tensor_tensor(st[:, level_slot(1), :, 2], st[:, 0, :, 1], c.istack[:, :].unsqueeze(1).to_broadcast([P, 4, RC]), ALU.add).then_inc(x0_set, 1)
                    level(j, 1)
                    product_masks(2 * j)
                    dve.wait_ge(x0_set, j + 1)
                    level(j, 2)
                    grow(j, 1)
                    level(j, 3)
                    grow(j, 2)
                if back:
                    carry(2 * j - 2)
                if ahead:
                    masks(2 * j + 2)
                if now:
                    level(j, 4)
                    grow(j, 3)
                if ahead:
                    masks(2 * j + 3)
                if now:
                    grow(j, 4)
                    product_masks(2 * j + 1)
                    grow_last(j)
                if back:
                    carry(2 * j - 1)
            dve.tensor_copy(c.s_out[:, p], c.s[:, 0]).then_inc(zeroed, 1)

        @block.scalar
        def _(act):
            def level(j, l):
                act.wait_ge(sq_ready, LEVELS * j + l)
                if l == 1 and j >= 1:
                    act.wait_ge(x_ready, j)
                for e in range(2):
                    half = slice(64 * e, 64 * e + 64)
                    act.activation(bd[half, level_slot(l), :, 0, half], p_a[half], ACT.Copy).then_inc(a_set, 1)
                act.activation(st[:, level_slot(l), :, 0], p_a, ACT.Copy).then_inc(a_set, 1)

            def turned(i):
                act.wait_ge(t_ready, i + 1)
                if i >= RING:
                    act.wait_ge(s_ready, i - RING + 1)
                    act.wait_ge(y_set, i - RING + 1)
                act.activation(kbt[:, i % RING], p_t[:, :, 0], ACT.Copy).then_inc(t_set, 1)
                act.activation(uv[0:RC, i % RING].rearrange("p u e v -> p u (e v)"), p_t[0:RC, :, 1], ACT.Copy).then_inc(t_set, 1)

            def right(i):
                act.wait_ge(r_ready, i + 1)
                act.activation(rs[:, :, :], p_r, ACT.Copy).then_inc(r_set, 1)

            def corrected(i):
                act.wait_ge(u_ready, i + 1)
                act.activation(uv[64:128, i % RING], p_u[64:128], ACT.Copy).then_inc(u_set, 1)
            act.wait_ge(zeroed, 6)
            for j in range(ROUNDS + 1):
                now, back = j < ROUNDS, j >= 1
                if now:
                    level(j, 1)
                if back:
                    right(2 * j - 2)
                if now:
                    level(j, 2)
                if back:
                    corrected(2 * j - 2)
                if now:
                    turned(2 * j)
                    level(j, 3)
                    level(j, 4)
                if back:
                    right(2 * j - 1)
                if now:
                    level(j, 5)
                if back:
                    corrected(2 * j - 1)
                if now:
                    turned(2 * j + 1)

        @block.gpsimd
        def _(pool):
            for i in range(N):
                pool.wait_ge(w_set, i + 1)
                if i >= 2:
                    pool.wait_ge(x0_set, i // 2)
                    pool.wait_ge(sq_ready, LEVELS * (i // 2 - 1) + 1)
                for e in range(2):
                    half = slice(64 * e, 64 * e + 64)
                    pool.tensor_copy(st[half, 0, 2 * (i % 2):2 * (i % 2) + 2, 0:2], bd[half, 0, 2 * (i % 2):2 * (i % 2) + 2, :, half]).then_inc(st0_set, 1)
                    pool.wait_ge(st0_set, 2 * i + e + 1)


def phase_d_norm(c):
    nc, io = c.nc, c.io
    with ExitStack() as ctx:
        def sb(name, shape):
            return ctx.enter_context(nc.sbuf_tensor(name, shape, F32))

        sem = semaphores(nc, ctx)
        hid_g = sb("m_hid_g", [P, NT])
        w_g = sb("m_w_g", [P, 4 * P])
        sq, std, g = (sb(f"m_{n}", [P, 2, 512]) for n in ("sq", "std", "g"))
        eps = sb("m_eps", [P, 1])
        p_c, p_v, p_g = (ctx.enter_context(nc.psum_tensor(f"m_{n}", [P, 2, 512], F32)) for n in ("pc", "pv", "pg"))
        loaded, centered, squared, var_ready, std_set, dve_own, done, gate_ready = (sem(f"m_{n}") for n in (
            "loaded", "centered", "squared", "var_ready", "std_set", "dve_own", "done", "gate_ready"))
        stored = sem("m_stored")
        block = ctx.enter_context(nc.Block())
        items = [(p, first, width) for p in range(HEADS_P) for first, width in BLOCKS]

        @block.sync
        def _(sp):
            sp.dma_start(hid_g[:, :], c.hid_g).then_inc(loaded, 16)
            sp.dma_start(w_g[:, :], io["w_g2"]).then_inc(loaded, 16)
            sp.dma_start(io["new_s"], c.s_out[:, :, :, :]).then_inc(stored, 16)
            sp.wait_ge(stored, 16)

        @block.tensor
        def _(pe):
            def center(n):
                p, first, width = items[n]
                if n >= 2:
                    pe.wait_ge(done, n - 1)
                pe.matmul(p_c[:, n % 2, 0:width], c.center64[:, :], c.xa[:, p, first:first + width], start=True, stop=True).then_inc(centered, 1)
                pe.matmul(p_g[:, n % 2, 0:width], w_g[:, p * P:(p + 1) * P], hid_g[:, first:first + width], start=True, stop=True).then_inc(gate_ready, 1)
            pe.wait_ge(loaded, 32)
            center(0)
            for n, (p, first, width) in enumerate(items):
                if n + 1 < len(items):
                    center(n + 1)
                pe.wait_ge(squared, n + 1)
                if n >= 2:
                    pe.wait_ge(std_set, n - 1)
                pe.matmul(p_v[:, n % 2, 0:width], c.mean64[:, :], sq[:, n % 2, 0:width], start=True, stop=True).then_inc(var_ready, 1)

        @block.scalar
        def _(act):
            act.wait_ge(dve_own, 1)
            for n, (p, first, width) in enumerate(items):
                act.wait_ge(centered, n + 1)
                act.activation(sq[:, n % 2, 0:width], p_c[:, n % 2, 0:width], ACT.Square).then_inc(squared, 1)
                act.wait_ge(var_ready, n + 1)
                if n >= 2:
                    act.wait_ge(done, n - 1)
                act.activation(std[:, n % 2, 0:width], p_v[:, n % 2, 0:width], ACT.Sqrt, bias=eps[:, 0:1]).then_inc(std_set, 1)

        @block.vector
        def _(dve):
            own = Own(dve, dve_own)
            own.did(dve.memset(eps[:, :], 64e-5))
            for n, (p, first, width) in enumerate(items):
                y = c.y[:, p, first:first + width]
                r, t = std[:, n % 2, 0:width], g[:, n % 2, 0:width]
                dve.wait_ge(std_set, n + 1)
                own.did(dve.reciprocal(r, r))
                own.settle()
                own.did(dve.tensor_tensor(t, r, p_c[:, n % 2, 0:width], ALU.mult))
                own.settle()
                own.did(dve.scalar_tensor_tensor(t, t, c.vec[:, VEC["rwkv_ln_g"] + p:VEC["rwkv_ln_g"] + p + 1], y, ALU.mult, ALU.add))
                own.settle()
                dve.wait_ge(gate_ready, n + 1)
                dve.scalar_tensor_tensor(y, t, c.vec[:, VEC["rwkv_ln_b"] + p:VEC["rwkv_ln_b"] + p + 1], p_g[:, n % 2, 0:width],
                                         ALU.add, ALU.mult).then_inc(done, 1)
                dve.wait_ge(done, n + 1)


def phase_d_constants(c):
    nc = c.nc
    with ExitStack() as ctx:
        sem = semaphores(nc, ctx, "k_")
        zero, made, sel, own_dve = (sem(n) for n in ("zero", "made", "sel", "own_dve"))
        block = ctx.enter_context(nc.Block())

        @block.vector
        def _(dve):
            own = Own(dve, own_dve)
            own.did(dve.memset(c.ar[:, :, :, :, :, :], 0.0))
            own.did(dve.memset(c.bb[:, :, :, :, :], 0.0))
            own.did(dve.memset(c.keep[:, :], 1.0))
            own.did(dve.memset(c.blockones[:, :], 0.0))
            own.settle()
            own.did(dve.memset(c.keep[:, :].rearrange("p (n t) -> p n t", t=RC)[:, :, 0:1], 0.0))
            for e in range(2):
                half = slice(64 * e, 64 * e + 64)
                own.did(dve.memset(c.blockones[half, half], 1.0))
                own.did(dve.tensor_copy(c.istack[half, :], c.ident[half, half]))
            ka = VEC["rwkv_k_a"]
            own.did(dve.tensor_scalar(c.one_less_ka[:, :], c.vec[:, ka:ka + 4], -1.0, 1.0, ALU.mult, ALU.add))
            own.settle()
            own.did(dve.tensor_scalar(c.mean64[:, :], c.blockones[:, :], 1.0 / 64, None, ALU.mult))
            own.settle()
            own.did(dve.tensor_tensor(c.center64[:, :], c.ident[:, :], c.mean64[:, :], ALU.subtract))
            own.settle()

        @block.gpsimd
        def _(pool):
            pool.memset(c.mask_na[:, :, :, :], 1.0).then_inc(zero, 1)
            pool.memset(c.mask_g[:, :, :], 1.0).then_inc(zero, 1)
            pool.wait_ge(zero, 2)
            n = 0
            for u in range(2):
                sgn = 1 - 2 * u
                for x in range(2):
                    rows_after = sgn * (1 - 2 * x)
                    for e in range(2):
                        v = c.mask_na[:, u, x, 64 * e:64 * e + 64]
                        pool.affine_select(out=v, in_=v, compare_op=ALU.is_gt, fill=0.0, base=-64 * e * rows_after,
                                           pattern=[[-rows_after, 64]], channel_multiplier=rows_after).then_inc(made, 1)
                        n += 1
                        pool.wait_ge(made, n)
                for half in range(2):
                    for x, cmp in ((0, ALU.is_gt), (1, ALU.is_ge)):
                        v = c.mask_g[64 * half:64 * half + 64, u, 64 * x:64 * x + 64]
                        pool.affine_select(out=v, in_=v, compare_op=cmp, fill=0.0, base=0, pattern=[[sgn, 64]],
                                           channel_multiplier=-sgn).then_inc(made, 1)
                        n += 1
                        pool.wait_ge(made, n)
            for e in range(2):
                v = c.mask_na[64 * e:64 * e + 64, :, :, 64 * (1 - e):64 * (1 - e) + 64]
                pool.memset(v, 0.0).then_inc(sel, 1)
                pool.wait_ge(sel, e + 1)


def phase_d(c):
    nc = c.nc
    with ExitStack() as ctx:
        def sb(name, shape):
            return ctx.enter_context(nc.sbuf_tensor(name, shape, F32))
        c.hid = sb("d_hid", [P, 2, NT])
        c.w2 = sb("d_w2", [P, 2, 4 * P])
        c.s_in, c.s_out = sb("d_s_in", [P, HEADS_P, 2, RC]), sb("d_s_out", [P, HEADS_P, 2, RC])
        c.keep, c.pend = sb("d_keep", [P, 256]), sb("d_pend", [P, RCH, 2])
        c.blockones, c.mean64, c.center64 = sb("d_blockones", [P, P]), sb("d_mean64", [P, P]), sb("d_center64", [P, P])
        c.istack, c.one_less_ka = sb("d_istack", [P, RC]), sb("d_one_less_ka", [P, 4])
        c.mask_na, c.mask_g = sb("d_mask_na", [P, 2, 2, P]), sb("d_mask_g", [P, 2, P])
        c.s = sb("d_s", [P, 2, 2, RC])
        phase_d_project(c)
        with ExitStack() as inner:
            def sb(name, shape):
                return inner.enter_context(nc.sbuf_tensor(name, shape, F32))
            c.ar = sb("d_ar", [P, 2, RCH, 2, 2, RC])
            c.kb = sb("d_kb", [P, 2, RCH, 2, RC])
            c.bb = sb("d_bb", [P, 2, RCH, 2, RC])
            c.v = sb("d_v", [P, NT])
            phase_d_constants(c)
            for p in range(HEADS_P):
                phase_d_prepare(c, p)
                phase_d_scan(c, p)
        phase_d_norm(c)


NEXP, GROUPS, PER_GROUP = 16, 4, 4
DEXP = 256
SLOT_TILES = (2 * NT + NEXP * (P - 1)) // P
REPS = [("gate1", 16), ("shift2", 24), ("gain2", None), ("gate2", 40)]


def phase_e_merge(c, merged):
    nc, io = c.nc, c.io
    with ExitStack() as ctx:
        def sb(name, shape):
            return ctx.enter_context(nc.sbuf_tensor(name, shape, F32))
        sem = semaphores(nc, ctx, "e_")
        wp = sb("e_wp", [P, 2, 4, D])
        sig = sb("e_sig", [P, 2, 2, 512])
        tmp = sb("e_tmp", [P, 2, 512])
        diag = sb("e_diag", [P, 2, 4, P])
        pp = ctx.enter_context(nc.psum_tensor("e_pp", [P, 2, 2, 512], F32))
        pr = ctx.enter_context(nc.psum_tensor("e_pr", [P, 2, 512], F32))
        w_in, sig_in, diag_set, rep_ready, rep_set = (sem(n) for n in ("w_in", "sig_in", "diag_set", "rep_ready", "rep_set"))
        sig_slot = [sem("sig_in0"), sem("sig_in1")]
        ready, scaled_a, scaled_b, added = (sem(n) for n in ("ready", "scaled_a", "scaled_b", "added"))
        items = [(f, m) for f in range(KD) for m in range(3)]
        reps = [(r, s, half) for r in range(4) for s in range(2) for half in range(2)]
        block = ctx.enter_context(nc.Block())

        @block.sync
        def _(sp):
            for x in range(2):
                sp.dma_start(wp[:, x], io["w_branch"][x]).then_inc(w_in, 16)
            for n, (f, m) in enumerate(items):
                first, width = BLOCKS[m]
                if n >= 2:
                    sp.wait_ge(scaled_b, n - 1)
                for x in range(2):
                    sp.dma_start(sig[:, n % 2, x, 0:width], c.sig[4 + 8 * x + f, :, first:first + width]).then_inc(sig_slot[n % 2], 16)

        @block.tensor
        def _(pe):
            for n in range(len(reps)):
                pe.wait_ge(diag_set, n + 1)
                if n >= 2:
                    pe.wait_ge(rep_set, n - 1)
                pe.matmul(pr[:, n % 2], c.ones[:, :], diag[:, n % 2], start=True, stop=True).then_inc(rep_ready, 1)
            pe.wait_ge(w_in, 32)
            for n, (f, m) in enumerate(items):
                first, width = BLOCKS[m]
                if n >= 2:
                    pe.wait_ge(scaled_b, n - 1)
                for x in range(2):
                    for k in range(4):
                        mm = pe.matmul(pp[:, n % 2, x, 0:width], wp[:, x, k, f * P:(f + 1) * P], c.y[:, 4 * x + k, first:first + width],
                                       start=(k == 0), stop=(k == 3))
                mm.then_inc(ready, 1)

        @block.vector
        def _(dve):
            for n, (r, s, half) in enumerate(reps):
                at = REPS[r][1]
                src = c.gain[:, 1, 4 * half:4 * half + 4, s] if at is None else c.mod[:, at + 4 * half:at + 4 * half + 4, s]
                if n >= 2:
                    dve.wait_ge(rep_ready, n - 1)
                dve.tensor_tensor(diag[:, n % 2], c.ident[:, :].unsqueeze(1).to_broadcast([P, 4, P]),
                                  src.unsqueeze(2).to_broadcast([P, 4, P]), ALU.mult).then_inc(diag_set, 1)
            for n, (f, m) in enumerate(items):
                first, width = BLOCKS[m]
                out = merged[:, f, first:first + width]
                dve.wait_ge(ready, n + 1)
                dve.wait_ge(sig_slot[n % 2], 32 * (n // 2 + 1))
                if n >= 2:
                    dve.wait_ge(added, n - 1)
                dve.tensor_tensor(tmp[:, n % 2, 0:width], sig[:, n % 2, 0, 0:width], pp[:, n % 2, 0, 0:width], ALU.mult).then_inc(scaled_a, 1)
                dve.wait_ge(scaled_a, n + 1)
                dve.tensor_tensor(out, sig[:, n % 2, 1, 0:width], pp[:, n % 2, 1, 0:width], ALU.mult).then_inc(scaled_b, 1)

        @block.gpsimd
        def _(pool):
            for n, (f, m) in enumerate(items):
                first, width = BLOCKS[m]
                out = merged[:, f, first:first + width]
                pool.wait_ge(scaled_b, n + 1)
                pool.tensor_tensor(out, out, tmp[:, n % 2, 0:width], ALU.add).then_inc(added, 1)
                pool.wait_ge(added, n + 1)

        @block.scalar
        def _(act):
            for n, (r, s, half) in enumerate(reps):
                dst = c.gate2 if r == 3 else c.rep[:, r]
                act.wait_ge(rep_ready, n + 1)
                act.activation(dst[:, s, 512 * half:512 * half + 512], pr[:, n % 2], ACT.Copy).then_inc(rep_set, 1)


def phase_e_rows(c, merged):
    nc, io = c.nc, c.io
    with ExitStack() as ctx:
        def sb(name, shape):
            return ctx.enter_context(nc.sbuf_tensor(name, shape, F32))
        sem = semaphores(nc, ctx, "o_")
        wo = sb("o_wo", [P, KD, D])
        wr = sb("o_wr", [P, KD, 20])
        br = sb("o_br", [P, 20])
        x = sb("o_x", [P, 2, D])
        h2 = sb("o_h2", [P, 2, D])
        ht = sb("o_ht", [P, 2, KD, P])
        stat = sb("o_stat", [P, 4, TILES])
        po = ctx.enter_context(nc.psum_tensor("o_po", [P, 2, 512], F32))
        pt = ctx.enter_context(nc.psum_tensor("o_pt", [P, 2, 4, P], F32))
        pl = ctx.enter_context(nc.psum_tensor("o_pl", [P, 2, 512], F32))
        w_in, projected, scaled, x2_set, squared, var_set, std_set, own_dve, h2_set = (sem(n) for n in (
            "w_in", "projected", "scaled", "x2_set", "squared", "var_set", "std_set", "own_dve", "h2_set"))
        x_in, h2_stored = [sem("x_in0"), sem("x_in1")], [sem("h2_stored0"), sem("h2_stored1")]
        turned, ht_set, logit_ready, logit_set = (sem(n) for n in ("turned", "ht_set", "logit_ready", "logit_set"))
        block = ctx.enter_context(nc.Block())

        def store(sp, t):
            sp.wait_ge(h2_set, t + 1)
            sp.dma_start(c.h2[t * P:(t + 1) * P, :], h2[:, t % 2]).then_inc(h2_stored[t % 2], 16)

        def logit(dve, t):
            dve.wait_ge(logit_ready, t + 1)
            dve.tensor_tensor(c.logits[:, t], br[:, :], pl[:, t % 2, 0:20], ALU.add).then_inc(logit_set, 1)

        @block.sync
        def _(sp):
            sp.dma_start(wo[:, :, :], io["w_out"]).then_inc(w_in, 16)
            sp.dma_start(wr[:, :, :], io["w_router"]).then_inc(w_in, 16)
            sp.dma_start(br[:, :], io["b_router"].partition_broadcast(P)).then_inc(w_in, 16)
            for t in range(TILES):
                if t >= 2:
                    sp.wait_ge(x2_set, 2 * t - 2)
                sp.dma_start(x[:, t % 2], io["x"][t * P:(t + 1) * P, :]).then_inc(x_in[t % 2], 16)
                if t >= 1:
                    store(sp, t - 1)
            store(sp, TILES - 1)
            for i in range(2):
                sp.wait_ge(h2_stored[i], 16 * TILES // 2)

        @block.tensor
        def _(pe):
            def project(t):
                for half in range(2):
                    n = 2 * t + half
                    if n >= 2:
                        pe.wait_ge(scaled, n - 1)
                    for k in range(KD):
                        mm = pe.matmul(po[:, n % 2], merged[:, k, t * P:(t + 1) * P], wo[:, k, 512 * half:512 * half + 512],
                                       start=(k == 0), stop=(k == KD - 1))
                    mm.then_inc(projected, 1)

            def turn(t):
                pe.wait_ge(h2_set, t + 1)
                for half in range(2):
                    n = 2 * t + half
                    if n >= 2:
                        pe.wait_ge(ht_set, n - 1)
                    for j in range(4):
                        k = 4 * half + j
                        mm = pe.transpose(pt[:, half, j], h2[:, t % 2, k * P:(k + 1) * P], c.ident[:, :])
                    mm.then_inc(turned, 1)

            def logits(t):
                pe.wait_ge(ht_set, 2 * t + 2)
                if t >= 2:
                    pe.wait_ge(logit_set, t - 1)
                for k in range(KD):
                    mm = pe.matmul(pl[:, t % 2, 0:20], ht[:, t % 2, k], wr[:, k], start=(k == 0), stop=(k == KD - 1))
                mm.then_inc(logit_ready, 1)
            pe.wait_ge(w_in, 48)
            for t in range(TILES + 2):
                if t < TILES:
                    project(t)
                if 1 <= t < TILES + 1:
                    turn(t - 1)
                if t >= 2:
                    logits(t - 2)

        @block.vector
        def _(dve):
            own = Own(dve, own_dve)
            for t in range(TILES):
                s = 0 if t < PROMPT // P else 1
                x2 = c.x2[:, t]
                for half in range(2):
                    n = 2 * t + half
                    cols = slice(512 * half, 512 * half + 512)
                    dve.wait_ge(projected, n + 1)
                    dve.tensor_tensor(x2[:, cols], c.rep[:, 0, s, cols], po[:, n % 2], ALU.mult).then_inc(scaled, 1)
                dve.wait_ge(x_in[t % 2], 16 * (t // 2 + 1))
                for half in range(2):
                    cols = slice(512 * half, 512 * half + 512)
                    dve.wait_ge(scaled, 2 * t + half + 1)
                    dve.tensor_tensor(x2[:, cols], x2[:, cols], x[:, t % 2, cols], ALU.add).then_inc(x2_set, 1)
                dve.wait_ge(squared, t + 1)
                dve.tensor_scalar(stat[:, 1, t:t + 1], stat[:, 0, t:t + 1], 1.0 / D, NORM_EPS, ALU.mult, ALU.add).then_inc(var_set, 1)
                dve.wait_ge(std_set, t + 1)
                own.did(dve.reciprocal(stat[:, 3, t:t + 1], stat[:, 2, t:t + 1]))
                own.settle()
                if t >= 2:
                    dve.wait_ge(h2_stored[t % 2], 16 * (t // 2))
                    dve.wait_ge(turned, 2 * (t - 1))
                own.did(dve.scalar_tensor_tensor(h2[:, t % 2], x2, stat[:, 3, t:t + 1],
                                                 c.rep[:, 2, s], ALU.mult, ALU.mult))
                own.settle()
                dve.tensor_tensor(h2[:, t % 2], h2[:, t % 2], c.rep[:, 1, s], ALU.add).then_inc(h2_set, 1)
                if t >= 2:
                    logit(dve, t - 2)
            for t in range(TILES - 2, TILES):
                logit(dve, t)

        @block.scalar
        def _(act):
            def turn(t):
                for half in range(2):
                    act.wait_ge(turned, 2 * t + half + 1)
                    if t >= 2 and half == 0:
                        act.wait_ge(logit_ready, t - 1)
                    act.activation(ht[:, t % 2, 4 * half:4 * half + 4], pt[:, half], ACT.Copy).then_inc(ht_set, 1)
            for t in range(TILES):
                act.wait_ge(x2_set, 2 * t + 2)
                if t >= 1:
                    act.wait_ge(squared, t)
                act.activation(c.junk[:, :], c.x2[:, t], ACT.Square, accum_out=stat[:, 0, t:t + 1]).then_inc(squared, 1)
                act.wait_ge(var_set, t + 1)
                act.activation(stat[:, 2, t:t + 1], stat[:, 1, t:t + 1], ACT.Sqrt).then_inc(std_set, 1)
                if t >= 1:
                    turn(t - 1)
            turn(TILES - 1)


def phase_e_route(c):
    nc, io = c.nc, c.io
    I32 = mybir.dt.int32
    with ExitStack() as ctx:
        def sb(name, shape, dt=F32):
            return ctx.enter_context(nc.sbuf_tensor(name, shape, dt))
        sem = semaphores(nc, ctx, "r_")
        T = TILES
        prio, expert_prio = sb("r_prio", [P, 4]), None
        triu = sb("r_triu", [P, P])
        thr, tile_no, token = sb("r_thr", [P, 10]), sb("r_tile_no", [P, SLOT_TILES]), sb("r_token", [P, T])
        one16 = sb("r_one16", [P, NEXP])
        m, t4, oh, oh1, oh2, es = (sb(f"r_{n}", [P, T, 4]) for n in ("m", "t4", "oh", "oh1", "oh2", "es"))
        t16 = sb("r_t16", [P, T, 4, 4])
        gmax, gsum, m1, m2, den, s1 = (sb(f"r_{n}", [P, T]) for n in ("gmax", "gsum", "m1", "m2", "den", "s1"))
        pick = sb("r_pick", [P, 2, T, NEXP])
        both, pos, base = sb("r_both", [P, T, NEXP]), sb("r_pos", [P, T, NEXP]), sb("r_base", [P, T + 1, NEXP])
        cmp10, ntiles, ends, starts = sb("r_cmp10", [P, NEXP, 10]), sb("r_ntiles", [P, NEXP]), sb("r_ends", [P, NEXP]), sb("r_starts", [P, NEXP])
        cmp35, owner = sb("r_cmp35", [P, SLOT_TILES, NEXP]), sb("r_owner", [P, SLOT_TILES])
        slotf = sb("r_slotf", [P, 2, T])
        zrow = sb("r_zrow", [SLOT_TILES, P])
        listed = sb("r_listed", [SLOT_TILES, P])
        pc = ctx.enter_context(nc.psum_tensor("r_pc", [P, 2, 512], F32))
        pl = ctx.enter_context(nc.psum_tensor("r_pl", [P, 512], F32))
        own_dve, made, made2, exp_in, exp_set, both_set, counted, slot_set, owner_set = (sem(n) for n in (
            "own_dve", "made", "made2", "exp_in", "exp_set", "both_set", "counted", "slot_set", "owner_set"))
        zero_stored, scattered, list_in, list_turned, fg_in = (sem(n) for n in ("zero_stored", "scattered", "list_in", "list_turned", "fg_in"))
        block = ctx.enter_context(nc.Block())

        @block.gpsimd
        def _(pool):
            n = 0

            def step(ins):
                nonlocal n
                ins.then_inc(made, 1)
                n += 1
                pool.wait_ge(made, n)
            step(pool.memset(zrow[:, :], 0.0))
            pool.dma_start(c.slot_list.rearrange("(q p) o -> q (p o)", p=P), zrow[:, :]).then_inc(zero_stored, 16)
            step(pool.memset(triu[:, :], 1.0))
            step(pool.affine_select(out=triu[:, :], in_=triu[:, :], compare_op=ALU.is_gt, fill=0.0, base=0,
                                    pattern=[[1, P]], channel_multiplier=-1))
            step(pool.iota(prio[:, :], pattern=[[-1, 4]], base=4, channel_multiplier=0, allow_small_or_imprecise_dtypes=True))
            step(pool.iota(thr[:, :], pattern=[[P, 10]], base=0, channel_multiplier=0, allow_small_or_imprecise_dtypes=True))
            step(pool.iota(tile_no[:, :], pattern=[[1, SLOT_TILES]], base=0, channel_multiplier=0, allow_small_or_imprecise_dtypes=True))
            step(pool.iota(token[:, :], pattern=[[P, T]], base=0, channel_multiplier=1, allow_small_or_imprecise_dtypes=True))
            step(pool.memset(one16[:, :], 1.0))
            pool.sem_inc(made2, 1)
            pool.wait_ge(zero_stored, 16)
            pool.wait_ge(slot_set, 1)
            for k in range(2):
                for t in range(T):
                    pool.indirect_dma_start(c.slot_list, bass.IndirectOffsetOnAxis(ap=c.slot[:, k, t:t + 1], axis=0),
                                            token[:, t:t + 1], None).then_inc(scattered, 16)
            pool.wait_ge(scattered, 2 * T * 16)
            pool.dma_start(listed[:, :], c.slot_list.rearrange("(q p) o -> q (p o)", p=P)).then_inc(list_in, 16)

        @block.sync
        def _(sp):
            sp.dma_start(c.fgain[:, :], io["final_g"].partition_broadcast(P)).then_inc(fg_in, 16)
            sp.wait_ge(fg_in, 16)

        @block.vector
        def _(dve):
            own = Own(dve, own_dve)

            def do(ins):
                own.did(ins)
                own.settle()

            def bc(ap, n):
                return ap.unsqueeze(2).to_broadcast([P, T, n])

            def first_best(out, values, best):
                do(dve.tensor_tensor(out, values, bc(best, 4), ALU.is_equal))
                do(dve.tensor_tensor(out, out, prio[:, :].unsqueeze(1).to_broadcast([P, T, 4]), ALU.mult))
                do(dve.tensor_reduce(s1[:, :], out, AX.X, ALU.max))
                do(dve.tensor_tensor(out, out, bc(s1[:, :], 4), ALU.is_equal))
            g = c.logits[:, :, 0:4]
            e = c.logits[:, :, 4:20].rearrange("p t (g e) -> p t g e", g=4)
            dve.wait_ge(made2, 1)
            do(dve.tensor_reduce(gmax[:, :], g, AX.X, ALU.max))
            do(dve.tensor_tensor(t4[:, :, :], g, bc(gmax[:, :], 4), ALU.subtract))
            dve.sem_inc(exp_in, 1)
            first_best(oh[:, :, :], g, gmax[:, :])
            do(dve.tensor_tensor(t16[:, :, :, :], e, oh[:, :, :].unsqueeze(3).to_broadcast([P, T, 4, 4]), ALU.mult))
            do(dve.tensor_reduce(es[:, :, :], t16[:, :, :, :].rearrange("p t g e -> p t e g"), AX.X, ALU.add))
            do(dve.tensor_reduce(m1[:, :], es[:, :, :], AX.X, ALU.max))
            first_best(oh1[:, :, :], es[:, :, :], m1[:, :])
            do(dve.scalar_tensor_tensor(es[:, :, :], oh1[:, :, :], -3e38, es[:, :, :], ALU.mult, ALU.add))
            do(dve.tensor_reduce(m2[:, :], es[:, :, :], AX.X, ALU.max))
            first_best(oh2[:, :, :], es[:, :, :], m2[:, :])
            do(dve.tensor_tensor(m2[:, :], m2[:, :], m1[:, :], ALU.subtract))
            dve.sem_inc(exp_in, 1)
            for k, o in enumerate((oh1, oh2)):
                do(dve.tensor_tensor(pick[:, k].rearrange("p t (g e) -> p t g e", g=4), oh[:, :, :].unsqueeze(3).to_broadcast([P, T, 4, 4]),
                                     o[:, :, :].unsqueeze(2).to_broadcast([P, T, 4, 4]), ALU.mult))
            dve.tensor_tensor(both[:, :, :], pick[:, 0], pick[:, 1], ALU.add).then_inc(both_set, 1)
            dve.wait_ge(exp_set, 2)
            do(dve.tensor_reduce(gsum[:, :], t4[:, :, :], AX.X, ALU.add))
            do(dve.tensor_scalar(den[:, :], m2[:, :], 1.0, None, ALU.add))
            do(dve.tensor_tensor(den[:, :], den[:, :], gsum[:, :], ALU.mult))
            do(dve.reciprocal(c.cw[:, 0], den[:, :]))
            do(dve.tensor_tensor(c.cw[:, 1], c.cw[:, 0], m2[:, :], ALU.mult))
            dve.wait_ge(counted, 1)
            ranks = pc[:, 0, 0:T * NEXP].rearrange("p (t e) -> p t e", e=NEXP)
            sums = pc[:, 1, 0:T * NEXP].rearrange("p (t e) -> p t e", e=NEXP)
            do(dve.memset(base[:, 0], 0.0))
            for t in range(T):
                do(dve.tensor_tensor(base[:, t + 1], base[:, t], sums[:, t], ALU.add))
            do(dve.tensor_tensor(cmp10[:, :, :], base[:, T].unsqueeze(2).to_broadcast([P, NEXP, 10]),
                                 thr[:, :].unsqueeze(1).to_broadcast([P, NEXP, 10]), ALU.is_gt))
            do(dve.tensor_reduce(ntiles[:, :], cmp10[:, :, :], AX.X, ALU.add))
            do(dve.tensor_tensor_scan(ends[:, :], one16[:, :], ntiles[:, :], 0.0, ALU.mult, ALU.add))
            do(dve.tensor_tensor(starts[:, :], ends[:, :], ntiles[:, :], ALU.subtract))
            do(dve.tensor_scalar(starts[:, :], starts[:, :], float(P), None, ALU.mult))
            do(dve.tensor_tensor(pos[:, :, :], base[:, 0:T], ranks, ALU.add))
            do(dve.tensor_tensor(pos[:, :, :], pos[:, :, :], starts[:, :].unsqueeze(1).to_broadcast([P, T, NEXP]), ALU.add))
            for k in range(2):
                do(dve.tensor_tensor(both[:, :, :], pick[:, k], pos[:, :, :], ALU.mult))
                do(dve.tensor_reduce(slotf[:, k], both[:, :, :], AX.X, ALU.add))
            dve.tensor_copy(c.slot[:, :, :], slotf[:, :, :]).then_inc(slot_set, 1)
            do(dve.tensor_tensor(cmp35[:, :, :], tile_no[:, :].unsqueeze(2).to_broadcast([P, SLOT_TILES, NEXP]),
                                 ends[:, :].unsqueeze(1).to_broadcast([P, SLOT_TILES, NEXP]), ALU.is_ge))
            do(dve.tensor_reduce(owner[:, :], cmp35[:, :, :], AX.X, ALU.add))
            do(dve.tensor_scalar(owner[:, :], owner[:, :], float(NEXP - 1), None, ALU.min))
            do(dve.tensor_copy(c.owner[:, :], owner[0:1, :]))
            dve.wait_ge(list_turned, 1)
            do(dve.tensor_copy(c.rows_of[:, :], pl[:, 0:SLOT_TILES]))

        @block.scalar
        def _(act):
            act.wait_ge(exp_in, 1)
            act.activation(t4[:, :, :], t4[:, :, :], ACT.Exp).then_inc(exp_set, 1)
            act.wait_ge(exp_in, 2)
            act.activation(m2[:, :], m2[:, :], ACT.Exp).then_inc(exp_set, 1)

        @block.tensor
        def _(pe):
            pe.wait_ge(made2, 1)
            pe.wait_ge(both_set, 1)
            pe.matmul(pc[:, 0, 0:T * NEXP], triu[:, :], both[:, :, :].rearrange("p t e -> p (t e)"), start=True, stop=True)
            pe.matmul(pc[:, 1, 0:T * NEXP], c.ones[:, :], both[:, :, :].rearrange("p t e -> p (t e)"), start=True, stop=True).then_inc(counted, 1)
            pe.wait_ge(list_in, 16)
            pe.transpose(pl[:, 0:SLOT_TILES], listed[:, :], c.ident[0:SLOT_TILES, 0:SLOT_TILES]).then_inc(list_turned, 1)


def phase_f_experts(c):
    nc, io = c.nc, c.io
    RING = 2
    with ExitStack() as ctx:
        def sb(name, shape):
            return ctx.enter_context(nc.sbuf_tensor(name, shape, F32))
        sem = semaphores(nc, ctx, "f_")
        w13 = sb("f_w13", [P, RING, 2, KD, DEXP])
        w2 = sb("f_w2", [P, RING, 2, D])
        xg, xt, out = sb("f_xg", [P, RING, D]), sb("f_xt", [P, RING, KD, P]), sb("f_out", [P, RING, D])
        act_t = sb("f_act", [P, RING, 2, P])
        pt = ctx.enter_context(nc.psum_tensor("f_pt", [P, 2, 4, P], F32))
        pab = ctx.enter_context(nc.psum_tensor("f_pab", [P, RING, 2, 512], F32))
        po = ctx.enter_context(nc.psum_tensor("f_po", [P, 2, 512], F32))
        w13_in, w2_in, x_in = ([sem(f"{n}{i}") for i in range(RING)] for n in ("w13_in", "w2_in", "x_in"))
        turned, ab_ready, o_ready = ([sem(f"{n}{i}") for i in range(RING)] for n in ("turned", "ab_ready", "o_ready"))
        xt_set, silu_set, prod_set, out_act, out_dve, out_stored = ([sem(f"{n}{i}") for i in range(RING)] for n in (
            "xt_set", "silu_set", "prod_set", "out_act", "out_dve", "out_stored"))
        block = ctx.enter_context(nc.Block())
        pairs, odd = divmod(SLOT_TILES, RING)

        def turns(engine, body):
            for b in range(RING):
                body(0, b)
            with engine.Fori(1, pairs) as i:
                for b in range(RING):
                    body(i, b)
            for b in range(odd):
                body(pairs, b)

        @block.sync
        def _(sp):
            for q in range(SLOT_TILES):
                i, b = divmod(q, RING)
                e = sp.value_load(c.owner[0:1, q:q + 1], min_val=0, max_val=NEXP - 1)
                wait_reuse(sp, ab_ready[b], i)
                sp.dma_start(w13[:, b], io["w13"][bass.ds(e, 1)].rearrange("o p w k f -> p (o w) k f")).then_inc(w13_in[b], 16)
                wait_reuse(sp, o_ready[b], i)
                sp.dma_start(w2[:, b], io["w2"][bass.ds(e, 1)].rearrange("o p k n -> p (o k) n")).then_inc(w2_in[b], 16)

        @block.gpsimd
        def _(pool):
            for q in range(SLOT_TILES):
                i, b = divmod(q, RING)
                wait_reuse(pool, turned[b], 2 * i)
                pool.indirect_dma_start(xg[:, b], None, c.h2, bass.IndirectOffsetOnAxis(ap=c.rows_of[:, q:q + 1], axis=0)).then_inc(x_in[b], 16)

        @block.tensor
        def _(pe):
            def tile(i, b):
                pe.wait_ge(x_in[b], i * 16 + 16)
                for half in range(2):
                    if b == 0:
                        wait_reuse(pe, xt_set[1], i * 2)
                    else:
                        pe.wait_ge(xt_set[0], i * 2 + 2)
                    for j in range(4):
                        k = 4 * half + j
                        mm = pe.transpose(pt[:, half, j], xg[:, b, k * P:(k + 1) * P], c.ident[:, :])
                    mm.then_inc(turned[b], 1)
                pe.wait_ge(w13_in[b], i * 16 + 16)
                pe.wait_ge(xt_set[b], i * 2 + 2)
                wait_reuse(pe, prod_set[b], i)
                for w in range(2):
                    for f in range(2):
                        for k in range(KD):
                            mm = pe.matmul(pab[:, b, w, f * P:(f + 1) * P], w13[:, b, w, k, f * P:(f + 1) * P], xt[:, b, k],
                                           start=(k == 0), stop=(k == KD - 1))
                mm.then_inc(ab_ready[b], 1)
                pe.wait_ge(w2_in[b], i * 16 + 16)
                pe.wait_ge(prod_set[b], i + 1)
                if b == 0:
                    wait_reuse(pe, out_act[1], i)
                    wait_reuse(pe, out_dve[1], i)
                else:
                    pe.wait_ge(out_act[0], i + 1)
                    pe.wait_ge(out_dve[0], i + 1)
                for half in range(2):
                    for f in range(2):
                        mm = pe.matmul(po[:, half], act_t[:, b, f], w2[:, b, f, 512 * half:512 * half + 512], start=(f == 0), stop=(f == 1))
                mm.then_inc(o_ready[b], 1)
            turns(pe, tile)

        @block.scalar
        def _(act):
            def tile(i, b):
                for half in range(2):
                    act.wait_ge(turned[b], i * 2 + (half + 1))
                    if half == 0:
                        wait_reuse(act, ab_ready[b], i)
                    act.activation(xt[:, b, 4 * half:4 * half + 4], pt[:, half], ACT.Copy).then_inc(xt_set[b], 1)
                act.wait_ge(ab_ready[b], i + 1)
                wait_reuse(act, o_ready[b], i)
                act.activation(act_t[:, b].rearrange("p f t -> p (f t)"), pab[:, b, 0, 0:DEXP], ACT.Silu).then_inc(silu_set[b], 1)
                act.wait_ge(o_ready[b], i + 1)
                wait_reuse(act, out_stored[b], i * 16)
                act.activation(out[:, b, 0:512], po[:, 0], ACT.Copy).then_inc(out_act[b], 1)
                act.wait_ge(out_act[b], i + 1)
                act.wait_ge(out_dve[b], i + 1)
                act.dma_start(c.ys[bass.ds((i * RING + b) * P, P), :], out[:, b]).then_inc(out_stored[b], 16)
            turns(act, tile)
            for b in range(RING):
                act.wait_ge(out_stored[b], 16 * (pairs + (b < odd)))

        @block.vector
        def _(dve):
            def tile(i, b):
                dve.wait_ge(silu_set[b], i + 1)
                a = act_t[:, b].rearrange("p f t -> p (f t)")
                dve.tensor_tensor(a, a, pab[:, b, 1, 0:DEXP], ALU.mult).then_inc(prod_set[b], 1)
                dve.wait_ge(o_ready[b], i + 1)
                wait_reuse(dve, out_stored[b], i * 16)
                dve.tensor_copy(out[:, b, 512:D], po[:, 1]).then_inc(out_dve[b], 1)
            turns(dve, tile)


def phase_f_combine(c):
    nc, io = c.nc, c.io
    with ExitStack() as ctx:
        def sb(name, shape):
            return ctx.enter_context(nc.sbuf_tensor(name, shape, F32))
        sem = semaphores(nc, ctx, "g_")
        R = 3
        y = sb("g_y", [P, R, 2, D])
        stat = sb("g_stat", [P, 4, TILES])
        y_in, stored = [sem(f"y_in{i}") for i in range(R)], [sem(f"stored{i}") for i in range(R)]
        own_dve, x3_set, squared, var_set, std_set, normed, done = (sem(n) for n in (
            "own_dve", "x3_set", "squared", "var_set", "std_set", "normed", "done"))
        block = ctx.enter_context(nc.Block())

        @block.gpsimd
        def _(pool):
            for t in range(TILES):
                if t >= R:
                    pool.wait_ge(stored[t % R], 16 * (t // R))
                for k in range(2):
                    pool.indirect_dma_start(y[:, t % R, k], None, c.ys, bass.IndirectOffsetOnAxis(ap=c.slot[:, k, t:t + 1], axis=0)).then_inc(y_in[t % R], 16)

        @block.vector
        def _(dve):
            own = Own(dve, own_dve)

            def combine(t):
                s = 0 if t < PROMPT // P else 1
                a, b = y[:, t % R, 0], y[:, t % R, 1]
                dve.wait_ge(y_in[t % R], 32 * (t // R + 1))
                own.did(dve.tensor_scalar(a, a, c.cw[:, 0, t:t + 1], None, ALU.mult))
                own.settle()
                own.did(dve.scalar_tensor_tensor(b, b, c.cw[:, 1, t:t + 1], a, ALU.mult, ALU.add))
                own.settle()
                own.did(dve.tensor_tensor(b, b, c.gate2[:, s], ALU.mult))
                own.settle()
                dve.tensor_tensor(c.x2[:, t], c.x2[:, t], b, ALU.add).then_inc(x3_set, 1)

            def finish(t):
                dve.wait_ge(squared, t + 1)
                dve.tensor_scalar(stat[:, 1, t:t + 1], stat[:, 0, t:t + 1], 1.0 / D, NORM_EPS, ALU.mult, ALU.add).then_inc(var_set, 1)
                dve.wait_ge(std_set, t + 1)
                own.did(dve.reciprocal(stat[:, 3, t:t + 1], stat[:, 2, t:t + 1]))
                own.settle()
                dve.scalar_tensor_tensor(y[:, t % R, 0], c.x2[:, t], stat[:, 3, t:t + 1], c.fgain[:, :], ALU.mult, ALU.mult).then_inc(done, 1)
            for t in range(TILES + 1):
                if t < TILES:
                    combine(t)
                if t >= 1:
                    finish(t - 1)

        @block.scalar
        def _(act):
            for t in range(TILES):
                act.wait_ge(x3_set, t + 1)
                if t >= 1:
                    act.wait_ge(squared, t)
                act.activation(c.junk[:, :], c.x2[:, t], ACT.Square, accum_out=stat[:, 0, t:t + 1]).then_inc(squared, 1)
                act.wait_ge(var_set, t + 1)
                act.activation(stat[:, 2, t:t + 1], stat[:, 1, t:t + 1], ACT.Sqrt).then_inc(std_set, 1)

        @block.sync
        def _(sp):
            for t in range(TILES):
                sp.wait_ge(done, t + 1)
                sp.dma_start(io["y_out"][t * P:(t + 1) * P, :], y[:, t % R, 0]).then_inc(stored[t % R], 16)
            for i in range(R):
                sp.wait_ge(stored[i], 16 * len(range(i, TILES, R)))


def phases_e_f(c):
    nc = c.nc
    I32 = mybir.dt.int32
    with ExitStack() as ctx:
        def sb(name, shape, dt=F32):
            return ctx.enter_context(nc.sbuf_tensor(name, shape, dt))
        c.gate2, c.junk = sb("f_gate2", [P, 2, D]), sb("f_junk", [P, D])
        c.logits, c.cw = sb("f_logits", [P, TILES, 20]), sb("f_cw", [P, 2, TILES])
        c.slot, c.rows_of, c.owner = sb("f_slot", [P, 2, TILES], I32), sb("f_rows_of", [P, SLOT_TILES], I32), sb("f_owner", [1, SLOT_TILES], I32)
        c.fgain = sb("f_fgain", [P, D])
        with ExitStack() as inner:
            c.rep = inner.enter_context(nc.sbuf_tensor("e_rep", [P, 3, 2, D], F32))
            merged = inner.enter_context(nc.sbuf_tensor("e_merged", [P, KD, NT], F32))
            phase_e_merge(c, merged)
            c.x2 = c.y[:, :, :].rearrange("p a b -> p (a b)").rearrange("p (t n) -> p t n", n=D)
            phase_e_rows(c, merged)
        phase_e_route(c)
        phase_f_experts(c)
        phase_f_combine(c)


def program(nc, io):
    with ExitStack() as ctx:
        c = allocate(nc, ctx, io)
        with nc.sbuf_tensor("h", [P, KD, NT], F32) as h:
            c.h = h
            phase_a(c)
            phase_b(c)
        phase_c(c)
        phase_d(c)
        phases_e_f(c)


def lay_out(inp):
    import numpy as np
    a = {k: np.asarray(v) for k, v in inp.items()}
    o = {}
    o["x"] = np.concatenate([a["x_prompt"][0], a["x_sample"][0]], 0)
    cond = np.stack([a["c_ctx"], a["c"][0]], -1)
    o["cond"] = cond.reshape(KD, P, 2).transpose(1, 0, 2)
    vec = [a[name].reshape(-1, P) for name, _ in VEC_PARTS]
    o["vecs"] = np.concatenate(vec, 0).T
    o["w_mod"] = a["w_mod"][0].reshape(KD, P, 12, 512).transpose(2, 1, 0, 3)
    o["w_in"] = a["w_in"][0].reshape(KD, P, 14, 256).transpose(2, 1, 0, 3)
    o["w_qkv"] = np.stack([a[n][0].transpose(1, 0, 2) for n in ("mlstm_w_q", "mlstm_w_k", "mlstm_w_v")], 1)
    w_if = np.zeros((P, BH, 2, ROWS), np.float32)
    b_if, m0 = np.zeros((ROWS, 2), np.float32), np.zeros((ROWS, 1), np.float32)
    for d in range(2):
        for g, n in enumerate(("i", "f")):
            w_if[:, :, g, 32 * d:32 * d + 4] = a["mlstm_w_" + n][0, d].reshape(BH, P, 4).transpose(1, 0, 2)
            b_if[32 * d:32 * d + 4, g] = a["mlstm_b_" + n][0, d]
        m0[32 * d:32 * d + 4, 0] = a["state_mlstm_m"][0, 0, d]
    o["w_if"], o["b_if"], o["m0"] = w_if, b_if, m0
    o["c0"] = a["state_mlstm_C"][0, 0].reshape(8, P, P).transpose(1, 0, 2)
    o["n0"] = a["state_mlstm_n"][0, 0].reshape(8, P).T
    cols = [a["rwkv_w_r"][0], a["rwkv_w_k"][0], a["rwkv_w_v"][0]]
    cols += [a[n][0, d] for n in ("rwkv_w1", "rwkv_a1") for d in range(2)] + [a["rwkv_g1"][0]]
    o["w_rwkv"] = np.concatenate(cols, 1).reshape(4, P, 15, P).transpose(1, 0, 2, 3)
    o["w_rank"] = np.stack([a["rwkv_w2"][0].reshape(P, 4 * P), a["rwkv_a2"][0].reshape(P, 4 * P)], 1)
    o["w_g2"] = a["rwkv_g2"][0]
    o["s0"] = a["state_rwkv"][0, 0].reshape(2, 4, 2, RC, RC).transpose(2, 4, 1, 0, 3).reshape(P, 4, 2, RC)
    o["w_branch"] = np.stack([a[n][0].reshape(4, P, D).transpose(1, 0, 2) for n in ("rwkv_w_proj", "mlstm_w_proj")])
    o["w_out"] = a["w_out"][0].reshape(KD, P, D).transpose(1, 0, 2)
    o["w_router"] = np.concatenate([a["moe_w_group"][0], a["moe_w_expert"][0]], 1).reshape(KD, P, 20).transpose(1, 0, 2)
    o["b_router"] = np.concatenate([a["moe_b_group"][0], a["moe_b_expert"][0]])
    o["final_g"] = a["final_norm_g"]
    w13 = np.stack([a["moe_w1"][0], a["moe_w3"][0]], 1)
    o["w13"] = w13.reshape(NEXP, 2, KD, P, DEXP).transpose(0, 3, 1, 2, 4)
    o["w2"] = a["moe_w2"][0].reshape(NEXP, 2, P, D).transpose(0, 2, 1, 3)
    return {k: np.ascontiguousarray(v) for k, v in o.items()}


OUTPUTS = {"y_out": (NT, D), "new_s": (P, HEADS_P, 2, RC), "new_c": (2, BH, P, P), "new_n": (2, P, BH), "new_m": (2, BH)}


def kernel(**inputs):
    import numpy as np
    from concourse import bacc
    from concourse.bass_utils import run_bass_kernel_spmd

    nc = bacc.Bacc("TRN2", target_bir_lowering=False, num_devices=1)
    arrays = {f"in_{name}": a for name, a in lay_out(inputs).items()}
    io = {name[3:]: nc.dram_tensor(name, a.shape, mybir.dt.from_np(a.dtype), kind="ExternalInput").ap() for name, a in arrays.items()}
    for name, shape in OUTPUTS.items():
        io[name] = nc.dram_tensor(f"out_{name}", shape, F32, kind="ExternalOutput").ap()
    program(nc, io)
    r = run_bass_kernel_spmd(nc, [arrays], core_ids=[0]).results[0]
    y = np.asarray(r["out_y_out"])
    s = np.asarray(r["out_new_s"]).reshape(2, RC, HEADS_P, 2, RC).transpose(3, 2, 0, 4, 1).reshape(1, 1, 2, 2 * HEADS_P, RC, RC)
    n = np.asarray(r["out_new_n"]).transpose(0, 2, 1)[None, None]
    return y[None, :PROMPT], y[None, PROMPT:], s, np.asarray(r["out_new_c"])[None, None], n, np.asarray(r["out_new_m"])[None, None]
```

```python
from contextlib import ExitStack

import concourse.bass as bass
from concourse import mybir

F32 = mybir.dt.float32
ACT = mybir.ActivationFunctionType
ALU = mybir.AluOpType
AX = mybir.AxisListType

P = 128
D = 1024
KD = D // P
PROMPT, SAMPLE = 256, 1024
NT = PROMPT + SAMPLE
TILES = NT // P
BLOCKS = [(0, 256), (256, 512), (768, 512)]
STREAMS = [(0, PROMPT), (PROMPT, SAMPLE)]
XA_PAD = NT + 4
NORM_EPS = 1e-6

VEC_PARTS = [("b_mod", 48), ("norm1_g", 8), ("norm2_g", 8), ("rwkv_mu", 24), ("rwkv_w0", 8), ("rwkv_a0", 8),
             ("rwkv_k_k", 4), ("rwkv_k_a", 4), ("rwkv_r_k", 4), ("rwkv_ln_g", 4), ("rwkv_ln_b", 4),
             ("mlstm_conv", 36), ("mlstm_ln_g", 4)]
VEC = {}
NVEC = 0
for _name, _n in VEC_PARTS:
    VEC[_name] = NVEC
    NVEC += _n


def xa_col(t):
    return t + 1 if t < PROMPT else t + 3


class Own:

    def __init__(self, engine, sem, start=0):
        self.engine, self.sem, self.n = engine, sem, start

    def did(self, instruction):
        instruction.then_inc(self.sem, 1)
        self.n += 1
        return self.n

    def settle(self):
        self.engine.wait_ge(self.sem, self.n)


def semaphores(nc, ctx, prefix=""):
    mine = []

    def retire():
        nc.clear_and_free_semaphores(mine)
        nc.all_engine_barrier()
    ctx.callback(retire)

    def sem(name):
        mine.append(nc.alloc_semaphore(prefix + name))
        return mine[-1]
    return sem


def wait_reuse(engine, sem, count):
    if not (isinstance(count, int) and count == 0):
        engine.wait_ge(sem, count)


class Core:
    pass


def allocate(nc, ctx, io):
    c = Core()
    c.nc, c.io = nc, io

    def sb(name, shape):
        return ctx.enter_context(nc.sbuf_tensor(name, shape, F32))

    c.vec = sb("vec", [P, NVEC])
    c.ident = sb("ident", [P, P])
    c.ones = sb("ones", [P, P])
    c.mod = sb("mod", [P, 48, 2])
    c.gain = sb("gain", [P, 2, KD, 2])
    c.xa = sb("xa", [P, 4, XA_PAD])
    c.y = sb("y", [P, 8, NT])
    c.sig = nc.dram_tensor("sig_scratch", (20, P, NT), F32, kind="Internal").ap()
    c.rkv = nc.dram_tensor("rkv_scratch", (3, 4, P, NT), F32, kind="Internal").ap()
    c.hid_g = nc.dram_tensor("hid_g_scratch", (P, NT), F32, kind="Internal").ap()
    c.h2 = nc.dram_tensor("h2_scratch", (NT, D), F32, kind="Internal").ap()
    c.slot_list = nc.dram_tensor("slot_list_scratch", (SLOT_TILES * P, 1), F32, kind="Internal").ap()
    c.ys = nc.dram_tensor("ys_scratch", (SLOT_TILES * P, D), F32, kind="Internal").ap()
    return c


def norm_statistics(act, own, x, tile, junk, sumsq):
    return act.activation(junk, x, ACT.Square, accum_out=sumsq[:, tile:tile + 1])


MOD_PARTS, MOD_FIRST = 12, 4


def phase_a(c):
    nc, io = c.nc, c.io
    with ExitStack() as ctx:
        def sb(name, shape):
            return ctx.enter_context(nc.sbuf_tensor(name, shape, F32))

        sem = semaphores(nc, ctx)
        WRING = 3
        x = sb("a_x", [P, TILES, D])
        wmod = sb("a_wmod", [P, WRING, KD, 512])
        cc = sb("a_cc", [P, KD, 2])
        junk = sb("a_junk", [P, D])
        stat = sb("a_stat", [P, 3, TILES])
        tp = ctx.enter_context(nc.psum_tensor("a_tp", [P, 4, 512], F32))
        consts_in, ident_set, cond_silu = sem("a_consts_in"), sem("a_ident_set"), sem("a_cond_silu")
        w_in = [sem(f"a_w_in{i}") for i in range(WRING)]
        x_in = [sem(f"a_x_in{i}") for i in range(TILES)]
        w_used, mod_half = sem("a_w_used"), sem("a_mod_half")
        squares, std_set, x_scaled = sem("a_squares"), sem("a_std_set"), sem("a_x_scaled")
        turned, act_evac, dve_evac, dve_own = sem("a_turned"), sem("a_act_evac"), sem("a_dve_evac"), sem("a_dve_own")
        block = ctx.enter_context(nc.Block())

        @block.sync
        def _(sp):
            sp.dma_start(cc[:, :, :], io["cond"]).then_inc(consts_in, 16)
            sp.dma_start(c.vec[:, :], io["vecs"]).then_inc(consts_in, 16)
            for g in range(MOD_FIRST):
                if g >= WRING:
                    sp.wait_ge(w_used, g - WRING + 1)
                sp.dma_start(wmod[:, g % WRING], io["w_mod"][g]).then_inc(w_in[g % WRING], 16)
                if g < 2:
                    for t in range(5 * g, 5 * g + 5):
                        sp.dma_start(x[:, t], io["x"][t * P:(t + 1) * P, :]).then_inc(x_in[t], 16)

        @block.gpsimd
        def _(pool):
            pool.memset(c.ones[:, :], 1.0).then_inc(ident_set, 1)
            pool.wait_ge(ident_set, 1)
            pool.affine_select(out=c.ident[:, :], in_=c.ones[:, :], compare_op=ALU.is_equal, fill=0.0, base=0,
                               pattern=[[-1, P]], channel_multiplier=1).then_inc(ident_set, 1)

        @block.scalar
        def _(act):
            act.wait_ge(consts_in, 32)
            act.activation(c.cs[:, :, :], cc[:, :, :], ACT.Silu).then_inc(cond_silu, 1)
            for t in range(TILES):
                act.wait_ge(x_in[t], 16)
                act.activation(junk[:, :], x[:, t], ACT.Square, accum_out=stat[:, 0, t:t + 1]).then_inc(squares, 1)
                act.wait_ge(squares, t + 1)
            act.wait_ge(dve_own, 1)
            act.activation(stat[:, 2], stat[:, 1], ACT.Sqrt).then_inc(std_set, 1)
            act.wait_ge(mod_half, 2)
            for n in range(0, 24, 2):
                feature_evac(act, c, tp, turned, act_evac, n, 0, c.y)

        @block.vector
        def _(dve):
            dve.wait_ge(squares, TILES)
            dve.tensor_scalar(stat[:, 1], stat[:, 0], 1.0 / D, NORM_EPS, ALU.mult, ALU.add).then_inc(dve_own, 1)
            dve.wait_ge(std_set, 1)
            dve.reciprocal(stat[:, 1], stat[:, 2]).then_inc(dve_own, 1)
            dve.wait_ge(dve_own, 2)
            for t in range(TILES):
                dve.tensor_scalar(x[:, t], x[:, t], stat[:, 1, t:t + 1], None, ALU.mult).then_inc(x_scaled, 1)
            dve.wait_ge(w_used, MOD_FIRST)
            dve.tensor_tensor(c.mod[:, 0:16, :], c.pm[:, 0:16, :],
                              c.vec[:, 0:16].unsqueeze(2).to_broadcast([P, 16, 2]), ALU.add).then_inc(mod_half, 1)
            dve.wait_ge(mod_half, 1)
            dve.scalar_tensor_tensor(c.gain[:, 0], c.mod[:, 8:16, :], 1.0,
                                     c.vec[:, VEC["norm1_g"]:VEC["norm1_g"] + 8].unsqueeze(2).to_broadcast([P, 8, 2]),
                                     ALU.add, ALU.mult).then_inc(mod_half, 1)
            dve.wait_ge(mod_half, 2)
            for n in range(1, 24, 2):
                feature_evac(dve, c, tp, turned, dve_evac, n, 0, c.y)

        @block.tensor
        def _(pe):
            pe.wait_ge(cond_silu, 1)

            for g in range(MOD_FIRST):
                pe.wait_ge(w_in[g % WRING], 16 * (g // WRING + 1))
                modulation(pe, c, g, wmod[:, g % WRING]).then_inc(w_used, 1)
            pe.wait_ge(ident_set, 2)
            for n in range(24):
                feature_turn(pe, c, x, tp, turned, act_evac, dve_evac, x_scaled, n)


def modulation(pe, c, g, w):
    for j in range(4):
        for k in range(KD):
            mm = pe.matmul(c.pm[:, 4 * g + j, :], w[:, k, j * P:(j + 1) * P], c.cs[:, k, :], start=(k == 0), stop=(k == KD - 1))
    return mm


def feature_turn(pe, c, x, tp, turned, act_evac, dve_evac, x_scaled, n):
    b, k = divmod(n, KD)
    first, width = BLOCKS[b]
    if k == 0:
        pe.wait_ge(x_scaled, (first + width) // P)
    if n >= 4:
        pe.wait_ge(act_evac if n % 2 == 0 else dve_evac, (n - 4) // 2 + 1)
    for i in range(width // P):
        mm = pe.transpose(tp[:, n % 4, i * P:(i + 1) * P], x[:, first // P + i, k * P:(k + 1) * P], c.ident[:, :])
    mm.then_inc(turned, 1)


def feature_evac(eng, c, tp, turned, evac, n, norm, h):
    b, k = divmod(n, KD)
    first, width = BLOCKS[b]
    s = 0 if b == 0 else 1
    gain = c.gain[:, norm, k, s:s + 1]
    shift = c.mod[:, 24 * norm + k, s:s + 1]
    eng.wait_ge(turned, n + 1)
    out, src = h[:, k, first:first + width], tp[:, n % 4, 0:width]
    if n % 2 == 0:
        eng.activation(out, src, ACT.Identity, bias=shift, scale=gain).then_inc(evac, 1)
    else:
        eng.tensor_scalar(out, src, gain, shift, ALU.mult, ALU.add).then_inc(evac, 1)


def rounded(ap):
    return ap.bitcast(mybir.dt.float32r)


def phase_b(c):
    nc, io = c.nc, c.io
    with ExitStack() as ctx:
        sem = semaphores(nc, ctx)
        w = ctx.enter_context(nc.sbuf_tensor("b_w", [P, KD, 256], F32))
        w_lo = ctx.enter_context(nc.sbuf_tensor("b_w_lo", [P, 2, KD, 256], F32))
        w_hi = ctx.enter_context(nc.sbuf_tensor("b_w_hi", [P, 2, KD, 256], F32))
        h_hi = ctx.enter_context(nc.sbuf_tensor("b_h_hi", [P, KD, NT], F32))
        h_lo = ctx.enter_context(nc.sbuf_tensor("b_h_lo", [P, KD, NT], F32))
        stage = ctx.enter_context(nc.sbuf_tensor("b_stage", [P, 2, NT], F32))
        wmod = c.y[:, 4:8].rearrange("p a t -> p (a t)")[:, 0:KD * 512].rearrange("p (k n) -> p k n", k=KD)
        ps = [ctx.enter_context(nc.psum_tensor(f"b_ps{i}", [P, 3, 512], F32)) for i in range(2)]
        w_in, projected, copied, bank_free = sem("b_w_in"), sem("b_projected"), sem("b_copied"), sem("b_bank_free")
        sig_part, sig_set, padded = sem("b_sig_part"), sem("b_sig_set"), sem("b_padded")
        sig_stored = [sem(f"b_sig_stored{i}") for i in range(2)]
        h_hi_set, h_split, w_hi_set, w_split = sem("b_h_hi_set"), sem("b_h_split"), sem("b_w_hi_set"), sem("b_w_split")
        partial = ctx.enter_context(nc.sbuf_tensor("b_partial", [P, 2, 512], F32))
        mod_in, mod_term, mod_summed, mod_set = (sem(f"b_{n}") for n in ("mod_in", "mod_term", "mod_summed", "mod_set"))
        TERMS = 2 * KD
        block = ctx.enter_context(nc.Block())

        def load(sp, i, g):
            sp.dma_start(w[:, :, :], io["w_in"][bass.ds(i * 2 + g, 1)].rearrange("o p k n -> p (o k) n")).then_inc(w_in, 16)

        @block.sync
        def _(sp):
            load(sp, 0, 0)
            sp.wait_ge(w_split, 1)
            load(sp, 0, 1)
            with sp.Fori(1, 7) as i:
                for g in range(2):
                    sp.wait_ge(w_split, i * 2 + g)
                    load(sp, i, g)

        @block.tensor
        def _(pe):
            def project(j, h_waits=False):
                for n, (first, width) in enumerate(BLOCKS):
                    if h_waits:
                        pe.wait_ge(h_split, n + 1)
                    for k in range(KD):
                        for i, (wt, ht) in enumerate(((w_lo, h_hi), (w_hi, h_lo), (w_hi, h_hi))):
                            mm = pe.matmul(ps[j % 2][:, n, 0:width], rounded(wt[:, j // 2, k, (j % 2) * P:(j % 2 + 1) * P]),
                                           rounded(ht[:, k, first:first + width]), start=(k == 0 and i == 0), stop=(k == KD - 1 and i == 2))
                mm.then_inc(projected, 1)
            def sum_part(n):
                pe.wait_ge(mod_term, n * TERMS + TERMS)
                for j in range(4):
                    for s in range(2):
                        mm = pe.matmul(c.pm[:, bass.ds(n * 4 + (4 * MOD_FIRST + j), 1), s:s + 1], partial[:, s, j * P:(j + 1) * P],
                                       c.ones[:, 0:1], start=True, stop=True)
                mm.then_inc(mod_summed, 1)
            for f in range(8):
                if f % 2 == 0:
                    pe.wait_ge(w_split, f // 2 + 1)
                if f >= 2:
                    pe.wait_ge(copied, f - 1)
                project(f % 4, h_waits=(f == 0))
                if f in (3, 5, 7):
                    sum_part((f - 3) // 2)
            with pe.Fori(0, 5) as i:
                for j in range(4):
                    if j % 2 == 0:
                        pe.wait_ge(w_split, i * 2 + (j // 2 + 5))
                    pe.wait_ge(bank_free, i * 4 + (j + 1))
                    project(j)
                sum_part(i + 3)

        @block.vector
        def _(dve):
            def split_w(i, g):
                dve.wait_ge(w_hi_set, i * 2 + (g + 1))
                dve.tensor_tensor(rounded(w_lo[:, g]), w[:, :, :], w_hi[:, g], ALU.subtract).then_inc(w_split, 1)

            def make_part(n):
                dve.wait_ge(mod_in, n * 16 + 16)
                wait_reuse(dve, mod_summed, n)
                for k in range(KD):
                    for s in range(2):
                        if k == 0:
                            term = dve.tensor_scalar(partial[:, s], wmod[:, k], c.cs[:, k, s:s + 1], None, ALU.mult)
                        else:
                            if s == 0:
                                dve.wait_ge(mod_term, n * TERMS + 2 * k)
                            term = dve.scalar_tensor_tensor(partial[:, s], wmod[:, k], c.cs[:, k, s:s + 1], partial[:, s], ALU.mult, ALU.add)
                        term.then_inc(mod_term, 1)
            split_w(0, 0)
            for n, (first, width) in enumerate(BLOCKS):
                dve.wait_ge(h_hi_set, n + 1)
                cols = slice(first, first + width)
                dve.tensor_tensor(rounded(h_lo[:, :, cols]), c.y[:, :, cols], h_hi[:, :, cols], ALU.subtract).then_inc(h_split, 1)
            split_w(0, 1)
            dve.wait_ge(h_split, 3)
            dve.memset(c.xa[:, :, 0:1], 0.0).then_inc(padded, 1)
            dve.memset(c.xa[:, :, PROMPT + 1:PROMPT + 3], 0.0).then_inc(padded, 1)
            dve.memset(c.xa[:, :, XA_PAD - 1:XA_PAD], 0.0).then_inc(padded, 1)
            for f in range(8):
                dve.wait_ge(projected, f + 1)
                for n, (first, width) in enumerate(BLOCKS):
                    at = xa_col(first)
                    out = c.xa[:, f, at:at + width] if f < 4 else c.y[:, f - 4, first:first + width]
                    cp = dve.tensor_copy(out, ps[f % 2][:, n, 0:width])
                cp.then_inc(copied, 1)
                if f % 2 == 1 and f < 7:
                    split_w(1 + f // 4, f % 4 // 2)
                    make_part((f - 1) // 2)
            split_w(2, 1)
            with dve.Fori(0, 4) as i:
                make_part(i + 3)
                for g in range(2):
                    split_w(i + 3, g)
            make_part(7)
            dve.wait_ge(mod_summed, MOD_PARTS - MOD_FIRST)
            dve.tensor_tensor(c.mod[:, 16:48, :], c.pm[:, 16:48, :],
                              c.vec[:, 16:48].unsqueeze(2).to_broadcast([P, 32, 2]), ALU.add).then_inc(mod_set, 1)
            dve.wait_ge(mod_set, 1)
            dve.scalar_tensor_tensor(c.gain[:, 1], c.mod[:, 32:40, :], 1.0,
                                     c.vec[:, VEC["norm2_g"]:VEC["norm2_g"] + 8].unsqueeze(2).to_broadcast([P, 8, 2]),
                                     ALU.add, ALU.mult).then_inc(mod_set, 1)

        @block.scalar
        def _(act):
            def load_part(n):
                if isinstance(n, int) and n == 0:
                    act.wait_ge(h_split, 3)
                else:
                    act.wait_ge(mod_term, n * TERMS)
                act.dma_start(wmod[:, :, :], io["w_mod"][bass.ds(n + MOD_FIRST, 1)].rearrange("o p k n -> p (o k) n")).then_inc(mod_in, 16)

            def high_w(i, g):
                act.wait_ge(w_in, i * 32 + 16 * (g + 1))
                if not (isinstance(i, int) and i == 0):
                    act.wait_ge(projected, i * 4 + (2 * g - 2))
                act.activation(rounded(w_hi[:, g]), w[:, :, :], ACT.Copy).then_inc(w_hi_set, 1)

            def sigmoids(i, j):
                act.wait_ge(projected, i * 4 + (8 + j + 1))
                if j >= 2:
                    act.wait_ge(sig_stored[j % 2], i * 32 + 16)
                else:
                    wait_reuse(act, sig_stored[j % 2], i * 32)
                for n, (first, width) in enumerate(BLOCKS):
                    a = act.activation(stage[:, j % 2, first:first + width], ps[j % 2][:, n, 0:width], ACT.Sigmoid)
                    if n < 2:
                        a.then_inc(sig_part, 1)
                a.then_inc(sig_set, 1)
                act.wait_ge(sig_set, i * 4 + (j + 1))
                act.sem_inc(bank_free, 1)
            high_w(0, 0)
            for n, (first, width) in enumerate(BLOCKS):
                cols = slice(first, first + width)
                act.activation(rounded(h_hi[:, :, cols]), c.y[:, :, cols], ACT.Copy).then_inc(h_hi_set, 1)
            load_part(0)
            high_w(0, 1)
            for n in range(1, 4):
                high_w(1 + (n - 1) // 2, (n - 1) % 2)
                load_part(n)
            for j in range(2):
                act.wait_ge(copied, 7 + j)
                act.sem_inc(bank_free, 1)
            high_w(2, 1)
            for j in range(4):
                sigmoids(0, j)
                if j % 2 == 1:
                    high_w(3, j // 2)
            with act.Fori(1, 4) as i:
                load_part(i + 3)
                for j in range(4):
                    sigmoids(i, j)
                    if j % 2 == 1:
                        high_w(i + 3, j // 2)
            load_part(7)
            for j in range(4):
                sigmoids(4, j)

        @block.gpsimd
        def _(pool):
            with pool.Fori(0, 5) as i:
                for j in range(4):
                    pool.wait_ge(sig_set, i * 4 + (j + 1))
                    pool.wait_ge(sig_part, i * 8 + (2 * j + 2))
                    pool.dma_start(c.sig[bass.ds(i * 4 + j, 1)].rearrange("o p t -> p (o t)"), stage[:, j % 2]).then_inc(sig_stored[j % 2], 16)
            for j in range(2):
                pool.wait_ge(sig_stored[j], 10 * 16)


CH = 128
NCH = NT // CH
BH = 4
ROWS = 36
BIG = 1e30
CONV_STEPS = BH * (1 + 8 + 2)
GATE_STEPS = 19


def phase_c_prepare(c):
    nc, io = c.nc, c.io
    with ExitStack() as ctx:
        def sb(name, shape):
            return ctx.enter_context(nc.sbuf_tensor(name, shape, F32))

        sem = semaphores(nc, ctx)
        uc = c.y[:, 4:8]
        w = sb("c_w", [P, 3, BH, P])
        wif = sb("c_wif", [P, BH, 2, ROWS])
        bif = sb("c_bif", [ROWS, 2])
        gb, keep = sb("c_beta_rows", [ROWS, NT]), sb("c_keep", [ROWS, NT])
        lf, li = c.rows[:, 1], c.rows[:, 2]
        mprev = sb("c_mprev", [ROWS, NCH])
        ps = [ctx.enter_context(nc.psum_tensor(f"c_ps{i}", [P, 3, 512], F32)) for i in range(2)]
        pt = ctx.enter_context(nc.psum_tensor("c_pt", [P, 2, BH, P], F32))
        loaded, conv_done, uc_set = sem("c_loaded"), sem("c_conv_done"), sem("c_uc_set")
        wide_ready, wide_act, wide_dve = sem("c_wide_ready"), sem("c_wide_act"), sem("c_wide_dve")
        tok_ready, tok_read = sem("c_tok_ready"), sem("c_tok_read")
        gate_act, gate_dve = sem("c_gate_act"), sem("c_gate_dve")
        masks, masks_pool = sem("c_masks"), sem("c_masks_pool")
        beta_turned = sem("c_beta_turned")
        conv = VEC["mlstm_conv"]
        block = ctx.enter_context(nc.Block())

        @block.sync
        def _(sp):
            sp.dma_start(w[:, :, :, :], io["w_qkv"]).then_inc(loaded, 16)
            sp.dma_start(wif[:, :, :, :], io["w_if"]).then_inc(loaded, 16)
            sp.dma_start(bif[:, :], io["b_if"]).then_inc(loaded, 16)
            sp.dma_start(c.m0[:, :], io["m0"]).then_inc(loaded, 16)
            sp.dma_start(c.cn[:, 1, :, 0:P], io["c0"]).then_inc(loaded, 16)
            sp.dma_start(c.n0[:, :], io["n0"]).then_inc(loaded, 16)

        @block.gpsimd
        def _(pool):
            pool.memset(c.cmask[:, :, :], 0.0).then_inc(masks_pool, 1)
            pool.wait_ge(masks_pool, 1)
            for d in range(2):
                sgn = 1 - 2 * d
                pool.affine_select(out=c.cmask[:, d], in_=c.cmask[:, d], compare_op=ALU.is_ge, fill=-BIG, base=0,
                                   pattern=[[sgn, CH]], channel_multiplier=-sgn).then_inc(masks, 1)
            pool.memset(keep[:, :], 1.0).then_inc(masks_pool, 1)
            pool.wait_ge(masks_pool, 2)
            for d in range(2):
                part = keep[32 * d:32 * d + 4, :].rearrange("p (n t) -> p n t", t=CH)
                at = (CH - 1) * d
                pool.memset(part[:, :, at:at + 1], 0.0).then_inc(masks, 1)

        @block.tensor
        def _(pe):
            def wide(n, lhs, rhs, rows):
                if n >= 2:
                    pe.wait_ge(wide_act if n % 2 == 0 else wide_dve, (n - 2) // 2 + 1)
                for m, (first, width) in enumerate(BLOCKS):
                    for k in range(len(lhs)):
                        mm = pe.matmul(ps[n % 2][0:rows, m, 0:width], lhs[k], rhs[k][:, first:first + width],
                                       start=(k == 0), stop=(k == len(lhs) - 1))
                mm.then_inc(wide_ready, 1)

            def tok(n, src, which):
                if n >= 2:
                    pe.wait_ge(tok_read, n - 1)
                t = n % NCH
                for h in range(BH):
                    mm = pe.matmul(pt[:, n % 2, h], src[:, h, t * P:(t + 1) * P], w[:, which, h], start=True, stop=True)
                mm.then_inc(tok_ready, 1)
            pe.wait_ge(loaded, 96)
            for n in range(NCH):
                tok(n, c.y, 2)
            pe.wait_ge(uc_set, BH)
            for g in range(2):
                wide(g, [wif[:, k, g, :] for k in range(BH)], [uc[:, k] for k in range(BH)], ROWS)
            for h in range(BH):
                for which in range(2):
                    wide(2 + 2 * h + which, [w[:, which, h]], [uc[:, h]], P)
            for n in range(NCH, 2 * NCH):
                tok(n, uc, 1)
            pe.wait_ge(wide_act, 1 + BH)
            pe.wait_ge(gate_dve, GATE_STEPS)
            for ch in range(NCH):
                mm = pe.transpose(ps[0][:, 0, ch * ROWS:(ch + 1) * ROWS], gb[:, ch * CH:(ch + 1) * CH], c.ident[0:ROWS, 0:ROWS])
            mm.then_inc(beta_turned, 1)

        @block.vector
        def _(dve):
            own = Own(dve, conv_done)
            last = [0] * BH
            for tap, (dy, dx) in enumerate([(1, 1)] + [(a, b) for a in range(3) for b in range(3) if (a, b) != (1, 1)]):
                for k in range(BH):
                    wcol = c.vec[:, conv + (3 * dy + dx) * BH + k:conv + (3 * dy + dx) * BH + k + 1]
                    u_lat = c.y[:, k, PROMPT:].rearrange("p (r w) -> p r w", w=64)
                    o_lat = uc[:, k, PROMPT:].rearrange("p (r w) -> p r w", w=64)
                    if tap == 0:
                        last[k] = own.did(dve.tensor_scalar(uc[:, k], c.y[:, k], wcol, None, ALU.mult))
                        continue
                    dve.wait_ge(conv_done, last[k])
                    r0, r1 = max(0, 1 - dy), 16 - max(0, dy - 1)
                    x0, x1 = max(0, 1 - dx), 64 - max(0, dx - 1)
                    o = o_lat[:, r0:r1, x0:x1]
                    last[k] = own.did(dve.scalar_tensor_tensor(
                        o, u_lat[:, r0 + dy - 1:r1 + dy - 1, x0 + dx - 1:x1 + dx - 1], wcol, o, ALU.mult, ALU.add))
                    if dy == 1:
                        x0, x1 = max(0, 1 - dx), PROMPT - max(0, dx - 1)
                        o = uc[:, k, x0:x1]
                        last[k] = own.did(dve.scalar_tensor_tensor(
                            o, c.y[:, k, x0 + dx - 1:x1 + dx - 1], wcol, o, ALU.mult, ALU.add))
            assert own.n == CONV_STEPS, own.n
            own = Own(dve, gate_dve)
            own.did(dve.memset(c.rows[:, 3], 0.0))
            dve.wait_ge(wide_ready, 2)
            dve.wait_ge(loaded, 96)
            for m, (first, width) in enumerate(BLOCKS):
                cp = dve.tensor_scalar(lf[:, first:first + width], ps[1][0:ROWS, m, 0:width], bif[:, 1:2], None, ALU.add)
                cp.then_inc(wide_dve if m == 2 else gate_dve, 1)
            own.n += 2
            for h in range(BH):
                dve.wait_ge(wide_ready, 2 + 2 * h + 2)
                for m, (first, width) in enumerate(BLOCKS):
                    cp = dve.tensor_scalar(c.kt[:, h, first:first + width], ps[1][:, m, 0:width], P ** -0.5, None, ALU.mult)
                cp.then_inc(wide_dve, 1)
            dve.wait_ge(gate_act, 3)
            own.did(dve.scalar_tensor_tensor(lf[:, :], lf[:, :], 0.0, gb[:, :], ALU.min, ALU.subtract))
            own.settle()
            dve.wait_ge(masks, 4)
            b, m = gb, c.rows[:, 3]
            fwd, bwd = (slice(0, 4), slice(None)), (slice(32, 36), slice(None, None, -1))
            for rows, step in (fwd, bwd):
                own.did(dve.tensor_tensor_scan(b[rows, step], keep[rows, step], lf[rows, step], 0.0, ALU.mult, ALU.add))
                for s, (first, width) in enumerate(STREAMS):
                    def part(t):
                        v = t[rows, first:first + width]
                        return v if step.step is None else v[:, ::-1]
                    own.did(dve.tensor_tensor_scan(part(m), part(lf), part(li), c.m0[rows, 0:1] if s else 0.0,
                                                   ALU.add, ALU.max))
            own.settle()
            mc = m.rearrange("p (n t) -> p n t", t=CH)
            own.did(dve.memset(mprev[:, :], 0.0))
            own.settle()
            own.did(dve.tensor_copy(mprev[0:4, 1:NCH], mc[0:4, 0:NCH - 1, CH - 1]))
            own.did(dve.tensor_copy(mprev[32:36, 0:NCH - 1], mc[32:36, 1:NCH, 0]))
            own.settle()
            edges = (0, PROMPT // CH, NCH)
            own.did(dve.tensor_copy(mprev[0:4, edges[1]:edges[1] + 1], c.m0[0:4, 0:1]))
            own.did(dve.tensor_copy(mprev[32:36, NCH - 1:NCH], c.m0[32:36, 0:1]))
            own.did(dve.memset(mprev[32:36, edges[1] - 1:edges[1]], 0.0))
            own.did(dve.tensor_tensor(c.rows[:, 0], b[:, :], m, ALU.subtract))
            own.settle()
            own.did(dve.tensor_tensor(b[:, :], li[:, :], b[:, :], ALU.subtract))
            own.did(dve.tensor_tensor(c.rows[:, 1].rearrange("p (n t) -> p n t", t=CH),
                                      c.rows[:, 0].rearrange("p (n t) -> p n t", t=CH),
                                      mprev[:, :].unsqueeze(2).to_broadcast([ROWS, NCH, CH]), ALU.add))
            own.settle()
            assert own.n == GATE_STEPS, own.n
            for d in range(2):
                own.did(dve.tensor_copy(c.sel[:, 4 * d:4 * d + 4, :],
                                        c.ident[0:ROWS, 32 * d:32 * d + 4].unsqueeze(2).to_broadcast([ROWS, 4, P])))
            own.did(dve.memset(c.cn[:, 0], 0.0))
            own.did(dve.tensor_copy(c.cn[:, 1, :, P:2 * P], c.n0[:, :].unsqueeze(2).to_broadcast([P, 8, P])))
            own.did(dve.scalar_tensor_tensor(c.center[:, :], c.ones[:, :], -1.0 / P, c.ident[:, :], ALU.mult, ALU.add))
            dve.wait_ge(beta_turned, 1)
            own.did(dve.tensor_copy(c.betat[:, :, :], ps[0][:, 0, 0:NCH * ROWS].rearrange("p (n r) -> p n r", r=ROWS)))

        @block.scalar
        def _(act):
            for n in range(NCH):
                act.wait_ge(tok_ready, n + 1)
                act.activation(c.vtok[:, n], pt[:, n % 2], ACT.Copy).then_inc(tok_read, 1)
            act.wait_ge(conv_done, CONV_STEPS)
            for k in range(BH):
                act.activation(uc[:, k], uc[:, k], ACT.Silu).then_inc(uc_set, 1)
            act.wait_ge(loaded, 96)
            act.wait_ge(wide_ready, 1)
            for m, (first, width) in enumerate(BLOCKS):
                cp = act.activation(li[:, first:first + width], ps[0][0:ROWS, m, 0:width], ACT.Identity, bias=bif[:, 0:1])
                cp.then_inc(wide_act if m == 2 else uc_set, 1)
            for h in range(BH):
                act.wait_ge(wide_ready, 2 + 2 * h + 1)
                for m, (first, width) in enumerate(BLOCKS):
                    cp = act.activation(c.qt[:, h, first:first + width], ps[0][:, m, 0:width], ACT.Copy)
                cp.then_inc(wide_act, 1)
            act.wait_ge(wide_dve, 1)
            act.wait_ge(gate_dve, 3)
            for n, (func, src, kw) in enumerate([(ACT.Abs, lf, {}), (ACT.Exp, gb, {"scale": -1.0}), (ACT.Ln, gb, {"bias": 1.0})]):
                if n:
                    act.wait_ge(gate_act, n)
                act.activation(gb[:, :], src[:, :], func, **kw).then_inc(gate_act, 1)
            for n in range(NCH, 2 * NCH):
                act.wait_ge(tok_ready, n + 1)
                act.activation(c.ktok[:, n - NCH], pt[:, n % 2], ACT.Copy, scale=P ** -0.5).then_inc(tok_read, 1)
            act.wait_ge(gate_dve, GATE_STEPS)
            act.activation(c.rows[:, 1], c.rows[:, 1], ACT.Exp).then_inc(gate_act, 1)
            act.activation(c.rows[:, 2], c.rows[:, 3], ACT.Exp, scale=-1.0).then_inc(gate_act, 1)


def phase_c_scan(c):
    nc, io = c.nc, c.io
    order = []
    np_, ns = PROMPT // CH, SAMPLE // CH
    for i in range(ns):
        order += [(1, 0, np_ + i), (1, 1, np_ + ns - 1 - i)]
        if i < np_:
            order += [(0, 0, i), (0, 1, np_ - 1 - i)]
    before, seen, first_of = [], {}, {}
    for j, (s, d, ch) in enumerate(order):
        before.append(seen.get((s, d)))
        seen[(s, d)] = j
        first_of.setdefault(ch, j)
    N = len(order)
    seconds = [sum(first_of[ch] != i for i, (_, _, ch) in enumerate(order[:j])) for j in range(N)]
    with ExitStack() as ctx:
        def sb(name, shape):
            return ctx.enter_context(nc.sbuf_tensor(name, shape, F32))

        def pb(name, shape):
            return ctx.enter_context(nc.psum_tensor(name, shape, F32))

        sem = semaphores(nc, ctx)
        expo, sd, qi, kw = (sb(f"s_{n}", [P, 2, BH, P]) for n in ("expo", "sd", "qi", "kw"))
        hn = sb("s_hn", [P, BH, P])
        absd = sb("s_absd", [P, BH, P])
        decay = sb("s_decay", [P, 2, BH])
        p_ab, p_ib, p_st, p_nu, p_de = pb("s_ab", [P, 2, BH, P]), pb("s_ib", [P, BH, P]), pb("s_st", [P, BH, P]), pb("s_nu", [P, BH, P]), pb("s_de", [P, BH, P])
        p_dc = pb("s_dc", [P, BH, 2 * P])
        ab_ready, ib_ready, st_ready, nd_ready, en_ready, dc_ready = (sem(f"s_{n}_ready") for n in ("ab", "ib", "st", "nd", "en", "dc"))
        e1_set, qi_set, sd_set, cn_set, mx_set, h_set, dve_own = (sem(f"s_{n}") for n in ("e1_set", "qi_set", "sd_set", "cn_set", "mx_set", "h_set", "dve_own"))
        exp_set, abs_set, kw_set, added, stored = (sem(f"s_{n}") for n in ("exp_set", "abs_set", "kw_set", "added", "stored"))
        kw_part, n_set, num_set = sem("s_kw_part"), sem("s_n_set"), sem("s_num_set")
        block = ctx.enter_context(nc.Block())

        def row(which, ch):
            return c.rows[:, which, ch * CH:(ch + 1) * CH]

        @block.tensor
        def _(pe):
            def spread(bank, which, j, ready):
                s, d, ch = order[j]
                for h in range(BH):
                    mm = pe.matmul(bank[:, h], c.sel[:, 4 * d + h], row(which, ch), start=True, stop=True)
                mm.then_inc(ready, 1)

            def alpha_inter(j):
                if j >= 2:
                    pe.wait_ge(mx_set, j - 1)
                spread(p_ab[:, j % 2], 0, j, ab_ready)
                if j >= 1:
                    pe.wait_ge(qi_set, j)
                spread(p_ib, 1, j, ib_ready)

            def scores(j):
                s, d, ch = order[j]
                if j >= 1:
                    pe.wait_ge(sd_set, j)
                for h in range(BH):
                    mm = pe.matmul(p_st[:, h], c.kt[:, h, ch * CH:(ch + 1) * CH], c.qt[:, h, ch * CH:(ch + 1) * CH], start=True, stop=True)
                mm.then_inc(st_ready, 1)
            alpha_inter(0)
            scores(0)
            for j, (s, d, ch) in enumerate(order):
                pe.wait_ge(qi_set, j + 1)
                pe.wait_ge(sd_set, j + 1)
                if before[j] is not None:
                    pe.wait_ge(cn_set, before[j] + 1)
                if j >= 1:
                    pe.wait_ge(num_set, j)
                    pe.wait_ge(abs_set, j)
                for h in range(BH):
                    cn = c.cn[:, s, 4 * d + h]
                    pe.matmul(p_nu[:, h], c.vtok[:, ch, h], sd[:, j % 2, h], start=True, stop=False)
                    pe.matmul(p_nu[:, h], cn[:, 0:P], qi[:, j % 2, h], start=False, stop=True)
                for h in range(BH):
                    cn = c.cn[:, s, 4 * d + h]
                    pe.matmul(p_de[:, h], c.ones[:, :], sd[:, j % 2, h], start=True, stop=False)
                    mm = pe.matmul(p_de[:, h], cn[:, P:2 * P], qi[:, j % 2, h], start=False, stop=True)
                mm.then_inc(nd_ready, 1)
                if j + 1 < N:
                    alpha_inter(j + 1)
                    scores(j + 1)
                pe.wait_ge(e1_set, j + 1)
                spread(p_ab[:, j % 2], 2, j, en_ready)
                pe.wait_ge(kw_set, j + 1)
                if j >= 1:
                    pe.wait_ge(cn_set, j)
                for h in range(BH):
                    pe.matmul(p_dc[:, h, 0:P], kw[:, j % 2, h], c.vtok[:, ch, h], start=True, stop=True)
                    mm = pe.matmul(p_dc[:, h, P:2 * P], kw[:, j % 2, h], c.ones[:, :], start=True, stop=True)
                mm.then_inc(dc_ready, 1)

        @block.vector
        def _(dve):
            own = Own(dve, dve_own)
            def finish(j):
                s, d, ch = order[j]
                dve.wait_ge(dc_ready, j + 1)
                for h in range(BH):
                    cn = c.cn[:, s, 4 * d + h]
                    cp = dve.scalar_tensor_tensor(cn, cn, decay[:, j % 2, h:h + 1], p_dc[:, h], ALU.mult, ALU.add)
                    if h < BH - 1:
                        own.did(cp)
                own.settle()
                cp.then_inc(cn_set, 1)
                if seen[(0, d)] == j and s == 0:
                    dve.wait_ge(cn_set, j + 1)
                    dve.tensor_copy(c.n0[:, 4 * d:4 * d + 4], c.cn[:, 0, 4 * d:4 * d + 4, P]).then_inc(n_set, 1)
                dve.wait_ge(en_ready, j + 1)
                dve.wait_ge(abs_set, j + 1)
                dve.tensor_tensor(absd[:, :, :], absd[:, :, :], p_ab[:, j % 2], ALU.max).then_inc(mx_set, 1)
                dve.wait_ge(mx_set, j + 1)
                own.did(dve.reciprocal(absd[:, :, :], absd[:, :, :]))
                own.settle()
                dve.wait_ge(num_set, j + 1)
                out = c.y[:, 4:8, ch * CH:(ch + 1) * CH]
                if first_of[ch] != j:
                    out = hn[:, :, :]
                dve.tensor_tensor(out, absd[:, :, :], hn[:, :, :], ALU.mult).then_inc(h_set, 1)

            def weights(j):
                s, d, ch = order[j]
                dve.wait_ge(ab_ready, j + 1)
                for h in range(BH):
                    cp = dve.scalar_tensor_tensor(expo[:, j % 2, h], p_ab[:, j % 2, h],
                                                  c.betat[:, ch, 32 * d + h:32 * d + h + 1], c.cmask[:, d], ALU.add, ALU.min)
                    if h < BH - 1:
                        own.did(cp)
                own.settle()
                cp.then_inc(e1_set, 1)
                dve.wait_ge(ib_ready, j + 1)
                end = (CH - 1) * (1 - d)
                own.did(dve.tensor_copy(decay[:, j % 2], p_ib[:, :, end]))
                own.settle()
                dve.tensor_tensor(qi[:, j % 2], c.qt[:, :, ch * CH:(ch + 1) * CH], p_ib[:, :, :], ALU.mult).then_inc(qi_set, 1)
            weights(0)
            for j in range(N):
                dve.wait_ge(exp_set, j + 1)
                dve.wait_ge(st_ready, j + 1)
                dve.tensor_tensor(sd[:, j % 2], expo[:, j % 2], p_st[:, :, :], ALU.mult).then_inc(sd_set, 1)
                if j >= 1:
                    finish(j - 1)
                if j + 1 < N:
                    weights(j + 1)
            finish(N - 1)

        @block.scalar
        def _(act):
            for j in range(N):
                act.wait_ge(e1_set, j + 1)
                act.activation(expo[:, j % 2], expo[:, j % 2], ACT.Exp).then_inc(exp_set, 1)
                act.wait_ge(nd_ready, j + 1)
                if j >= 1:
                    act.wait_ge(h_set, j)
                act.activation(absd[:, :, :], p_de[:, :, :], ACT.Abs).then_inc(abs_set, 1)
                if j >= 1 and seconds[j] > 0:
                    act.wait_ge(added, seconds[j])
                act.activation(hn[:, :, :], p_nu[:, :, :], ACT.Copy).then_inc(num_set, 1)

        @block.gpsimd
        def _(pool):
            def add(j):
                s, d, ch = order[j]
                if first_of[ch] != j:
                    y = c.y[:, 4:8, ch * CH:(ch + 1) * CH]
                    pool.wait_ge(h_set, j + 1)
                    pool.tensor_tensor(y, y, hn[:, :, :], ALU.add).then_inc(added, 1)
            for j, (s, d, ch) in enumerate(order):
                end = (CH - 1) * (1 - d)
                pool.wait_ge(exp_set, j + 1)
                if j >= 2:
                    pool.wait_ge(dc_ready, j - 1)
                for h in range(BH):
                    cp = pool.tensor_scalar(kw[:, j % 2, h], c.ktok[:, ch, h], expo[:, j % 2, h, end:end + 1], None, ALU.mult)
                    cp.then_inc(kw_set if h == BH - 1 else kw_part, 1)
                if j >= 1:
                    add(j - 1)
            add(N - 1)

        @block.sync
        def _(sp):
            for d in range(2):
                sp.wait_ge(cn_set, seen[(0, d)] + 1)
                sp.dma_start(io["new_c"][d].rearrange("h k v -> k h v"), c.cn[:, 0, 4 * d:4 * d + 4, 0:P]).then_inc(stored, 16)
                sp.wait_ge(n_set, d + 1)
                sp.dma_start(io["new_n"][d], c.n0[:, 4 * d:4 * d + 4]).then_inc(stored, 16)
                at = (PROMPT - 1) * (1 - d)
                sp.dma_start(io["new_m"][d].rearrange("(h o) -> h o", o=1), c.rows[32 * d:32 * d + 4, 3, at:at + 1]).then_inc(stored, 16)
            sp.wait_ge(stored, 6 * 16)


def phase_head_norm(c, name, src, center, per_slot, eps_value, gain):
    nc, io = c.nc, c.io
    rwkv = name == "ya"
    heads, size = 4 * per_slot, P // per_slot
    with ExitStack() as ctx:
        def sb(n, shape):
            return ctx.enter_context(nc.sbuf_tensor(f"{name}_{n}", shape, F32))

        def pb(n):
            return ctx.enter_context(nc.psum_tensor(f"{name}_{n}", [P, 2, 512], F32))
        sem = semaphores(nc, ctx, name + "_")
        other = sb("other", [P, 4, NT] if not rwkv else [P, NT + 4 * P])
        mean, spread = sb("mean", [P, 4, heads]), sb("spread", [heads, 4, P])
        root, eps = sb("root", [heads, NT]), sb("eps", [heads, 1])
        sq = sb("sq", [P, 2, 512])
        p_c, p_v, p_r = pb("pc"), pb("pv"), pb("pr")
        p_g = pb("pg") if rwkv else None
        loaded, made, centered, copied, squared, var_done, var_ready, std_set, inv_set, spread_ready = (sem(n) for n in (
            "loaded", "made", "centered", "copied", "squared", "var_done", "var_ready", "std_set", "inv_set", "spread_ready"))
        scaled, pooled, pooled2, done, stored = (sem(n) for n in ("scaled", "pooled", "pooled2", "done", "stored"))
        items = [(p, m, slice(first, first + width), width) for m, (first, width) in enumerate(BLOCKS) for p in range(4)]
        N = len(items)
        MADE = 2 + 2 * heads
        y = c.y[:, 0:4] if rwkv else src
        block = ctx.enter_context(nc.Block())

        @block.sync
        def _(sp):
            if rwkv:
                sp.dma_start(other[:, 0:NT], c.hid_g).then_inc(loaded, 16)
                sp.dma_start(other[:, NT:], io["w_g2"]).then_inc(loaded, 16)
                sp.dma_start(io["new_s"], c.s_out[:, :, :, :]).then_inc(stored, 16)
                sp.wait_ge(stored, 16)
            else:
                sp.dma_start(other[:, 0:2], c.sig[0:2].rearrange("h p t -> p h t")).then_inc(loaded, 16)
                sp.dma_start(other[:, 2:4], c.sig[2:4].rearrange("h p t -> p h t")).then_inc(loaded, 16)

        @block.tensor
        def _(pe):
            def center_item(n):
                p, m, cols, width = items[n]
                if n >= 2:
                    pe.wait_ge(copied, n - 1)
                pe.matmul(p_c[:, n % 2, 0:width], center, src[:, p, cols], start=True, stop=True).then_inc(centered, 1)

            def variance(n):
                p, m, cols, width = items[n]
                pe.wait_ge(squared, n + 1)
                if p == 0 and m >= 2:
                    pe.wait_ge(std_set, m - 1)
                pe.matmul(p_v[0:heads, m % 2, 0:width], mean[:, p, :], sq[:, n % 2, 0:width],
                          start=(p == 0), stop=(p == 3)).then_inc(var_ready if p == 3 else var_done, 1)

            def spread_item(n):
                p, m, cols, width = items[n]
                pe.wait_ge(inv_set, m + 1)
                if n >= 2:
                    pe.wait_ge(scaled, n - 1)
                    if rwkv:
                        pe.wait_ge(done, n - 1)
                mm = pe.matmul(p_r[:, n % 2, 0:width], spread[:, p, :], root[:, cols], start=True, stop=True)
                if rwkv:
                    mm = pe.matmul(p_g[:, n % 2, 0:width], other[:, NT + p * P:NT + (p + 1) * P], other[:, cols], start=True, stop=True)
                mm.then_inc(spread_ready, 1)
            pe.wait_ge(made, MADE)
            pe.wait_ge(loaded, 32)
            for n in range(N + 4):
                if n < N:
                    center_item(n)
                if 1 <= n <= N:
                    variance(n - 1)
                if n >= 4:
                    spread_item(n - 4)

        @block.scalar
        def _(act):
            act.wait_ge(made, 1)
            for n, (p, m, cols, width) in enumerate(items):
                act.wait_ge(copied, n + 1)
                if n >= 2:
                    act.wait_ge(var_done, n - 1 - (n - 1) // 4)
                    if n >= 5:
                        act.wait_ge(var_ready, (n - 1) // 4)
                act.activation(sq[:, n % 2, 0:width], src[:, p, cols], ACT.Square).then_inc(squared, 1)
                if p == 3:
                    act.wait_ge(var_ready, m + 1)
                    act.activation(root[:, cols], p_v[0:heads, m % 2, 0:width], ACT.Sqrt, bias=eps[:, 0:1]).then_inc(std_set, 1)


        @block.vector
        def _(dve):
            own = Own(dve, made)
            own.did(dve.memset(eps[:, :], eps_value))
            own.did(dve.memset(mean[:, :, :], 0.0))
            own.settle()
            for p in range(4):
                for e in range(per_slot):
                    h = per_slot * p + e
                    own.did(dve.memset(mean[size * e:size * e + size, p, h:h + 1], 1.0 / size))
                    own.did(dve.tensor_copy(spread[:, p, size * e:size * e + size], c.ident[0:heads, h:h + 1].to_broadcast([heads, size])))

            assert own.n == MADE

            def scale(n):
                p, m, cols, width = items[n]
                dve.wait_ge(spread_ready, n + 1)
                dve.wait_ge(squared, n + 1)
                if not rwkv:
                    dve.wait_ge(pooled, n + 1)
                dve.scalar_tensor_tensor(src[:, p, cols], src[:, p, cols], c.vec[:, VEC[gain] + p:VEC[gain] + p + 1], p_r[:, n % 2, 0:width],
                                         ALU.mult, ALU.mult).then_inc(scaled, 1)

            def gated(n):
                p, m, cols, width = items[n]
                dve.wait_ge(pooled2, n + 1)
                dve.tensor_tensor(y[:, p, cols], y[:, p, cols], p_g[:, n % 2, 0:width], ALU.mult).then_inc(done, 1)
            for n in range(N + 4):
                if n < N:
                    p, m, cols, width = items[n]
                    dve.wait_ge(centered, n + 1)
                    dve.tensor_copy(src[:, p, cols], p_c[:, n % 2, 0:width]).then_inc(copied, 1)
                if n >= 4:
                    p, m, cols, width = items[n - 4]
                    if p == 0:
                        dve.wait_ge(std_set, m + 1)
                        dve.reciprocal(root[:, cols], root[:, cols]).then_inc(inv_set, 1)
                    scale(n - 4)
                    if rwkv and n >= 5:
                        gated(n - 5)
            if rwkv:
                gated(N - 1)

        @block.gpsimd
        def _(pool):
            for n, (p, m, cols, width) in enumerate(items):
                if rwkv:
                    pool.tensor_scalar(y[:, p, cols], y[:, p, cols], c.vec[:, VEC["rwkv_ln_b"] + p:VEC["rwkv_ln_b"] + p + 1], None,
                                       ALU.add).then_inc(pooled, 1)
                else:
                    pool.wait_ge(loaded, 32)
                    pool.wait_ge(squared, n + 1)
                    pool.tensor_tensor(src[:, p, cols], src[:, p, cols], other[:, p, cols], ALU.mult).then_inc(pooled, 1)
                pool.wait_ge(pooled, n + 1)
            if rwkv:
                for n, (p, m, cols, width) in enumerate(items):
                    pool.wait_ge(scaled, n + 1)
                    pool.tensor_tensor(y[:, p, cols], y[:, p, cols], src[:, p, cols], ALU.add).then_inc(pooled2, 1)
                    pool.wait_ge(pooled2, n + 1)


def phase_c(c):
    nc = c.nc
    with ExitStack() as ctx:
        def sb(name, shape):
            return ctx.enter_context(nc.sbuf_tensor(name, shape, F32))
        c.center = sb("c_center", [P, P])
        with ExitStack() as inner:
            def sb(name, shape):
                return inner.enter_context(nc.sbuf_tensor(name, shape, F32))
            c.qt, c.kt = sb("c_qt", [P, BH, NT]), sb("c_kt", [P, BH, NT])
            c.ktok, c.vtok = sb("c_ktok", [P, NCH, BH, P]), sb("c_vtok", [P, NCH, BH, P])
            c.rows = sb("c_rows", [ROWS, 4, NT])
            c.betat = sb("c_betat", [P, NCH, ROWS])
            c.sel, c.cmask = sb("c_sel", [ROWS, 8, P]), sb("c_cmask", [P, 2, CH])
            c.cn = sb("c_cn", [P, 2, 8, 2 * P])
            c.m0, c.n0 = sb("c_m0", [ROWS, 1]), sb("c_n0", [P, 8])
            phase_c_prepare(c)
            phase_c_scan(c)
        phase_head_norm(c, "yb", c.y[:, 4:8], c.center[:, :], 1, 1e-5, "mlstm_ln_g")


RC = 64
RCH = NT // RC
HEADS_P = 4
DECAY_C = 0.6065306597126334


def phase_d_project(c):
    nc, io = c.nc, c.io
    jobs = [("r", 0, 0, 4), ("k", 2, 4, 4), ("v", 3, 8, 4), ("w", 1, 12, 1), ("i", 4, 13, 1), ("g", 5, 14, 1)]
    RING = 6
    with ExitStack() as ctx:
        def sb(name, shape):
            return ctx.enter_context(nc.sbuf_tensor(name, shape, F32))

        sem = semaphores(nc, ctx)
        w = sb("d_w", [P, 4, 15, P])
        mix = sb("d_mix", [P, RING, NT])
        stage = sb("d_stage", [P, 3, NT])
        ps = [ctx.enter_context(nc.psum_tensor(f"d_ps{i}", [P, 3, 512], F32)) for i in range(2)]
        w_in, shift_own, mixed, chunk_ready, used = (sem(f"d_{n}") for n in ("w_in", "shift_own", "mixed", "chunk_ready", "used"))
        staged, staged_part = sem("d_staged"), sem("d_staged_part")
        stored = [sem(f"d_stored{i}") for i in range(3)]
        loaded, proj_read, hid_set = sem("d_loaded"), sem("d_proj_read"), sem("d_hid_set")
        chunks = [(name, j, f, col + f) for j, (name, _, col, n) in enumerate(jobs) for f in range(n)]
        xx = c.y
        block = ctx.enter_context(nc.Block())

        @block.sync
        def _(sp):
            sp.dma_start(w[:, :, :, :], io["w_rwkv"]).then_inc(w_in, 16)
            sp.dma_start(c.w2[:, :, :], io["w_rank"]).then_inc(loaded, 16)
            sp.dma_start(c.s_in[:, :, :, :], io["s0"]).then_inc(loaded, 16)
            count = [0] * 3
            n = 0
            for name, j, f, col in chunks:
                if name in "rkvg":
                    dst = c.rkv[{"r": 0, "k": 1, "v": 2}[name], f] if name != "g" else c.hid_g
                    sp.wait_ge(staged, n + 1)
                    sp.wait_ge(staged_part, 2 * n + 2)
                    sp.dma_start(dst, stage[:, n % 3]).then_inc(stored[n % 3], 16)
                    count[n % 3] += 16
                    n += 1
            for i in range(3):
                sp.wait_ge(stored[i], count[i])
            sp.wait_ge(loaded, 32)

        @block.vector
        def _(dve):
            own = Own(dve, shift_own)
            for s, (first, width) in enumerate(STREAMS):
                at = xa_col(first)
                own.did(dve.tensor_tensor(xx[:, 0:4, first:first + width], c.xa[:, :, at - 1:at - 1 + width],
                                          c.xa[:, :, at + 1:at + 1 + width], ALU.add))
            own.settle()
            for s, (first, width) in enumerate(STREAMS):
                at = xa_col(first)
                for k in range(4):
                    own.did(dve.scalar_tensor_tensor(xx[:, k, first:first + width], xx[:, k, first:first + width], 0.5,
                                                     c.xa[:, k, at:at + width], ALU.mult, ALU.subtract))
            own.settle()
            for q in range(4 * len(jobs)):
                j, k = divmod(q, 4)
                if q >= RING:
                    dve.wait_ge(used, (q - RING) // 4 + 1)
                mu = VEC["rwkv_mu"] + 4 * jobs[j][1] + k
                for s, (first, width) in enumerate(STREAMS):
                    cp = dve.scalar_tensor_tensor(mix[:, q % RING, first:first + width], xx[:, k, first:first + width],
                                                  c.vec[:, mu:mu + 1], c.xa[:, k, xa_col(first):xa_col(first) + width],
                                                  ALU.mult, ALU.add)
                    if s == 0:
                        own.did(cp)
                own.settle()
                cp.then_inc(mixed, 1)

        @block.tensor
        def _(pe):
            pe.wait_ge(w_in, 16)
            for n, (name, j, f, col) in enumerate(chunks):
                pe.wait_ge(mixed, 4 * j + 4)
                if n >= 2:
                    pe.wait_ge(proj_read, n - 1)
                for m, (first, width) in enumerate(BLOCKS):
                    for k in range(4):
                        mm = pe.matmul(ps[n % 2][:, m, 0:width], w[:, k, col], mix[:, (4 * j + k) % RING, first:first + width],
                                       start=(k == 0), stop=(k == 3))
                mm.then_inc(chunk_ready, 1)
                if f == jobs[j][3] - 1:
                    pe.wait_ge(chunk_ready, n + 1)
                    pe.sem_inc(used, 1)

        @block.scalar
        def _(act):
            n_st = 0
            for n, (name, j, f, col) in enumerate(chunks):
                func = {"w": ACT.Tanh, "g": ACT.Sigmoid}.get(name, ACT.Copy)
                act.wait_ge(chunk_ready, n + 1)
                if name in "wi":
                    dst = c.hid[:, "wi".index(name)]
                else:
                    dst = stage[:, n_st % 3]
                    if n_st >= 3:
                        act.wait_ge(stored[n_st % 3], 16 * (n_st // 3))
                for m, (first, width) in enumerate(BLOCKS):
                    a = act.activation(dst[:, first:first + width], ps[n % 2][:, m, 0:width], func)
                    a.then_inc((hid_set if name in "wi" else (staged_part if m < 2 else staged)), 1)
                if name in "wi":
                    act.wait_ge(hid_set, 3 * ("wi".index(name) + 1))
                else:
                    n_st += 1
                    act.wait_ge(staged, n_st)
                act.sem_inc(proj_read, 1)


def phase_d_prepare(c, p):
    nc, io = c.nc, c.io
    with ExitStack() as ctx:
        def sb(name, shape):
            return ctx.enter_context(nc.sbuf_tensor(name, shape, F32))

        sem = semaphores(nc, ctx, f"p{p}_")
        rk = sb(f"p{p}_rk", [P, 2, NT])
        sg = c.y[:, p]
        kn = c.xa[:, p, 0:NT]
        cum, eneg, av, kd, kds = (sb(f"p{p}_{n}", [P, NT]) for n in ("cum", "eneg", "av", "kd", "kds"))
        ps = [ctx.enter_context(nc.psum_tensor(f"p{p}_ps{i}", [P, 3, 512], F32)) for i in range(2)]
        loaded, wide_ready, banks_act, banks_dve = sem("loaded"), sem("wide_ready"), sem("banks_act"), sem("banks_dve")
        sq_set, sg_set, av_set, eneg_set, epos_set, ex_set = (sem(n) for n in ("sq_set", "sg_set", "av_set", "eneg_set", "epos_set", "ex_set"))
        cum_set, sx_set, own_dve, r_done, a_done = (sem(n) for n in ("cum_set", "sx_set", "own_dve", "r_done", "a_done"))
        r_done_p, a_done_p, b_set, bb_done, bb_done_p, bonus_in = (sem(n) for n in ("r_done_p", "a_done_p", "b_set", "bb_done", "bb_done_p", "bonus_in"))
        kd_done, neg_b = sem("kd_done"), sem("neg_b")
        block = ctx.enter_context(nc.Block())
        wide = [("u", 0), ("ss", 0), ("a", 0), ("u", 1), ("a", 1), ("bonus", 0)]
        reader = [banks_act, banks_act, banks_act, banks_act, banks_act, banks_dve]

        def vec(name, k):
            return c.vec[:, VEC[name] + k:VEC[name] + k + 1]

        def per_chunk(t):
            return t.rearrange("p (n t) -> p n t", t=RC)

        @block.sync
        def _(sp):
            sp.dma_start(rk[:, :, :], c.rkv[0:2, p].rearrange("w p t -> p w t")).then_inc(loaded, 16)
            sp.dma_start(c.v[:, :], c.rkv[2, p]).then_inc(loaded, 16)

        @block.tensor
        def _(pe):
            for n, (kind, d) in enumerate(wide):
                if n >= 2:
                    pe.wait_ge(banks_act, 3 * (n - 1))
                if kind == "ss":
                    pe.wait_ge(sq_set, 1)
                if kind == "bonus":
                    pe.wait_ge(bonus_in, 1)
                for m, (first, width) in enumerate(BLOCKS):
                    cols = slice(first, first + width)
                    if kind in "ua":
                        which, half = "ua".index(kind), slice(64 * d, 64 * d + 64)
                        lhs, rhs = c.w2[half, which, p * P:(p + 1) * P], c.hid[half, which, cols]
                    else:
                        lhs, rhs = c.blockones[:, :], (eneg if kind == "ss" else kd)[:, cols]
                    mm = pe.matmul(ps[n % 2][:, m, 0:width], lhs, rhs, start=True, stop=True)
                mm.then_inc(wide_ready, 1)

        @block.scalar
        def _(act):
            def from_banks(n, out, func, done, **kw):
                act.wait_ge(wide_ready, n + 1)
                for m, (first, width) in enumerate(BLOCKS):
                    act.activation(out[:, first:first + width], ps[n % 2][:, m, 0:width], func, **kw).then_inc(banks_act, 1)
                act.wait_ge(banks_act, 3 * (n + 1))
                act.sem_inc(done, 1)
            act.wait_ge(loaded, 32)
            act.activation(eneg[:, :], rk[:, 1], ACT.Square, scale=vec("rwkv_k_k", p)).then_inc(sq_set, 1)
            from_banks(0, sg, ACT.Sigmoid, sg_set, bias=vec("rwkv_w0", p))
            from_banks(1, kn, ACT.Sqrt, sq_set)
            from_banks(2, av, ACT.Sigmoid, av_set, bias=vec("rwkv_a0", p))
            for d in range(2):
                if d == 1:
                    act.wait_ge(a_done, 1)
                    act.wait_ge(a_done_p, 1)
                    from_banks(3, sg, ACT.Sigmoid, sg_set, bias=vec("rwkv_w0", 4 + p))
                    act.wait_ge(neg_b, 1)
                    act.wait_ge(b_set, 2)
                    from_banks(4, av, ACT.Sigmoid, av_set, bias=vec("rwkv_a0", 4 + p))
                act.wait_ge(cum_set, 5 * (d + 1))
                if d == 0:
                    act.wait_ge(wide_ready, 2)
                else:
                    act.wait_ge(r_done, 2)
                    act.wait_ge(r_done_p, 1)
                act.activation(eneg[:, :], cum[:, :], ACT.Exp, scale=-DECAY_C).then_inc(eneg_set, 1)
                act.wait_ge(sx_set, d + 1)
                act.activation(sg, sg, ACT.Exp, scale=-DECAY_C).then_inc(ex_set, 1)
                act.wait_ge(eneg_set, d + 1)
                act.activation(cum[:, :], cum[:, :], ACT.Exp, scale=DECAY_C).then_inc(epos_set, 1)

        @block.vector
        def _(dve):
            own = Own(dve, own_dve)

            def normalize_key():
                dve.wait_ge(sq_set, 2)
                own.did(dve.tensor_scalar(kn[:, :], kn[:, :], 1e-12, None, ALU.max))
                own.settle()
                own.did(dve.reciprocal(kn[:, :], kn[:, :]))
                own.settle()
                own.did(dve.scalar_tensor_tensor(kn[:, :], rk[:, 1], vec("rwkv_k_k", p), kn[:, :], ALU.mult, ALU.mult))
                own.settle()
            for d in range(2):
                step = slice(None, None, 1 - 2 * d)
                dve.wait_ge(sg_set, d + 1)
                if d == 1:
                    dve.wait_ge(b_set, 2)
                for b in range(5):
                    cols = slice(256 * b, 256 * b + 256)
                    dve.tensor_tensor_scan(cum[:, cols][:, step], c.keep[:, :], sg[:, cols][:, step], 0.0,
                                           ALU.mult, ALU.add).then_inc(cum_set, 1)
                if d == 0:
                    normalize_key()
                dve.wait_ge(av_set, d + 1)
                kdd = kds if d == 0 else kd
                own.did(dve.tensor_scalar(kdd[:, :], av[:, :], vec("rwkv_k_a", p), c.one_less_ka[:, p:p + 1], ALU.mult, ALU.add))
                own.settle()
                own.did(dve.tensor_tensor(kdd[:, :], kdd[:, :], rk[:, 1], ALU.mult))
                dve.scalar_tensor_tensor(av[:, :], kn[:, :], -1.0, av[:, :], ALU.mult, ALU.mult).then_inc(neg_b, 1)
                own.settle()
                dve.wait_ge(eneg_set, d + 1)
                for first, width in STREAMS:
                    chunks = slice(first // RC, (first + width) // RC)
                    own.did(dve.tensor_copy(c.pend[:, chunks, d], per_chunk(eneg[:, :])[:, chunks][:, step, (RC - 1) * (1 - d)]))
                dve.tensor_tensor(c.ar[0:64, d, :, 1, 0, :], per_chunk(rk[0:64, 0]), per_chunk(eneg[0:64, :]), ALU.mult).then_inc(r_done, 1)
                own.settle()
                dve.sem_inc(r_done, 1)
                dve.wait_ge(ex_set, d + 1)
                dve.tensor_tensor(c.ar[0:64, d, :, 0, 0, :], per_chunk(kn[0:64, :]), per_chunk(sg[0:64]), ALU.mult).then_inc(a_done, 1)
                dve.wait_ge(epos_set, d + 1)
                dve.wait_ge(neg_b, d + 1)
                dve.tensor_tensor(c.kb[:, d, :, 1, :], per_chunk(av[:, :]), per_chunk(cum[:, :]), ALU.mult).then_inc(b_set, 1)
                dve.tensor_tensor(c.kb[:, d, :, 0, :], per_chunk(kdd[:, :]), per_chunk(cum[:, :]), ALU.mult).then_inc(b_set, 1)
                dve.wait_ge(b_set, 2 * d + 1)
                dve.tensor_copy(c.bb[0:64, d, :, 0, :], c.kb[0:64, d, :, 1, :]).then_inc(bb_done, 1)
            dve.wait_ge(b_set, 4)
            own.did(dve.tensor_tensor(kds[:, :], kds[:, :], kd[:, :], ALU.add))
            own.settle()
            dve.scalar_tensor_tensor(kd[:, :], rk[:, 0], vec("rwkv_r_k", p), kds[:, :], ALU.mult, ALU.mult).then_inc(bonus_in, 1)
            dve.wait_ge(wide_ready, 6)
            dve.wait_ge(a_done_p, 2)
            dve.wait_ge(a_done, 2)
            for m, (first, width) in enumerate(BLOCKS):
                own.did(dve.tensor_tensor(c.y[:, p, first:first + width], c.v[:, first:first + width], ps[1][:, m, 0:width], ALU.mult))
            own.settle()

        @block.gpsimd
        def _(pool):
            for d in range(2):
                if d == 1:
                    pool.wait_ge(bb_done_p, 1)
                pool.wait_ge(cum_set, 5 * (d + 1))
                pool.tensor_tensor(sg, cum[:, :], sg, ALU.subtract).then_inc(sx_set, 1)
                pool.wait_ge(sx_set, d + 1)
                pool.wait_ge(eneg_set, d + 1)
                pool.wait_ge(loaded, 32)
                pool.tensor_tensor(c.ar[64:128, d, :, 1, 1, :], per_chunk(rk[64:128, 0]), per_chunk(eneg[64:128, :]), ALU.mult).then_inc(r_done_p, 1)
                pool.wait_ge(r_done_p, d + 1)
                pool.wait_ge(ex_set, d + 1)
                if d == 0:
                    pool.wait_ge(neg_b, 1)
                pool.tensor_tensor(c.ar[64:128, d, :, 0, 1, :], per_chunk(kn[64:128, :]), per_chunk(sg[64:128]), ALU.mult).then_inc(a_done_p, 1)
                pool.wait_ge(a_done_p, d + 1)
                pool.wait_ge(b_set, 2 * d + 1)
                pool.tensor_copy(c.bb[64:128, d, :, 1, :], c.kb[64:128, d, :, 1, :]).then_inc(bb_done_p, 1)


def phase_d_scan(c, p):
    nc = c.nc
    np_, ns = PROMPT // RC, SAMPLE // RC
    steps = []
    for i in range(ns):
        steps.append((1, np_ + i, np_ + ns - 1 - i))
        if i < np_:
            steps.append((0, i, np_ - 1 - i))
    N = len(steps)
    ROUNDS = N // 2
    RING = 3
    before, last, seen, adds = [], {}, set(), []
    for i, (s, cf, cb) in enumerate(steps):
        before.append(last.get(s))
        last[s] = i
        adds.append(cf in seen)
        seen.update((cf, cb))
    LEVELS = 5

    def level_slot(l):
        return 0 if l == 0 else 1 + l % 2
    with ExitStack() as ctx:
        def sb(name, shape):
            return ctx.enter_context(nc.sbuf_tensor(f"q{p}_{name}", shape, F32))

        def pb(name, shape):
            return ctx.enter_context(nc.psum_tensor(f"q{p}_{name}", shape, F32))

        sem = semaphores(nc, ctx, f"q{p}_")
        gs = sb("gs", [P, RING, 2, 256])
        bd0 = sb("bd0", [P, 4, 2, P])
        bd = sb("bd", [P, 2, 4, P])
        st = sb("st", [P, 3, 4, 3, RC])
        tt = sb("tt", [P, 4, P])
        kbt = sb("kbt", [P, RING, 2, P])
        uv = sb("uv", [P, RING, 2, 2, RC])
        rs = sb("rs", [P, 2, RC])
        grown = c.s_out[:, p]
        p_gw, p_t, p_ru, p_yds = pb("pgw", [P, 512]), pb("pt", [P, 2, 2, P]), pb("pru", [P, 512]), pb("pyds", [P, 512])
        p_a = [pb(f"pa{h}", [P, 512]) for h in range(2)]
        p_nx = [pb(f"pnx{h}", [P, 512]) for h in range(2)]
        p_g = p_gw[:, :].rearrange("p (u t) -> p u t", u=2)
        p_w = p_gw[:, :].rearrange("p (u x s) -> p u x s", u=2, x=2)
        p_a = [t[:, 0:128].rearrange("p (u s) -> p u s", u=2) for t in p_a]
        p_nx = [t[:, 0:256].rearrange("p (u x s) -> p u x s", u=2, x=2) for t in p_nx]
        p_y, p_ds = (p_yds[:, first:first + 128].rearrange("p (u s) -> p u s", u=2) for first in (0, 128))
        p_r = p_ru[:, 0:128].rearrange("p (u v) -> p u v", u=2)
        p_u = p_ru[:, 256:512].rearrange("p (u e v) -> p u e v", u=2, e=2)
        g_ready, w_ready, t_ready, r_ready, u_ready, y_ready = (sem(n + "_ready") for n in ("g", "w", "t", "r", "u", "y"))
        g_set, w_set = sem("g_set"), sem("w_set")
        sq_ready, x_ready, st0_set, x0_set, grow_set, grow_part, a_set, n_set = ([sem(f"{n}{h}") for h in range(2)] for n in (
            "sq_ready", "x_ready", "st0_set", "x0_set", "grow_set", "grow_part", "a_set", "n_set"))
        t_set, r_set, u_set, state_set, y_set, own_dve, zeroed = (
            sem(n) for n in ("t_set", "r_set", "u_set", "state_set", "y_set", "own_dve", "zeroed"))
        block = ctx.enter_context(nc.Block())

        @block.tensor
        def _(pe):
            def masked_products(i):
                s, *ch = steps[i]
                if i >= 1:
                    pe.wait_ge(g_set, i)
                pe.wait_ge(w_set, min(N, 2 * (i // 2) + 2 + 2 * (i % 2)))
                for u in range(2):
                    mm = pe.matmul(p_g[:, u], c.kb[:, u, ch[u]], c.ar[:, u, ch[u]], start=True, stop=True)
                mm.then_inc(g_ready, 1)

            def system(i):
                s, *ch = steps[i]
                if i >= 1:
                    pe.wait_ge(w_set, i)
                if i >= 2:
                    pe.wait_ge(g_set, 2 * (i // 2) - 1)
                for u in range(2):
                    a, b = c.ar[:, u, ch[u], 0], c.bb[:, u, ch[u]]
                    pe.matmul(p_w[:, u, 0], a, b, start=True, stop=True)
                    mm = pe.matmul(p_w[:, u, 1], b, a, start=True, stop=True)
                mm.then_inc(w_ready, 1)

            def turn(i):
                s, *ch = steps[i]
                if i >= 1:
                    pe.wait_ge(t_set, 2 * i)
                for u in range(2):
                    pe.transpose(p_t[:, u, 0], c.kb[:, u, ch[u]], c.ident[:, :])
                    mm = pe.transpose(p_t[0:RC, u, 1], c.v[:, ch[u] * RC:(ch[u] + 1) * RC], c.ident[:, :])
                mm.then_inc(t_ready, 1)

            def square(i, l):
                j, h = divmod(i, 2)
                if l == 1:
                    pe.wait_ge(st0_set[h], 2 * (j + 1))
                    if j >= 1:
                        pe.wait_ge(a_set[h], 3 * LEVELS * j)
                        pe.wait_ge(grow_set[h], LEVELS * j)
                else:
                    pe.wait_ge(a_set[h], 3 * (LEVELS * j + l - 1))
                    pe.wait_ge(n_set[h], (LEVELS - 1) * j + l - 1)
                    if l == 2:
                        pe.wait_ge(x0_set[h], j + 1)
                    else:
                        pe.wait_ge(grow_set[h], LEVELS * j + l - 2)
                src = level_slot(l - 1)
                part = slice(1 if l == LEVELS else 0, 1 if l == 1 else 2)
                for u in range(2):
                    for e in range(2):
                        half = slice(64 * e, 64 * e + 64)
                        pe.matmul(p_a[h][half, u], st[half, src, 2 * h + u, 1], st[half, src, 2 * h + u, 0], start=True, stop=True)
                    power = bd0[:, 2 * h + u, 0] if l == 1 else bd[:, (l - 1) % 2, 2 * h + u]
                    mm = pe.matmul(p_nx[h][:, u, part], power, st[:, src, 2 * h + u, part.start + 1:part.stop + 1],
                                   start=True, stop=True)
                mm.then_inc(sq_ready[h], 1)

            def last_product(i):
                j, h = divmod(i, 2)
                pe.wait_ge(a_set[h], 3 * LEVELS * (j + 1))
                pe.wait_ge(grow_set[h], LEVELS * j + LEVELS - 1)
                src = level_slot(LEVELS)
                for u in range(2):
                    mm = pe.matmul(p_nx[h][:, u, 1], bd[:, LEVELS % 2, 2 * h + u], st[:, src, 2 * h + u, 2], start=True, stop=True)
                mm.then_inc(x_ready[h], 1)

            def right_side(i):
                s, *ch = steps[i]
                pe.wait_ge(g_set, i + 1)
                pe.wait_ge(t_set, 2 * (i + 1))
                if i >= 1:
                    pe.wait_ge(u_set, i)
                if before[i] is not None:
                    pe.wait_ge(state_set, before[i] + 1)
                for u in range(2):
                    for e in range(2):
                        pe.matmul(p_r[64 * e:64 * e + 64, u], gs[0:RC, i % RING, u, 64 * e:64 * e + 64], uv[0:RC, i % RING, u, e],
                                  start=True, stop=False, skip_group_check=True)
                    mm = pe.matmul(p_r[:, u], c.ar[:, u, ch[u], 0], c.s[:, s, u], start=False, stop=True, skip_group_check=True)
                mm.then_inc(r_ready, 1)

            def corrections(i):
                pe.wait_ge(r_set, i + 1)
                pe.wait_ge(grow_set[i % 2], LEVELS * (i // 2 + 1))
                for u in range(2):
                    for e in range(2):
                        mm = pe.matmul(p_u[64:128, u, e], tt[:, 2 * (i % 2) + u, 64 * e:64 * e + 64], rs[:, u], start=True, stop=True)
                mm.then_inc(u_ready, 1)

            def outputs(i):
                s, *ch = steps[i]
                pe.wait_ge(u_set, i + 1)
                if i >= 1:
                    pe.wait_ge(state_set, i)
                    pe.wait_ge(y_set, i)
                for u in range(2):
                    for e in range(2):
                        mm = pe.matmul(p_ds[64 * e:64 * e + 64, u], kbt[:, i % RING, u, 64 * e:64 * e + 64], uv[:, i % RING, u, e],
                                       start=True, stop=True)
                for u in range(2):
                    for e in range(2):
                        out = p_y[64 * e:64 * e + 64, u]
                        pe.matmul(out, uv[:, i % RING, u, e], gs[:, i % RING, u, 128 + 64 * e:128 + 64 * e + 64], start=True, stop=False)
                        mm = pe.matmul(out, c.s[:, s, u], c.ar[:, u, ch[u], 1, e, :], start=False, stop=True)
                mm.then_inc(y_ready, 1)
            pe.wait_ge(zeroed, 6)
            system(0)
            system(1)
            for j in range(ROUNDS + 1):
                now, ahead, back = j < ROUNDS, j + 1 < ROUNDS, j >= 1
                a, b = 2 * j, 2 * j + 1
                if now:
                    square(a, 1)
                if back:
                    right_side(a - 2)
                if now:
                    square(b, 1)
                    masked_products(a)
                    square(a, 2)
                if back:
                    corrections(a - 2)
                if now:
                    square(b, 2)
                    turn(a)
                    square(a, 3)
                if back:
                    outputs(a - 2)
                if now:
                    square(b, 3)
                if ahead:
                    system(a + 2)
                if now:
                    square(a, 4)
                if back:
                    right_side(b - 2)
                if now:
                    square(b, 4)
                if ahead:
                    system(b + 2)
                if now:
                    square(a, 5)
                if back:
                    corrections(b - 2)
                if now:
                    square(b, 5)
                    masked_products(b)
                    turn(b)
                    last_product(a)
                if back:
                    outputs(b - 2)
                if now:
                    last_product(b)

        @block.vector
        def _(dve):
            own = Own(dve, own_dve)
            for t in (bd[:, :, :, :], tt[:, :, :], c.s[:, 0], uv[:, :, :, :, :]):
                dve.memset(t, 0.0).then_inc(zeroed, 1)
            dve.tensor_copy(c.s[:, 1], c.s_in[:, p]).then_inc(zeroed, 1)
            dve.sem_inc(zeroed, 1)

            def masks(i):
                dve.wait_ge(w_ready, i + 1)
                dve.tensor_tensor(bd0[:, 2 * (i % 2):2 * (i % 2) + 2], p_w[:, :, :, :], c.mask_na[:, :, :, :], ALU.mult).then_inc(w_set, 1)

            def product_masks(i):
                dve.wait_ge(g_ready, i + 1)
                dve.tensor_tensor(gs[:, i % RING].rearrange("p u (x e t) -> p (u x) e t", x=2, e=2),
                                  p_g[:, :, :].rearrange("p u (x e t) -> p (u x) e t", x=2, e=2),
                                  c.mask_g[:, :, :].rearrange("p u (x t) -> p (u x) t", x=2).unsqueeze(2).to_broadcast([P, 4, 2, RC]),
                                  ALU.mult).then_inc(g_set, 1)

            def first_x(i):
                j, h = divmod(i, 2)
                dve.wait_ge(st0_set[h], 2 * (j + 1))
                if j >= 1:
                    dve.wait_ge(grow_set[h], LEVELS * j)
                mats = slice(2 * h, 2 * h + 2)
                dve.tensor_tensor(st[:, level_slot(1), mats, 2], st[:, 0, mats, 1], c.istack[:, :].unsqueeze(1).to_broadcast([P, 2, RC]),
                                  ALU.add).then_inc(x0_set[h], 1)

            def level(i, l):
                j, h = divmod(i, 2)
                dve.wait_ge(sq_ready[h], LEVELS * j + l)
                mats = slice(2 * h, 2 * h + 2)
                dve.tensor_copy(st[:, level_slot(l), mats, 1], p_nx[h][:, :, 0]).then_inc(n_set[h], 1)

            def grow(i, k):
                j, h = divmod(i, 2)
                mats = slice(2 * h, 2 * h + 2)
                dve.wait_ge(sq_ready[h], LEVELS * j + k + 1)
                if k == 1:
                    dve.wait_ge(x0_set[h], j + 1)
                else:
                    dve.wait_ge(grow_set[h], LEVELS * j + k - 1)
                dve.tensor_tensor(st[:, level_slot(k + 1), mats, 2], st[:, level_slot(k), mats, 2], p_nx[h][:, :, 1], ALU.add).then_inc(grow_set[h], 1)

            def grow_last(i):
                j, h = divmod(i, 2)
                dve.wait_ge(x_ready[h], j + 1)
                dve.wait_ge(grow_set[h], LEVELS * j + LEVELS - 1)
                if j >= 1:
                    dve.wait_ge(u_ready, i - 1)
                mats = slice(2 * h, 2 * h + 2)
                for e in range(2):
                    half = slice(64 * e, 64 * e + 64)
                    cp = dve.tensor_tensor(tt[half, mats, half], st[half, level_slot(LEVELS), mats, 2], p_nx[h][half, :, 1], ALU.add)
                    cp.then_inc(grow_set[h] if e else grow_part[h], 1)

            def carry(i):
                s, cf, cb = steps[i]
                dve.wait_ge(y_ready, i + 1)
                own.did(dve.tensor_tensor(grown, p_ds, c.s[:, s], ALU.add))
                own.settle()
                dve.tensor_tensor(c.s[:, s], grown, c.pend[:, cf, :].unsqueeze(2).to_broadcast([P, 2, RC]), ALU.mult).then_inc(state_set, 1)
                chunks_ = c.xa[:, p, 0:NT].rearrange("p (n t) -> p n t", t=RC)
                end = cb + (1 if cb > cf else -1)
                dst = chunks_[:, cf:(None if end < 0 else end):cb - cf]
                if adds[i]:
                    dve.tensor_tensor(dst, dst, p_y, ALU.add).then_inc(y_set, 1)
                else:
                    dve.tensor_copy(dst, p_y).then_inc(y_set, 1)
                dve.wait_ge(state_set, i + 1)
            masks(0)
            masks(1)
            for j in range(ROUNDS + 1):
                now, ahead, back = j < ROUNDS, j + 1 < ROUNDS, j >= 1
                a, b = 2 * j, 2 * j + 1
                if now:
                    first_x(a)
                    level(a, 1)
                    first_x(b)
                    level(b, 1)
                    product_masks(a)
                    level(a, 2)
                    grow(a, 1)
                    level(b, 2)
                    grow(b, 1)
                    level(a, 3)
                    grow(a, 2)
                if back:
                    carry(a - 2)
                if now:
                    level(b, 3)
                    grow(b, 2)
                if ahead:
                    masks(a + 2)
                if now:
                    level(a, 4)
                    grow(a, 3)
                    level(b, 4)
                    grow(b, 3)
                if ahead:
                    masks(b + 2)
                if now:
                    grow(a, 4)
                    grow(b, 4)
                    product_masks(b)
                    grow_last(a)
                if back:
                    carry(b - 2)
                if now:
                    grow_last(b)
            dve.tensor_copy(c.s_out[:, p], c.s[:, 0]).then_inc(zeroed, 1)

        @block.scalar
        def _(act):
            def level(i, l):
                j, h = divmod(i, 2)
                act.wait_ge(sq_ready[h], LEVELS * j + l)
                if l == 1 and j >= 1:
                    act.wait_ge(x_ready[h], j)
                mats = slice(2 * h, 2 * h + 2)
                for e in range(2):
                    half = slice(64 * e, 64 * e + 64)
                    act.activation(bd[half, l % 2, mats, half], p_a[h][half], ACT.Copy).then_inc(a_set[h], 1)
                act.activation(st[:, level_slot(l), mats, 0], p_a[h], ACT.Copy).then_inc(a_set[h], 1)

            def turned(i):
                act.wait_ge(t_ready, i + 1)
                if i >= RING:
                    act.wait_ge(y_ready, i - RING + 1)
                act.activation(kbt[:, i % RING], p_t[:, :, 0], ACT.Copy).then_inc(t_set, 1)
                act.activation(uv[0:RC, i % RING].rearrange("p u e v -> p u (e v)"), p_t[0:RC, :, 1], ACT.Copy).then_inc(t_set, 1)

            def right(i):
                act.wait_ge(r_ready, i + 1)
                act.activation(rs[:, :, :], p_r, ACT.Copy).then_inc(r_set, 1)

            def corrected(i):
                act.wait_ge(u_ready, i + 1)
                act.activation(uv[64:128, i % RING], p_u[64:128], ACT.Copy).then_inc(u_set, 1)
            act.wait_ge(zeroed, 6)
            for j in range(ROUNDS + 1):
                now, back = j < ROUNDS, j >= 1
                a, b = 2 * j, 2 * j + 1
                if now:
                    level(a, 1)
                if back:
                    right(a - 2)
                if now:
                    level(b, 1)
                    level(a, 2)
                if back:
                    corrected(a - 2)
                if now:
                    level(b, 2)
                    turned(a)
                    level(a, 3)
                    level(b, 3)
                    level(a, 4)
                if back:
                    right(b - 2)
                if now:
                    level(b, 4)
                    level(a, 5)
                if back:
                    corrected(b - 2)
                if now:
                    level(b, 5)
                    turned(b)

        @block.gpsimd
        def _(pool):
            for i in range(N):
                j, h = divmod(i, 2)
                mats = slice(2 * h, 2 * h + 2)
                pool.wait_ge(w_set, i + 1)
                if j >= 1:
                    pool.wait_ge(x0_set[h], j)
                    pool.wait_ge(sq_ready[h], LEVELS * (j - 1) + 1)
                for e in range(2):
                    half = slice(64 * e, 64 * e + 64)
                    pool.tensor_copy(st[half, 0, mats, 0:2], bd0[half, mats, :, half]).then_inc(st0_set[h], 1)
                    pool.wait_ge(st0_set[h], 2 * j + e + 1)


def phase_d_constants(c):
    nc = c.nc
    with ExitStack() as ctx:
        sem = semaphores(nc, ctx, "k_")
        zero, made, sel, own_dve = (sem(n) for n in ("zero", "made", "sel", "own_dve"))
        block = ctx.enter_context(nc.Block())

        @block.vector
        def _(dve):
            own = Own(dve, own_dve)
            own.did(dve.memset(c.ar[:, :, :, :, :, :], 0.0))
            own.did(dve.memset(c.bb[:, :, :, :, :], 0.0))
            own.did(dve.memset(c.keep[:, :], 1.0))
            own.did(dve.memset(c.blockones[:, :], 0.0))
            own.settle()
            own.did(dve.memset(c.keep[:, :].rearrange("p (n t) -> p n t", t=RC)[:, :, 0:1], 0.0))
            for e in range(2):
                half = slice(64 * e, 64 * e + 64)
                own.did(dve.memset(c.blockones[half, half], 1.0))
                own.did(dve.tensor_copy(c.istack[half, :], c.ident[half, half]))
            ka = VEC["rwkv_k_a"]
            own.did(dve.tensor_scalar(c.one_less_ka[:, :], c.vec[:, ka:ka + 4], -1.0, 1.0, ALU.mult, ALU.add))
            own.settle()
            own.did(dve.scalar_tensor_tensor(c.center64[:, :], c.blockones[:, :], -1.0 / 64, c.ident[:, :], ALU.mult, ALU.add))
            own.settle()

        @block.gpsimd
        def _(pool):
            pool.memset(c.mask_na[:, :, :, :], 1.0).then_inc(zero, 1)
            pool.memset(c.mask_g[:, :, :], 1.0).then_inc(zero, 1)
            pool.wait_ge(zero, 2)
            n = 0
            for u in range(2):
                sgn = 1 - 2 * u
                for x in range(2):
                    rows_after = sgn * (1 - 2 * x)
                    for e in range(2):
                        v = c.mask_na[:, u, x, 64 * e:64 * e + 64]
                        pool.affine_select(out=v, in_=v, compare_op=ALU.is_gt, fill=0.0, base=-64 * e * rows_after,
                                           pattern=[[-rows_after, 64]], channel_multiplier=rows_after).then_inc(made, 1)
                        n += 1
                        pool.wait_ge(made, n)
                for half in range(2):
                    for x, cmp in ((0, ALU.is_gt), (1, ALU.is_ge)):
                        v = c.mask_g[64 * half:64 * half + 64, u, 64 * x:64 * x + 64]
                        pool.affine_select(out=v, in_=v, compare_op=cmp, fill=0.0, base=0, pattern=[[sgn, 64]],
                                           channel_multiplier=-sgn).then_inc(made, 1)
                        n += 1
                        pool.wait_ge(made, n)
            for e in range(2):
                v = c.mask_na[64 * e:64 * e + 64, :, :, 64 * (1 - e):64 * (1 - e) + 64]
                pool.memset(v, 0.0).then_inc(sel, 1)
                pool.wait_ge(sel, e + 1)


def phase_d(c):
    nc = c.nc
    with ExitStack() as ctx:
        def sb(name, shape):
            return ctx.enter_context(nc.sbuf_tensor(name, shape, F32))
        c.hid = sb("d_hid", [P, 2, NT])
        c.w2 = sb("d_w2", [P, 2, 4 * P])
        c.s_in, c.s_out = sb("d_s_in", [P, HEADS_P, 2, RC]), sb("d_s_out", [P, HEADS_P, 2, RC])
        c.keep, c.pend = sb("d_keep", [P, 256]), sb("d_pend", [P, RCH, 2])
        c.blockones, c.center64 = sb("d_blockones", [P, P]), sb("d_center64", [P, P])
        c.istack, c.one_less_ka = sb("d_istack", [P, RC]), sb("d_one_less_ka", [P, 4])
        c.mask_na, c.mask_g = sb("d_mask_na", [P, 2, 2, P]), sb("d_mask_g", [P, 2, P])
        c.s = sb("d_s", [P, 2, 2, RC])
        phase_d_project(c)
        with ExitStack() as inner:
            def sb(name, shape):
                return inner.enter_context(nc.sbuf_tensor(name, shape, F32))
            c.ar = sb("d_ar", [P, 2, RCH, 2, 2, RC])
            c.kb = sb("d_kb", [P, 2, RCH, 2, RC])
            c.bb = sb("d_bb", [P, 2, RCH, 2, RC])
            c.v = sb("d_v", [P, NT])
            phase_d_constants(c)
            for p in range(HEADS_P):
                phase_d_prepare(c, p)
                phase_d_scan(c, p)
        phase_head_norm(c, "ya", c.xa[:, :, 0:NT], c.center64[:, :], 2, 64e-5, "rwkv_ln_g")


NEXP, GROUPS, PER_GROUP = 16, 4, 4
DEXP = 256
SLOT_TILES = (2 * NT + NEXP * (P - 1)) // P
REPS = [("gate1", 16), ("shift2", 24), ("gain2", None), ("gate2", 40)]


def phase_e_merge(c, merged):
    nc, io = c.nc, c.io
    with ExitStack() as ctx:
        def sb(name, shape):
            return ctx.enter_context(nc.sbuf_tensor(name, shape, F32))
        sem = semaphores(nc, ctx, "e_")
        wp = sb("e_wp", [P, 2, 4, D])
        sig = sb("e_sig", [P, 2, 2, 512])
        tmp = sb("e_tmp", [P, 2, 512])
        diag = sb("e_diag", [P, 2, 4, P])
        pp = ctx.enter_context(nc.psum_tensor("e_pp", [P, 2, 2, 512], F32))
        pr = ctx.enter_context(nc.psum_tensor("e_pr", [P, 2, 512], F32))
        w_in, sig_in, diag_set, rep_ready, rep_set = (sem(n) for n in ("w_in", "sig_in", "diag_set", "rep_ready", "rep_set"))
        sig_slot = [sem("sig_in0"), sem("sig_in1")]
        ready, scaled_a, scaled_b, added = (sem(n) for n in ("ready", "scaled_a", "scaled_b", "added"))
        items = [(f, m) for f in range(KD) for m in range(3)]
        reps = [(r, s, half) for r in range(4) for s in range(2) for half in range(2)]
        block = ctx.enter_context(nc.Block())

        @block.sync
        def _(sp):
            for x in range(2):
                sp.dma_start(wp[:, x], io["w_branch"][x]).then_inc(w_in, 16)
            for n, (f, m) in enumerate(items):
                first, width = BLOCKS[m]
                if n >= 2:
                    sp.wait_ge(scaled_b, n - 1)
                for x in range(2):
                    sp.dma_start(sig[:, n % 2, x, 0:width], c.sig[4 + 8 * x + f, :, first:first + width]).then_inc(sig_slot[n % 2], 16)

        @block.tensor
        def _(pe):
            for n in range(len(reps)):
                pe.wait_ge(diag_set, n + 1)
                if n >= 2:
                    pe.wait_ge(rep_set, n - 1)
                pe.matmul(pr[:, n % 2], c.ones[:, :], diag[:, n % 2], start=True, stop=True).then_inc(rep_ready, 1)
            pe.wait_ge(w_in, 32)
            for n, (f, m) in enumerate(items):
                first, width = BLOCKS[m]
                if n >= 2:
                    pe.wait_ge(scaled_b, n - 1)
                for x in range(2):
                    for k in range(4):
                        mm = pe.matmul(pp[:, n % 2, x, 0:width], wp[:, x, k, f * P:(f + 1) * P], c.y[:, 4 * x + k, first:first + width],
                                       start=(k == 0), stop=(k == 3))
                mm.then_inc(ready, 1)

        @block.vector
        def _(dve):
            for n, (r, s, half) in enumerate(reps):
                at = REPS[r][1]
                src = c.gain[:, 1, 4 * half:4 * half + 4, s] if at is None else c.mod[:, at + 4 * half:at + 4 * half + 4, s]
                if n >= 2:
                    dve.wait_ge(rep_ready, n - 1)
                dve.tensor_tensor(diag[:, n % 2], c.ident[:, :].unsqueeze(1).to_broadcast([P, 4, P]),
                                  src.unsqueeze(2).to_broadcast([P, 4, P]), ALU.mult).then_inc(diag_set, 1)
            for n, (f, m) in enumerate(items):
                first, width = BLOCKS[m]
                out = merged[:, f, first:first + width]
                dve.wait_ge(ready, n + 1)
                dve.wait_ge(sig_slot[n % 2], 32 * (n // 2 + 1))
                if n >= 2:
                    dve.wait_ge(added, n - 1)
                dve.tensor_tensor(tmp[:, n % 2, 0:width], sig[:, n % 2, 0, 0:width], pp[:, n % 2, 0, 0:width], ALU.mult).then_inc(scaled_a, 1)
                dve.wait_ge(scaled_a, n + 1)
                dve.tensor_tensor(out, sig[:, n % 2, 1, 0:width], pp[:, n % 2, 1, 0:width], ALU.mult).then_inc(scaled_b, 1)

        @block.gpsimd
        def _(pool):
            for n, (f, m) in enumerate(items):
                first, width = BLOCKS[m]
                out = merged[:, f, first:first + width]
                pool.wait_ge(scaled_b, n + 1)
                pool.tensor_tensor(out, out, tmp[:, n % 2, 0:width], ALU.add).then_inc(added, 1)
                pool.wait_ge(added, n + 1)

        @block.scalar
        def _(act):
            for n, (r, s, half) in enumerate(reps):
                dst = c.gate2 if r == 3 else c.rep[:, r]
                act.wait_ge(rep_ready, n + 1)
                act.activation(dst[:, s, 512 * half:512 * half + 512], pr[:, n % 2], ACT.Copy).then_inc(rep_set, 1)


def phase_e_rows(c, merged):
    nc, io = c.nc, c.io
    with ExitStack() as ctx:
        def sb(name, shape):
            return ctx.enter_context(nc.sbuf_tensor(name, shape, F32))
        sem = semaphores(nc, ctx, "o_")
        wo = sb("o_wo", [P, KD, D])
        wr = sb("o_wr", [P, KD, 20])
        br = sb("o_br", [P, 20])
        x = sb("o_x", [P, 2, D])
        h2 = sb("o_h2", [P, 2, D])
        ht = sb("o_ht", [P, 2, KD, P])
        stat = sb("o_stat", [P, 4, TILES])
        po = ctx.enter_context(nc.psum_tensor("o_po", [P, 2, 512], F32))
        pt = ctx.enter_context(nc.psum_tensor("o_pt", [P, 2, 4, P], F32))
        pl = ctx.enter_context(nc.psum_tensor("o_pl", [P, 2, 512], F32))
        w_in, projected, scaled, x2_set, squared, var_set, std_set, own_dve, h2_set = (sem(n) for n in (
            "w_in", "projected", "scaled", "x2_set", "squared", "var_set", "std_set", "own_dve", "h2_set"))
        x_in, h2_stored = [sem("x_in0"), sem("x_in1")], [sem("h2_stored0"), sem("h2_stored1")]
        turned, ht_set, logit_ready, logit_set = (sem(n) for n in ("turned", "ht_set", "logit_ready", "logit_set"))
        block = ctx.enter_context(nc.Block())

        def store(sp, t):
            sp.wait_ge(h2_set, t + 1)
            sp.dma_start(c.h2[t * P:(t + 1) * P, :], h2[:, t % 2]).then_inc(h2_stored[t % 2], 16)

        def logit(dve, t):
            dve.wait_ge(logit_ready, t + 1)
            dve.tensor_tensor(c.logits[:, t], br[:, :], pl[:, t % 2, 0:20], ALU.add).then_inc(logit_set, 1)

        @block.sync
        def _(sp):
            sp.dma_start(wo[:, :, :], io["w_out"]).then_inc(w_in, 16)
            sp.dma_start(wr[:, :, :], io["w_router"]).then_inc(w_in, 16)
            sp.dma_start(br[:, :], io["b_router"].partition_broadcast(P)).then_inc(w_in, 16)
            for t in range(TILES):
                if t >= 2:
                    sp.wait_ge(x2_set, 2 * t - 2)
                sp.dma_start(x[:, t % 2], io["x"][t * P:(t + 1) * P, :]).then_inc(x_in[t % 2], 16)
                if t >= 1:
                    store(sp, t - 1)
            store(sp, TILES - 1)
            for i in range(2):
                sp.wait_ge(h2_stored[i], 16 * TILES // 2)

        @block.tensor
        def _(pe):
            def project(t):
                for half in range(2):
                    n = 2 * t + half
                    if n >= 2:
                        pe.wait_ge(scaled, n - 1)
                    for k in range(KD):
                        mm = pe.matmul(po[:, n % 2], merged[:, k, t * P:(t + 1) * P], wo[:, k, 512 * half:512 * half + 512],
                                       start=(k == 0), stop=(k == KD - 1))
                    mm.then_inc(projected, 1)

            def turn(t):
                pe.wait_ge(h2_set, t + 1)
                for half in range(2):
                    n = 2 * t + half
                    if n >= 2:
                        pe.wait_ge(ht_set, n - 1)
                    for j in range(4):
                        k = 4 * half + j
                        mm = pe.transpose(pt[:, half, j], h2[:, t % 2, k * P:(k + 1) * P], c.ident[:, :])
                    mm.then_inc(turned, 1)

            def logits(t):
                pe.wait_ge(ht_set, 2 * t + 2)
                if t >= 2:
                    pe.wait_ge(logit_set, t - 1)
                for k in range(KD):
                    mm = pe.matmul(pl[:, t % 2, 0:20], ht[:, t % 2, k], wr[:, k], start=(k == 0), stop=(k == KD - 1))
                mm.then_inc(logit_ready, 1)
            pe.wait_ge(w_in, 48)
            for t in range(TILES + 2):
                if t < TILES:
                    project(t)
                if 1 <= t < TILES + 1:
                    turn(t - 1)
                if t >= 2:
                    logits(t - 2)

        @block.vector
        def _(dve):
            own = Own(dve, own_dve)
            for t in range(TILES):
                s = 0 if t < PROMPT // P else 1
                x2 = c.x2[:, t]
                for half in range(2):
                    n = 2 * t + half
                    cols = slice(512 * half, 512 * half + 512)
                    dve.wait_ge(projected, n + 1)
                    dve.tensor_tensor(x2[:, cols], c.rep[:, 0, s, cols], po[:, n % 2], ALU.mult).then_inc(scaled, 1)
                dve.wait_ge(x_in[t % 2], 16 * (t // 2 + 1))
                for half in range(2):
                    cols = slice(512 * half, 512 * half + 512)
                    dve.wait_ge(scaled, 2 * t + half + 1)
                    dve.tensor_tensor(x2[:, cols], x2[:, cols], x[:, t % 2, cols], ALU.add).then_inc(x2_set, 1)
                dve.wait_ge(squared, t + 1)
                dve.tensor_scalar(stat[:, 1, t:t + 1], stat[:, 0, t:t + 1], 1.0 / D, NORM_EPS, ALU.mult, ALU.add).then_inc(var_set, 1)
                dve.wait_ge(std_set, t + 1)
                own.did(dve.reciprocal(stat[:, 3, t:t + 1], stat[:, 2, t:t + 1]))
                own.settle()
                if t >= 2:
                    dve.wait_ge(h2_stored[t % 2], 16 * (t // 2))
                    dve.wait_ge(turned, 2 * (t - 1))
                own.did(dve.scalar_tensor_tensor(h2[:, t % 2], x2, stat[:, 3, t:t + 1],
                                                 c.rep[:, 2, s], ALU.mult, ALU.mult))
                own.settle()
                dve.tensor_tensor(h2[:, t % 2], h2[:, t % 2], c.rep[:, 1, s], ALU.add).then_inc(h2_set, 1)
                if t >= 2:
                    logit(dve, t - 2)
            for t in range(TILES - 2, TILES):
                logit(dve, t)

        @block.scalar
        def _(act):
            def turn(t):
                for half in range(2):
                    act.wait_ge(turned, 2 * t + half + 1)
                    if t >= 2 and half == 0:
                        act.wait_ge(logit_ready, t - 1)
                    act.activation(ht[:, t % 2, 4 * half:4 * half + 4], pt[:, half], ACT.Copy).then_inc(ht_set, 1)
            for t in range(TILES):
                act.wait_ge(x2_set, 2 * t + 2)
                if t >= 1:
                    act.wait_ge(squared, t)
                act.activation(c.junk[:, :], c.x2[:, t], ACT.Square, accum_out=stat[:, 0, t:t + 1]).then_inc(squared, 1)
                act.wait_ge(var_set, t + 1)
                act.activation(stat[:, 2, t:t + 1], stat[:, 1, t:t + 1], ACT.Sqrt).then_inc(std_set, 1)
                if t >= 1:
                    turn(t - 1)
            turn(TILES - 1)


def phase_e_route(c):
    nc, io = c.nc, c.io
    I32 = mybir.dt.int32
    with ExitStack() as ctx:
        def sb(name, shape, dt=F32):
            return ctx.enter_context(nc.sbuf_tensor(name, shape, dt))
        sem = semaphores(nc, ctx, "r_")
        T = TILES
        prio, expert_prio = sb("r_prio", [P, 4]), None
        triu = sb("r_triu", [P, P])
        thr, tile_no, token = sb("r_thr", [P, 10]), sb("r_tile_no", [P, SLOT_TILES]), sb("r_token", [P, T])
        one16 = sb("r_one16", [P, NEXP])
        m, t4, oh, oh1, oh2, es = (sb(f"r_{n}", [P, T, 4]) for n in ("m", "t4", "oh", "oh1", "oh2", "es"))
        t16 = sb("r_t16", [P, T, 4, 4])
        gmax, gsum, m1, m2, den, s1 = (sb(f"r_{n}", [P, T]) for n in ("gmax", "gsum", "m1", "m2", "den", "s1"))
        pick = sb("r_pick", [P, 2, T, NEXP])
        both, pos, base = sb("r_both", [P, T, NEXP]), sb("r_pos", [P, T, NEXP]), sb("r_base", [P, T + 1, NEXP])
        cmp10, ntiles, ends, starts = sb("r_cmp10", [P, NEXP, 10]), sb("r_ntiles", [P, NEXP]), sb("r_ends", [P, NEXP]), sb("r_starts", [P, NEXP])
        cmp35, owner = sb("r_cmp35", [P, SLOT_TILES, NEXP]), sb("r_owner", [P, SLOT_TILES])
        slotf = sb("r_slotf", [P, 2, T])
        zrow = sb("r_zrow", [SLOT_TILES, P])
        listed = sb("r_listed", [SLOT_TILES, P])
        pc = ctx.enter_context(nc.psum_tensor("r_pc", [P, 2, 512], F32))
        pl = ctx.enter_context(nc.psum_tensor("r_pl", [P, 512], F32))
        own_dve, made, made2, exp_in, exp_set, both_set, counted, slot_set, owner_set = (sem(n) for n in (
            "own_dve", "made", "made2", "exp_in", "exp_set", "both_set", "counted", "slot_set", "owner_set"))
        zero_stored, scattered, list_in, list_turned, fg_in = (sem(n) for n in ("zero_stored", "scattered", "list_in", "list_turned", "fg_in"))
        block = ctx.enter_context(nc.Block())

        @block.gpsimd
        def _(pool):
            n = 0

            def step(ins):
                nonlocal n
                ins.then_inc(made, 1)
                n += 1
                pool.wait_ge(made, n)
            step(pool.memset(zrow[:, :], 0.0))
            pool.dma_start(c.slot_list.rearrange("(q p) o -> q (p o)", p=P), zrow[:, :]).then_inc(zero_stored, 16)
            step(pool.memset(triu[:, :], 1.0))
            step(pool.affine_select(out=triu[:, :], in_=triu[:, :], compare_op=ALU.is_gt, fill=0.0, base=0,
                                    pattern=[[1, P]], channel_multiplier=-1))
            step(pool.iota(prio[:, :], pattern=[[-1, 4]], base=4, channel_multiplier=0, allow_small_or_imprecise_dtypes=True))
            step(pool.iota(thr[:, :], pattern=[[P, 10]], base=0, channel_multiplier=0, allow_small_or_imprecise_dtypes=True))
            step(pool.iota(tile_no[:, :], pattern=[[1, SLOT_TILES]], base=0, channel_multiplier=0, allow_small_or_imprecise_dtypes=True))
            step(pool.iota(token[:, :], pattern=[[P, T]], base=0, channel_multiplier=1, allow_small_or_imprecise_dtypes=True))
            step(pool.memset(one16[:, :], 1.0))
            pool.sem_inc(made2, 1)
            pool.wait_ge(zero_stored, 16)
            pool.wait_ge(slot_set, 1)
            for k in range(2):
                for t in range(T):
                    pool.indirect_dma_start(c.slot_list, bass.IndirectOffsetOnAxis(ap=c.slot[:, k, t:t + 1], axis=0),
                                            token[:, t:t + 1], None).then_inc(scattered, 16)
            pool.wait_ge(scattered, 2 * T * 16)
            pool.dma_start(listed[:, :], c.slot_list.rearrange("(q p) o -> q (p o)", p=P)).then_inc(list_in, 16)

        @block.sync
        def _(sp):
            sp.dma_start(c.fgain[:, :], io["final_g"].partition_broadcast(P)).then_inc(fg_in, 16)
            sp.wait_ge(fg_in, 16)

        @block.vector
        def _(dve):
            own = Own(dve, own_dve)

            def do(ins):
                own.did(ins)
                own.settle()

            def bc(ap, n):
                return ap.unsqueeze(2).to_broadcast([P, T, n])

            def first_best(out, values, best):
                do(dve.tensor_tensor(out, values, bc(best, 4), ALU.is_equal))
                do(dve.tensor_tensor(out, out, prio[:, :].unsqueeze(1).to_broadcast([P, T, 4]), ALU.mult))
                do(dve.tensor_reduce(s1[:, :], out, AX.X, ALU.max))
                do(dve.tensor_tensor(out, out, bc(s1[:, :], 4), ALU.is_equal))
            g = c.logits[:, :, 0:4]
            e = c.logits[:, :, 4:20].rearrange("p t (g e) -> p t g e", g=4)
            dve.wait_ge(made2, 1)
            do(dve.tensor_reduce(gmax[:, :], g, AX.X, ALU.max))
            do(dve.tensor_tensor(t4[:, :, :], g, bc(gmax[:, :], 4), ALU.subtract))
            dve.sem_inc(exp_in, 1)
            first_best(oh[:, :, :], g, gmax[:, :])
            do(dve.tensor_tensor(t16[:, :, :, :], e, oh[:, :, :].unsqueeze(3).to_broadcast([P, T, 4, 4]), ALU.mult))
            do(dve.tensor_reduce(es[:, :, :], t16[:, :, :, :].rearrange("p t g e -> p t e g"), AX.X, ALU.add))
            do(dve.tensor_reduce(m1[:, :], es[:, :, :], AX.X, ALU.max))
            first_best(oh1[:, :, :], es[:, :, :], m1[:, :])
            do(dve.scalar_tensor_tensor(es[:, :, :], oh1[:, :, :], -3e38, es[:, :, :], ALU.mult, ALU.add))
            do(dve.tensor_reduce(m2[:, :], es[:, :, :], AX.X, ALU.max))
            first_best(oh2[:, :, :], es[:, :, :], m2[:, :])
            do(dve.tensor_tensor(m2[:, :], m2[:, :], m1[:, :], ALU.subtract))
            dve.sem_inc(exp_in, 1)
            for k, o in enumerate((oh1, oh2)):
                do(dve.tensor_tensor(pick[:, k].rearrange("p t (g e) -> p t g e", g=4), oh[:, :, :].unsqueeze(3).to_broadcast([P, T, 4, 4]),
                                     o[:, :, :].unsqueeze(2).to_broadcast([P, T, 4, 4]), ALU.mult))
            dve.tensor_tensor(both[:, :, :], pick[:, 0], pick[:, 1], ALU.add).then_inc(both_set, 1)
            dve.wait_ge(exp_set, 2)
            do(dve.tensor_reduce(gsum[:, :], t4[:, :, :], AX.X, ALU.add))
            do(dve.tensor_scalar(den[:, :], m2[:, :], 1.0, None, ALU.add))
            do(dve.tensor_tensor(den[:, :], den[:, :], gsum[:, :], ALU.mult))
            do(dve.reciprocal(c.cw[:, 0], den[:, :]))
            do(dve.tensor_tensor(c.cw[:, 1], c.cw[:, 0], m2[:, :], ALU.mult))
            dve.wait_ge(counted, 1)
            ranks = pc[:, 0, 0:T * NEXP].rearrange("p (t e) -> p t e", e=NEXP)
            sums = pc[:, 1, 0:T * NEXP].rearrange("p (t e) -> p t e", e=NEXP)
            do(dve.memset(base[:, 0], 0.0))
            for t in range(T):
                do(dve.tensor_tensor(base[:, t + 1], base[:, t], sums[:, t], ALU.add))
            do(dve.tensor_tensor(cmp10[:, :, :], base[:, T].unsqueeze(2).to_broadcast([P, NEXP, 10]),
                                 thr[:, :].unsqueeze(1).to_broadcast([P, NEXP, 10]), ALU.is_gt))
            do(dve.tensor_reduce(ntiles[:, :], cmp10[:, :, :], AX.X, ALU.add))
            do(dve.tensor_tensor_scan(ends[:, :], one16[:, :], ntiles[:, :], 0.0, ALU.mult, ALU.add))
            do(dve.tensor_tensor(starts[:, :], ends[:, :], ntiles[:, :], ALU.subtract))
            do(dve.tensor_scalar(starts[:, :], starts[:, :], float(P), None, ALU.mult))
            do(dve.tensor_tensor(pos[:, :, :], base[:, 0:T], ranks, ALU.add))
            do(dve.tensor_tensor(pos[:, :, :], pos[:, :, :], starts[:, :].unsqueeze(1).to_broadcast([P, T, NEXP]), ALU.add))
            for k in range(2):
                do(dve.tensor_tensor(both[:, :, :], pick[:, k], pos[:, :, :], ALU.mult))
                do(dve.tensor_reduce(slotf[:, k], both[:, :, :], AX.X, ALU.add))
            dve.tensor_copy(c.slot[:, :, :], slotf[:, :, :]).then_inc(slot_set, 1)
            do(dve.tensor_tensor(cmp35[:, :, :], tile_no[:, :].unsqueeze(2).to_broadcast([P, SLOT_TILES, NEXP]),
                                 ends[:, :].unsqueeze(1).to_broadcast([P, SLOT_TILES, NEXP]), ALU.is_ge))
            do(dve.tensor_reduce(owner[:, :], cmp35[:, :, :], AX.X, ALU.add))
            do(dve.tensor_scalar(owner[:, :], owner[:, :], float(NEXP - 1), None, ALU.min))
            do(dve.tensor_copy(c.owner[:, :], owner[0:1, :]))
            dve.wait_ge(list_turned, 1)
            do(dve.tensor_copy(c.rows_of[:, :], pl[:, 0:SLOT_TILES]))

        @block.scalar
        def _(act):
            act.wait_ge(exp_in, 1)
            act.activation(t4[:, :, :], t4[:, :, :], ACT.Exp).then_inc(exp_set, 1)
            act.wait_ge(exp_in, 2)
            act.activation(m2[:, :], m2[:, :], ACT.Exp).then_inc(exp_set, 1)

        @block.tensor
        def _(pe):
            pe.wait_ge(made2, 1)
            pe.wait_ge(both_set, 1)
            pe.matmul(pc[:, 0, 0:T * NEXP], triu[:, :], both[:, :, :].rearrange("p t e -> p (t e)"), start=True, stop=True)
            pe.matmul(pc[:, 1, 0:T * NEXP], c.ones[:, :], both[:, :, :].rearrange("p t e -> p (t e)"), start=True, stop=True).then_inc(counted, 1)
            pe.wait_ge(list_in, 16)
            pe.transpose(pl[:, 0:SLOT_TILES], listed[:, :], c.ident[0:SLOT_TILES, 0:SLOT_TILES]).then_inc(list_turned, 1)


def phase_f_experts(c):
    nc, io = c.nc, c.io
    RING = 2
    with ExitStack() as ctx:
        def sb(name, shape):
            return ctx.enter_context(nc.sbuf_tensor(name, shape, F32))
        sem = semaphores(nc, ctx, "f_")
        w13 = sb("f_w13", [P, RING, 2, KD, DEXP])
        w2 = sb("f_w2", [P, RING, 2, D])
        xg, xt, out = sb("f_xg", [P, RING, D]), sb("f_xt", [P, RING, KD, P]), sb("f_out", [P, RING, D])
        act_t = sb("f_act", [P, RING, 2, P])
        pt = ctx.enter_context(nc.psum_tensor("f_pt", [P, 2, 4, P], F32))
        pab = ctx.enter_context(nc.psum_tensor("f_pab", [P, RING, 2, 512], F32))
        po = ctx.enter_context(nc.psum_tensor("f_po", [P, 2, 512], F32))
        w13_in, w2_in, x_in = ([sem(f"{n}{i}") for i in range(RING)] for n in ("w13_in", "w2_in", "x_in"))
        turned, ab_ready, o_ready = ([sem(f"{n}{i}") for i in range(RING)] for n in ("turned", "ab_ready", "o_ready"))
        xt_set, silu_set, prod_set, out_act, out_dve, out_stored = ([sem(f"{n}{i}") for i in range(RING)] for n in (
            "xt_set", "silu_set", "prod_set", "out_act", "out_dve", "out_stored"))
        block = ctx.enter_context(nc.Block())
        pairs, odd = divmod(SLOT_TILES, RING)

        assert odd == 1

        def turns(engine, body):
            for b in range(RING):
                body(0, b, False)
            with engine.Fori(1, pairs) as i:
                for b in range(RING):
                    body(i, b, False)
            body(pairs, 0, True)

        @block.sync
        def _(sp):
            for q in range(SLOT_TILES):
                i, b = divmod(q, RING)
                e = sp.value_load(c.owner[0:1, q:q + 1], min_val=0, max_val=NEXP - 1)
                wait_reuse(sp, ab_ready[b], i)
                sp.dma_start(w13[:, b], io["w13"][bass.ds(e, 1)].rearrange("o p w k f -> p (o w) k f")).then_inc(w13_in[b], 16)
                wait_reuse(sp, o_ready[b], i)
                sp.dma_start(w2[:, b], io["w2"][bass.ds(e, 1)].rearrange("o p k n -> p (o k) n")).then_inc(w2_in[b], 16)

        @block.gpsimd
        def _(pool):
            for q in range(SLOT_TILES):
                i, b = divmod(q, RING)
                wait_reuse(pool, turned[b], 2 * i)
                pool.indirect_dma_start(xg[:, b], None, c.h2, bass.IndirectOffsetOnAxis(ap=c.rows_of[:, q:q + 1], axis=0)).then_inc(x_in[b], 16)

        @block.tensor
        def _(pe):
            def turn(i, b, after=0):
                pe.wait_ge(x_in[b], i * 16 + 16 * (after + 1))
                for half in range(2):
                    if b == 1:
                        pe.wait_ge(xt_set[0], i * 2 + (half + 1))
                    elif after == 1:
                        pe.wait_ge(xt_set[1], i * 2 + (half + 1))
                    for j in range(4):
                        k = 4 * half + j
                        mm = pe.transpose(pt[:, half, j], xg[:, b, k * P:(k + 1) * P], c.ident[:, :])
                    mm.then_inc(turned[b], 1)

            def tile(i, b, last):
                pe.wait_ge(w13_in[b], i * 16 + 16)
                pe.wait_ge(xt_set[b], i * 2 + 2)
                wait_reuse(pe, prod_set[b], i)
                for w in range(2):
                    for f in range(2):
                        for k in range(KD):
                            mm = pe.matmul(pab[:, b, w, f * P:(f + 1) * P], w13[:, b, w, k, f * P:(f + 1) * P], xt[:, b, k],
                                           start=(k == 0), stop=(k == KD - 1))
                mm.then_inc(ab_ready[b], 1)
                if not last:
                    turn(i, 1 - b, b)
                pe.wait_ge(w2_in[b], i * 16 + 16)
                pe.wait_ge(prod_set[b], i + 1)
                if b == 0:
                    wait_reuse(pe, out_act[1], i)
                    wait_reuse(pe, out_dve[1], i)
                else:
                    pe.wait_ge(out_act[0], i + 1)
                    pe.wait_ge(out_dve[0], i + 1)
                for half in range(2):
                    for f in range(2):
                        mm = pe.matmul(po[:, half], act_t[:, b, f], w2[:, b, f, 512 * half:512 * half + 512], start=(f == 0), stop=(f == 1))
                mm.then_inc(o_ready[b], 1)
            turn(0, 0)
            turns(pe, tile)

        @block.scalar
        def _(act):
            def copy_turned(i, b, after=0):
                for half in range(2):
                    act.wait_ge(turned[b], i * 2 + (2 * after + half + 1))
                    if half == 0 and after == 1:
                        act.wait_ge(ab_ready[0], i + 1)
                    elif half == 0:
                        wait_reuse(act, ab_ready[b], i)
                    act.activation(xt[:, b, 4 * half:4 * half + 4], pt[:, half], ACT.Copy).then_inc(xt_set[b], 1)

            def tile(i, b, last):
                act.wait_ge(ab_ready[b], i + 1)
                wait_reuse(act, o_ready[b], i)
                act.activation(act_t[:, b].rearrange("p f t -> p (f t)"), pab[:, b, 0, 0:DEXP], ACT.Silu).then_inc(silu_set[b], 1)
                if not last:
                    copy_turned(i, 1 - b, b)
                act.wait_ge(o_ready[b], i + 1)
                wait_reuse(act, out_stored[b], i * 16)
                act.activation(out[:, b, 0:512], po[:, 0], ACT.Copy).then_inc(out_act[b], 1)
                act.wait_ge(out_act[b], i + 1)
                act.wait_ge(out_dve[b], i + 1)
                act.dma_start(c.ys[bass.ds((i * RING + b) * P, P), :], out[:, b]).then_inc(out_stored[b], 16)
            copy_turned(0, 0)
            turns(act, tile)
            for b in range(RING):
                act.wait_ge(out_stored[b], 16 * (pairs + (b < odd)))

        @block.vector
        def _(dve):
            def tile(i, b, last):
                dve.wait_ge(silu_set[b], i + 1)
                a = act_t[:, b].rearrange("p f t -> p (f t)")
                dve.tensor_tensor(a, a, pab[:, b, 1, 0:DEXP], ALU.mult).then_inc(prod_set[b], 1)
                dve.wait_ge(o_ready[b], i + 1)
                wait_reuse(dve, out_stored[b], i * 16)
                dve.tensor_copy(out[:, b, 512:D], po[:, 1]).then_inc(out_dve[b], 1)
            turns(dve, tile)


def phase_f_combine(c):
    nc, io = c.nc, c.io
    with ExitStack() as ctx:
        def sb(name, shape):
            return ctx.enter_context(nc.sbuf_tensor(name, shape, F32))
        sem = semaphores(nc, ctx, "g_")
        R = 3
        y = sb("g_y", [P, R, 2, D])
        stat = sb("g_stat", [P, 4, TILES])
        y_in, stored = [sem(f"y_in{i}") for i in range(R)], [sem(f"stored{i}") for i in range(R)]
        own_dve, x3_set, squared, var_set, std_set, normed, done = (sem(n) for n in (
            "own_dve", "x3_set", "squared", "var_set", "std_set", "normed", "done"))
        block = ctx.enter_context(nc.Block())

        @block.gpsimd
        def _(pool):
            for t in range(TILES):
                if t >= R:
                    pool.wait_ge(stored[t % R], 16 * (t // R))
                for k in range(2):
                    pool.indirect_dma_start(y[:, t % R, k], None, c.ys, bass.IndirectOffsetOnAxis(ap=c.slot[:, k, t:t + 1], axis=0)).then_inc(y_in[t % R], 16)

        @block.vector
        def _(dve):
            own = Own(dve, own_dve)

            def combine(t):
                s = 0 if t < PROMPT // P else 1
                a, b = y[:, t % R, 0], y[:, t % R, 1]
                dve.wait_ge(y_in[t % R], 32 * (t // R + 1))
                own.did(dve.tensor_scalar(a, a, c.cw[:, 0, t:t + 1], None, ALU.mult))
                own.settle()
                own.did(dve.scalar_tensor_tensor(b, b, c.cw[:, 1, t:t + 1], a, ALU.mult, ALU.add))
                own.settle()
                own.did(dve.tensor_tensor(b, b, c.gate2[:, s], ALU.mult))
                own.settle()
                dve.tensor_tensor(c.x2[:, t], c.x2[:, t], b, ALU.add).then_inc(x3_set, 1)

            def finish(t):
                dve.wait_ge(squared, t + 1)
                dve.tensor_scalar(stat[:, 1, t:t + 1], stat[:, 0, t:t + 1], 1.0 / D, NORM_EPS, ALU.mult, ALU.add).then_inc(var_set, 1)
                dve.wait_ge(std_set, t + 1)
                own.did(dve.reciprocal(stat[:, 3, t:t + 1], stat[:, 2, t:t + 1]))
                own.settle()
                dve.scalar_tensor_tensor(y[:, t % R, 0], c.x2[:, t], stat[:, 3, t:t + 1], c.fgain[:, :], ALU.mult, ALU.mult).then_inc(done, 1)
            for t in range(TILES + 1):
                if t < TILES:
                    combine(t)
                if t >= 1:
                    finish(t - 1)

        @block.scalar
        def _(act):
            for t in range(TILES):
                act.wait_ge(x3_set, t + 1)
                if t >= 1:
                    act.wait_ge(squared, t)
                act.activation(c.junk[:, :], c.x2[:, t], ACT.Square, accum_out=stat[:, 0, t:t + 1]).then_inc(squared, 1)
                act.wait_ge(var_set, t + 1)
                act.activation(stat[:, 2, t:t + 1], stat[:, 1, t:t + 1], ACT.Sqrt).then_inc(std_set, 1)

        @block.sync
        def _(sp):
            for t in range(TILES):
                sp.wait_ge(done, t + 1)
                sp.dma_start(io["y_out"][t * P:(t + 1) * P, :], y[:, t % R, 0]).then_inc(stored[t % R], 16)
            for i in range(R):
                sp.wait_ge(stored[i], 16 * len(range(i, TILES, R)))


def phases_e_f(c):
    nc = c.nc
    I32 = mybir.dt.int32
    with ExitStack() as ctx:
        def sb(name, shape, dt=F32):
            return ctx.enter_context(nc.sbuf_tensor(name, shape, dt))
        c.gate2, c.junk = sb("f_gate2", [P, 2, D]), sb("f_junk", [P, D])
        c.logits, c.cw = sb("f_logits", [P, TILES, 20]), sb("f_cw", [P, 2, TILES])
        c.slot, c.rows_of, c.owner = sb("f_slot", [P, 2, TILES], I32), sb("f_rows_of", [P, SLOT_TILES], I32), sb("f_owner", [1, SLOT_TILES], I32)
        c.fgain = sb("f_fgain", [P, D])
        with ExitStack() as inner:
            c.rep = inner.enter_context(nc.sbuf_tensor("e_rep", [P, 3, 2, D], F32))
            merged = inner.enter_context(nc.sbuf_tensor("e_merged", [P, KD, NT], F32))
            phase_e_merge(c, merged)
            c.x2 = c.y[:, :, :].rearrange("p a b -> p (a b)").rearrange("p (t n) -> p t n", n=D)
            phase_e_rows(c, merged)
        phase_e_route(c)
        phase_f_experts(c)
        phase_f_combine(c)


def program(nc, io):
    with ExitStack() as ctx:
        c = allocate(nc, ctx, io)
        with nc.sbuf_tensor("cs", [P, KD, 2], F32) as c.cs, nc.psum_tensor("pm", [P, 4 * MOD_PARTS, 2], F32) as c.pm:
            phase_a(c)
            phase_b(c)
        phase_c(c)
        phase_d(c)
        phases_e_f(c)


def lay_out(inp):
    import numpy as np
    a = {k: np.asarray(v) for k, v in inp.items()}
    o = {}
    o["x"] = np.concatenate([a["x_prompt"][0], a["x_sample"][0]], 0)
    cond = np.stack([a["c_ctx"], a["c"][0]], -1)
    o["cond"] = cond.reshape(KD, P, 2).transpose(1, 0, 2)
    vec = [a[name].reshape(-1, P) for name, _ in VEC_PARTS]
    o["vecs"] = np.concatenate(vec, 0).T
    o["w_mod"] = a["w_mod"][0].reshape(KD, P, 12, 512).transpose(2, 1, 0, 3)
    o["w_in"] = a["w_in"][0].reshape(KD, P, 14, 256).transpose(2, 1, 0, 3)
    o["w_qkv"] = np.stack([a[n][0].transpose(1, 0, 2) for n in ("mlstm_w_q", "mlstm_w_k", "mlstm_w_v")], 1)
    w_if = np.zeros((P, BH, 2, ROWS), np.float32)
    b_if, m0 = np.zeros((ROWS, 2), np.float32), np.zeros((ROWS, 1), np.float32)
    for d in range(2):
        for g, n in enumerate(("i", "f")):
            w_if[:, :, g, 32 * d:32 * d + 4] = a["mlstm_w_" + n][0, d].reshape(BH, P, 4).transpose(1, 0, 2)
            b_if[32 * d:32 * d + 4, g] = a["mlstm_b_" + n][0, d]
        m0[32 * d:32 * d + 4, 0] = a["state_mlstm_m"][0, 0, d]
    o["w_if"], o["b_if"], o["m0"] = w_if, b_if, m0
    o["c0"] = a["state_mlstm_C"][0, 0].reshape(8, P, P).transpose(1, 0, 2)
    o["n0"] = a["state_mlstm_n"][0, 0].reshape(8, P).T
    cols = [a["rwkv_w_r"][0], a["rwkv_w_k"][0], a["rwkv_w_v"][0]]
    cols += [a[n][0, d] for n in ("rwkv_w1", "rwkv_a1") for d in range(2)] + [a["rwkv_g1"][0]]
    o["w_rwkv"] = np.concatenate(cols, 1).reshape(4, P, 15, P).transpose(1, 0, 2, 3)
    o["w_rank"] = np.stack([a["rwkv_w2"][0].reshape(P, 4 * P), a["rwkv_a2"][0].reshape(P, 4 * P)], 1)
    o["w_g2"] = a["rwkv_g2"][0]
    o["s0"] = a["state_rwkv"][0, 0].reshape(2, 4, 2, RC, RC).transpose(2, 4, 1, 0, 3).reshape(P, 4, 2, RC)
    o["w_branch"] = np.stack([a[n][0].reshape(4, P, D).transpose(1, 0, 2) for n in ("rwkv_w_proj", "mlstm_w_proj")])
    o["w_out"] = a["w_out"][0].reshape(KD, P, D).transpose(1, 0, 2)
    o["w_router"] = np.concatenate([a["moe_w_group"][0], a["moe_w_expert"][0]], 1).reshape(KD, P, 20).transpose(1, 0, 2)
    o["b_router"] = np.concatenate([a["moe_b_group"][0], a["moe_b_expert"][0]])
    o["final_g"] = a["final_norm_g"]
    w13 = np.stack([a["moe_w1"][0], a["moe_w3"][0]], 1)
    o["w13"] = w13.reshape(NEXP, 2, KD, P, DEXP).transpose(0, 3, 1, 2, 4)
    o["w2"] = a["moe_w2"][0].reshape(NEXP, 2, P, D).transpose(0, 2, 1, 3)
    return {k: np.ascontiguousarray(v) for k, v in o.items()}


OUTPUTS = {"y_out": (NT, D), "new_s": (P, HEADS_P, 2, RC), "new_c": (2, BH, P, P), "new_n": (2, P, BH), "new_m": (2, BH)}


def kernel(**inputs):
    import numpy as np
    from concourse import bacc
    from concourse.bass_utils import run_bass_kernel_spmd

    nc = bacc.Bacc("TRN2", target_bir_lowering=False, num_devices=1)
    arrays = {f"in_{name}": a for name, a in lay_out(inputs).items()}
    io = {name[3:]: nc.dram_tensor(name, a.shape, mybir.dt.from_np(a.dtype), kind="ExternalInput").ap() for name, a in arrays.items()}
    for name, shape in OUTPUTS.items():
        io[name] = nc.dram_tensor(f"out_{name}", shape, F32, kind="ExternalOutput").ap()
    program(nc, io)
    r = run_bass_kernel_spmd(nc, [arrays], core_ids=[0]).results[0]
    y = np.asarray(r["out_y_out"])
    s = np.asarray(r["out_new_s"]).reshape(2, RC, HEADS_P, 2, RC).transpose(3, 2, 0, 4, 1).reshape(1, 1, 2, 2 * HEADS_P, RC, RC)
    n = np.asarray(r["out_new_n"]).transpose(0, 2, 1)[None, None]
    return y[None, :PROMPT], y[None, PROMPT:], s, np.asarray(r["out_new_c"])[None, None], n, np.asarray(r["out_new_m"])[None, None]
```
